# Optimizing a Trainium2 kernel written in Bass

```python
import math
import jax
import jax.numpy as jnp
from jax import lax
import numpy as np

D_MODEL = 1024
BATCH = 1
SEQ = 256
DEPTH = 2

CTX_LEN = 256
GRID_W = 64

DA_HEADS = 4
DA_HEAD_DIM = 64
DA_V_DIM = 2 * DA_HEAD_DIM
DA_QK_WIDTH = DA_HEADS * 2 * DA_HEAD_DIM
DA_WIDTH = DA_HEADS * DA_V_DIM
Q_BLOCK = 128
ROPE_THETA = 10000.0

GLA_HEADS = 4
GLA_DK = 64
GLA_DV = 128
GLA_K_WIDTH = GLA_HEADS * GLA_DK
GLA_WIDTH = GLA_HEADS * GLA_DV
GLA_GATE_RANK = 16
GLA_GATE_TAU = 16.0
GLA_CHUNK = 64

HY_WIDTH = 512
HY_POS_DIM = 33
HY_HIDDEN = 64
HY_TARGET = 1e-2
HY_FAST_PCT = 0.3
HY_SLOW_PCT = 1.5

N_BRANCH = 3
BRANCH_WIDTH = 512
D_FF = 2816
LN_EPS = 1e-5
DEEPNORM_ALPHA = (2.0 * DEPTH) ** 0.25
DEEPNORM_BETA = (8.0 * DEPTH) ** -0.25

PROJ_SPLITS = (DA_QK_WIDTH, DA_QK_WIDTH, DA_WIDTH,
               GLA_K_WIDTH, GLA_K_WIDTH, GLA_WIDTH, GLA_WIDTH, 2 * GLA_GATE_RANK,
               3 * HY_WIDTH, N_BRANCH * D_MODEL)
D_IN_PROJ = 7712

kernel_name = 'hybrid_diffattn_gla_hyena_deepnorm_block'

def _layer_norm(x):
    xf = x.astype(jnp.float32)
    mu = jnp.mean(xf, axis=-1, keepdims=True)
    var = jnp.mean(jnp.square(xf - mu), axis=-1, keepdims=True)
    return ((xf - mu) * lax.rsqrt(var + LN_EPS)).astype(x.dtype)

def _rms_norm(x, g):
    xf = x.astype(jnp.float32)
    y = xf * lax.rsqrt(jnp.mean(jnp.square(xf), axis=-1, keepdims=True) + LN_EPS)
    return (y * g).astype(x.dtype)

def _modulate(x, shift, scale):
    return _layer_norm(x) * (1.0 + scale) + shift

def _post_norm(x, y, gate, g, b):
    return _layer_norm(DEEPNORM_ALPHA * x + gate * y) * g + b

def _dwconv3(x, w, b):
    xp = jnp.pad(x, ((0, 0), (1, 1), (0, 0)))
    return xp[:, :-2] * w[0] + xp[:, 1:-1] * w[1] + xp[:, 2:] * w[2] + b

def _split_cols(p):
    idx, acc = [], 0
    for s in PROJ_SPLITS[:-1]:
        acc += s
        idx.append(acc)
    return jnp.split(p, idx, axis=-1)

def _axial_rope(x):
    length = x.shape[1]
    n_rows = length // GRID_W
    rows = jnp.repeat(jnp.arange(n_rows), GRID_W).astype(jnp.float32)
    cols = (jnp.arange(length) % GRID_W).astype(jnp.float32)
    n_freq = DA_HEAD_DIM // 4
    inv = ROPE_THETA ** (-jnp.arange(n_freq, dtype=jnp.float32) / n_freq)

    def rot(xh, pos):
        ang = pos[:, None] * inv
        cos = jnp.cos(ang)[None, :, None, None, :]
        sin = jnp.sin(ang)[None, :, None, None, :]
        x1, x2 = jnp.split(xh.astype(jnp.float32), 2, axis=-1)
        return jnp.concatenate([x1 * cos - x2 * sin, x2 * cos + x1 * sin], axis=-1)

    xr, xc = jnp.split(x, 2, axis=-1)
    return jnp.concatenate([rot(xr, rows), rot(xc, cols)], axis=-1).astype(x.dtype)

def _diff_attn_block(q, k, v, lam):
    s = jnp.einsum('bqhmd,bkhmd->bhmqk', q, k).astype(jnp.float32) * (DA_HEAD_DIM ** -0.5)
    p = jax.nn.softmax(s, axis=-1)
    a = p[:, :, 0] - lam * p[:, :, 1]
    return jnp.einsum('bhqk,bkhe->bqhe', a.astype(v.dtype), v)

def _flip(t):
    return jnp.flip(t, axis=2)

def _gla_states(k, v, log_a, s0):
    bsz, heads, length, dk = k.shape
    n = length // GLA_CHUNK
    kc = k.reshape(bsz, heads, n, GLA_CHUNK, dk)
    vc = v.reshape(bsz, heads, n, GLA_CHUNK, v.shape[-1])
    b = jnp.cumsum(log_a.reshape(bsz, heads, n, GLA_CHUNK, dk), axis=3)
    b_end = b[:, :, :, -1:, :]
    u = jnp.einsum('bhnck,bhncv->bhnkv', kc * jnp.exp(b_end - b), vc)
    chunk_decay = jnp.exp(b_end[:, :, :, 0, :])

    def step(s, inp):
        d_n, u_n = inp
        return d_n[..., None] * s + u_n, s

    s_final, s_start = lax.scan(step, s0, (jnp.moveaxis(chunk_decay, 2, 0), jnp.moveaxis(u, 2, 0)))
    return b, jnp.moveaxis(s_start, 0, 2), s_final

def _gla_output(q, k, v, b, s_start):
    bsz, heads, length, dk = q.shape
    n = length // GLA_CHUNK
    qc = q.reshape(bsz, heads, n, GLA_CHUNK, dk)
    kc = k.reshape(bsz, heads, n, GLA_CHUNK, dk)
    vc = v.reshape(bsz, heads, n, GLA_CHUNK, v.shape[-1])
    ref = b[:, :, :, GLA_CHUNK // 2:GLA_CHUNK // 2 + 1, :]
    att = jnp.einsum('bhnck,bhnsk->bhncs', qc * jnp.exp(b - ref), kc * jnp.exp(ref - b))
    tri = jnp.tril(jnp.ones((GLA_CHUNK, GLA_CHUNK), dtype=bool))
    att = jnp.where(tri, att, 0.0)
    o = (jnp.einsum('bhncs,bhnsv->bhncv', att, vc)
         + jnp.einsum('bhnck,bhnkv->bhncv', qc * jnp.exp(b), s_start))
    return o.reshape(bsz, heads, length, -1)

def _hyena_filters(length, p):
    t = jnp.linspace(0.0, 1.0, length, dtype=jnp.float32)[:, None]
    bands = (HY_POS_DIM - 1) // 2
    w = 2.0 * math.pi * jnp.arange(length, dtype=jnp.float32)[:, None] / length
    f = jnp.linspace(1e-4, bands - 1, bands, dtype=jnp.float32)[None, :]
    feat = jnp.concatenate([t, jnp.cos(f * w), -jnp.sin(f * w)], axis=-1)
    h = jnp.sin(p['hy_freq1'] * (feat @ p['hy_w1'] + p['hy_b1']))
    h = jnp.sin(p['hy_freq2'] * (h @ p['hy_w2'] + p['hy_b2']))
    h = (h @ p['hy_w3']).reshape(length, 2, HY_WIDTH)
    max_decay = math.log(HY_TARGET) / HY_FAST_PCT
    min_decay = math.log(HY_TARGET) / HY_SLOW_PCT
    deltas = jnp.abs(jnp.linspace(min_decay, max_decay, HY_WIDTH, dtype=jnp.float32))
    h = h * jnp.exp(-t * deltas)[:, None, :]
    return h[:, 0], h[:, 1]

def _long_conv(u, h_f, h_b):
    length = u.shape[1]
    n_fft = 2 * length
    taps = jnp.concatenate([h_f, jnp.zeros((1, h_f.shape[1]), h_f.dtype), h_b[:0:-1]], axis=0)
    uf = jnp.fft.rfft(u.astype(jnp.float32), n=n_fft, axis=1)
    tf = jnp.fft.rfft(taps.astype(jnp.float32), n=n_fft, axis=0)
    y = jnp.fft.irfft(uf * tf[None], n=n_fft, axis=1)[:, :length]
    return y.astype(u.dtype)

def _token_mixer(h_lat, h_ctx, p, layer_idx, with_ctx):
    bsz, length, _ = h_lat.shape
    c_len = h_ctx.shape[1]
    (a_q, a_k, a_v, g_q, g_k, g_v, g_r, g_z, hy_in, gate_logits) = _split_cols(h_lat @ p['w_in'])
    (ca_q, ca_k, ca_v, cg_q, cg_k, cg_v, cg_r, cg_z, chy_in, cgate_logits) = _split_cols(h_ctx @ p['w_in'])

    lam_init = 0.8 - 0.6 * math.exp(-0.3 * layer_idx)
    lam_p = p['da_lambda'].astype(jnp.float32)
    lam = jnp.exp(jnp.sum(lam_p[0] * lam_p[1])) - jnp.exp(jnp.sum(lam_p[2] * lam_p[3])) + lam_init
    q_lat = _axial_rope(a_q.reshape(bsz, length, DA_HEADS, 2, DA_HEAD_DIM))
    k_lat = _axial_rope(a_k.reshape(bsz, length, DA_HEADS, 2, DA_HEAD_DIM))
    v_lat = a_v.reshape(bsz, length, DA_HEADS, DA_V_DIM)
    k_ctx = ca_k.reshape(bsz, c_len, DA_HEADS, 2, DA_HEAD_DIM)
    v_ctx = ca_v.reshape(bsz, c_len, DA_HEADS, DA_V_DIM)
    k_all = jnp.concatenate([k_ctx, k_lat], axis=1)
    v_all = jnp.concatenate([v_ctx, v_lat], axis=1)
    n_blk = length // Q_BLOCK
    q_blocks = jnp.moveaxis(q_lat.reshape(bsz, n_blk, Q_BLOCK, DA_HEADS, 2, DA_HEAD_DIM), 1, 0)
    o_blocks = lax.map(lambda qb: _diff_attn_block(qb, k_all, v_all, lam), q_blocks)
    o_a = jnp.moveaxis(o_blocks, 0, 1).reshape(bsz, length, DA_HEADS, DA_V_DIM)
    y_a = (_rms_norm(o_a, p['da_norm_g']) * (1.0 - lam_init)).reshape(bsz, length, DA_WIDTH)

    def gla_inputs(q, k, v, z, n):
        q = q.reshape(bsz, n, GLA_HEADS, GLA_DK).transpose(0, 2, 1, 3).astype(jnp.float32) * (GLA_DK ** -0.5)
        k = k.reshape(bsz, n, GLA_HEADS, GLA_DK).transpose(0, 2, 1, 3).astype(jnp.float32)
        v = v.reshape(bsz, n, GLA_HEADS, GLA_DV).transpose(0, 2, 1, 3).astype(jnp.float32)
        z_f, z_b = jnp.split(z.astype(jnp.float32), 2, axis=-1)

        def log_decay(zd, d):
            la = jax.nn.log_sigmoid(zd @ p['gla_w_gate'][d] + p['gla_b_gate'][d]) / GLA_GATE_TAU
            return la.astype(jnp.float32).reshape(bsz, n, GLA_HEADS, GLA_DK).transpose(0, 2, 1, 3)

        return q, k, v, log_decay(z_f, 0), log_decay(z_b, 1)

    def gla_merge(o, r, n):
        o = _rms_norm(o.transpose(0, 2, 1, 3), p['gla_norm_g']).reshape(bsz, n, GLA_WIDTH)
        return o.astype(r.dtype) * jax.nn.silu(r)

    q_b, k_b, v_b, la_f, la_b = gla_inputs(g_q, g_k, g_v, g_z, length)
    cq_b, ck_b, cv_b, cla_f, cla_b = gla_inputs(cg_q, cg_k, cg_v, cg_z, c_len)
    s0 = jnp.zeros((bsz, GLA_HEADS, GLA_DK, GLA_DV), jnp.float32)
    cb_f, cst_f, cs_f = _gla_states(ck_b, cv_b, cla_f, s0)
    cb_b, cst_b, cs_b = _gla_states(_flip(ck_b), _flip(cv_b), _flip(cla_b), s0)
    b_f, st_f, _ = _gla_states(k_b, v_b, la_f, cs_f)
    b_b, st_b, _ = _gla_states(_flip(k_b), _flip(v_b), _flip(la_b), cs_b)
    o_b = (_gla_output(q_b, k_b, v_b, b_f, st_f)
           + _flip(_gla_output(_flip(q_b), _flip(k_b), _flip(v_b), b_b, st_b)))
    y_b = gla_merge(o_b, g_r, length)

    def hyena(hy, n):
        hy = _dwconv3(hy, p['hy_conv_w'], p['hy_conv_b'])
        x0, x1, vv = jnp.split(hy, 3, axis=-1)
        u = x1 * vv
        h_f, h_b = _hyena_filters(n, p)
        return x0 * (_long_conv(u, h_f, h_b) + p['hy_skip'] * u)

    y_c = hyena(hy_in, length)

    def merge(ya, yb, yc, logits, n):
        ys = jnp.stack([ya, yb.astype(ya.dtype), yc.astype(ya.dtype)], axis=2)
        proj = jnp.einsum('bngc,gcd->bngd', ys, p['w_branch'])
        gates = jax.nn.sigmoid(logits.reshape(bsz, n, N_BRANCH, D_MODEL))
        return jnp.sum(gates * proj, axis=2) @ p['w_out']

    out_lat = merge(y_a, y_b, y_c, gate_logits, length)
    if not with_ctx:
        return out_lat, None

    o_ca = _diff_attn_block(ca_q.reshape(bsz, c_len, DA_HEADS, 2, DA_HEAD_DIM), k_ctx, v_ctx, lam)
    y_ca = (_rms_norm(o_ca, p['da_norm_g']) * (1.0 - lam_init)).reshape(bsz, c_len, DA_WIDTH)
    o_cb = (_gla_output(cq_b, ck_b, cv_b, cb_f, cst_f)
            + _flip(_gla_output(_flip(cq_b), _flip(ck_b), _flip(cv_b), cb_b, cst_b)))
    y_cb = gla_merge(o_cb, cg_r, c_len)
    y_cc = hyena(chy_in, c_len)
    out_ctx = merge(y_ca, y_cb, y_cc, cgate_logits, c_len)
    return out_lat, out_ctx

def _conv_ffn(h, p):
    up = _dwconv3(h @ p['ffn_w_up'], p['ffn_conv_w'], p['ffn_conv_b'])
    a, g = jnp.split(up, 2, axis=-1)
    return (jax.nn.gelu(g) * a) @ p['ffn_w_down']

def setup_inputs(seed: int = 0) -> dict:
    key = jax.random.key(seed)
    ks = jax.random.split(key, 32)

    def nrm(i, shape, scale):
        return scale * jax.random.normal(ks[i], shape, jnp.float32)

    L = DEPTH
    D = D_MODEL
    return {
        'x': nrm(0, (BATCH, SEQ, D), 1.0),
        'c': nrm(1, (BATCH, D), 1.0),
        'ctx': nrm(2, (BATCH, CTX_LEN, D), 1.0),
        'c_ctx': nrm(3, (D,), 1.0),
        'w_ada': nrm(4, (L, D, 6 * D), 0.5 * D ** -0.5),
        'b_ada': nrm(5, (L, 6 * D), 0.02),
        'w_in': nrm(6, (L, D, D_IN_PROJ), D ** -0.5),
        'da_lambda': nrm(7, (L, 4, DA_HEAD_DIM), 0.1),
        'da_norm_g': 1.0 + nrm(8, (L, DA_V_DIM), 0.02),
        'gla_w_gate': nrm(9, (L, 2, GLA_GATE_RANK, GLA_K_WIDTH), GLA_GATE_RANK ** -0.5),
        'gla_b_gate': nrm(10, (L, 2, GLA_K_WIDTH), 0.1),
        'gla_norm_g': 1.0 + nrm(11, (L, GLA_DV), 0.02),
        'hy_conv_w': nrm(12, (L, 3, 3 * HY_WIDTH), 3 ** -0.5),
        'hy_conv_b': nrm(13, (L, 3 * HY_WIDTH), 0.02),
        'hy_w1': nrm(14, (L, HY_POS_DIM, HY_HIDDEN), HY_POS_DIM ** -0.5),
        'hy_b1': nrm(15, (L, HY_HIDDEN), 0.1),
        'hy_freq1': 1.0 + nrm(16, (L, HY_HIDDEN), 0.1),
        'hy_w2': nrm(17, (L, HY_HIDDEN, HY_HIDDEN), HY_HIDDEN ** -0.5),
        'hy_b2': nrm(18, (L, HY_HIDDEN), 0.1),
        'hy_freq2': 1.0 + nrm(19, (L, HY_HIDDEN), 0.1),
        'hy_w3': nrm(20, (L, HY_HIDDEN, 2 * HY_WIDTH), 0.05 * HY_HIDDEN ** -0.5),
        'hy_skip': 1.0 + nrm(21, (L, HY_WIDTH), 0.1),
        'w_branch': nrm(22, (L, N_BRANCH, BRANCH_WIDTH, D), BRANCH_WIDTH ** -0.5),
        'w_out': nrm(23, (L, D, D), DEEPNORM_BETA * D ** -0.5),
        'ln1_g': 1.0 + nrm(24, (L, D), 0.02),
        'ln1_b': nrm(25, (L, D), 0.02),
        'ffn_w_up': nrm(26, (L, D, 2 * D_FF), D ** -0.5),
        'ffn_conv_w': nrm(27, (L, 3, 2 * D_FF), 3 ** -0.5),
        'ffn_conv_b': nrm(28, (L, 2 * D_FF), 0.02),
        'ffn_w_down': nrm(29, (L, D_FF, D), DEEPNORM_BETA * D_FF ** -0.5),
        'ln2_g': 1.0 + nrm(30, (L, D), 0.02),
        'ln2_b': nrm(31, (L, D), 0.02),
    }

def reference(x, c, ctx, c_ctx, w_ada, b_ada, w_in, da_lambda, da_norm_g, gla_w_gate, gla_b_gate,
              gla_norm_g, hy_conv_w, hy_conv_b, hy_w1, hy_b1, hy_freq1, hy_w2, hy_b2, hy_freq2, hy_w3,
              hy_skip, w_branch, w_out, ln1_g, ln1_b, ffn_w_up, ffn_conv_w, ffn_conv_b, ffn_w_down,
              ln2_g, ln2_b):
    x_lat, x_ctx = x, ctx
    for l in range(DEPTH):
        with_ctx = l < DEPTH - 1
        p = {
            'w_in': w_in[l], 'da_lambda': da_lambda[l], 'da_norm_g': da_norm_g[l],
            'gla_w_gate': gla_w_gate[l], 'gla_b_gate': gla_b_gate[l], 'gla_norm_g': gla_norm_g[l],
            'hy_conv_w': hy_conv_w[l], 'hy_conv_b': hy_conv_b[l], 'hy_w1': hy_w1[l], 'hy_b1': hy_b1[l],
            'hy_freq1': hy_freq1[l], 'hy_w2': hy_w2[l], 'hy_b2': hy_b2[l], 'hy_freq2': hy_freq2[l],
            'hy_w3': hy_w3[l], 'hy_skip': hy_skip[l], 'w_branch': w_branch[l], 'w_out': w_out[l],
            'ffn_w_up': ffn_w_up[l], 'ffn_conv_w': ffn_conv_w[l], 'ffn_conv_b': ffn_conv_b[l],
            'ffn_w_down': ffn_w_down[l],
        }
        mod_lat = jax.nn.silu(c) @ w_ada[l] + b_ada[l]
        mod_ctx = jax.nn.silu(c_ctx) @ w_ada[l] + b_ada[l]
        sh1, sc1, g1, sh2, sc2, g2 = jnp.split(mod_lat[:, None, :], 6, axis=-1)
        csh1, csc1, cg1, csh2, csc2, cg2 = jnp.split(mod_ctx, 6)
        y_lat, y_ctx = _token_mixer(_modulate(x_lat, sh1, sc1), _modulate(x_ctx, csh1, csc1), p, l, with_ctx)
        x_lat = _post_norm(x_lat, y_lat, g1, ln1_g[l], ln1_b[l])
        x_lat = _post_norm(x_lat, _conv_ffn(_modulate(x_lat, sh2, sc2), p), g2, ln2_g[l], ln2_b[l])
        if with_ctx:
            x_ctx = _post_norm(x_ctx, y_ctx, cg1, ln1_g[l], ln1_b[l])
            x_ctx = _post_norm(x_ctx, _conv_ffn(_modulate(x_ctx, csh2, csc2), p), cg2, ln2_g[l], ln2_b[l])
    return x_lat


_drawn_inputs = setup_inputs


def setup_inputs(seed=0):
    import zlib

    import numpy as np

    out = dict(_drawn_inputs(seed))
    spreads = {}
    factors = {'ctx': 2.668,
     'b_ada': 3.782,
     'da_lambda': 8.0,
     'da_norm_g': 43.379,
     'gla_w_gate': 6.286,
     'gla_b_gate': 8.0,
     'gla_norm_g': 51.183,
     'hy_conv_b': 8.0,
     'hy_w1': 4.177,
     'hy_b1': 8.0,
     'hy_freq1': 8.0,
     'hy_w2': 4.224,
     'hy_b2': 8.0,
     'hy_freq2': 8.0,
     'hy_w3': 4.269,
     'hy_skip': 5.354,
     'ffn_conv_b': 8.0}
    for name, (base, spread) in spreads.items():
        noise = np.random.default_rng([zlib.crc32(name.encode()), seed]).standard_normal(out[name].shape)
        drawn = base * np.exp(spread * noise) if base else spread * noise
        out[name] = jnp.asarray(drawn.astype(out[name].dtype))
    for name, factor in factors.items():
        out[name] = (out[name] * factor).astype(out[name].dtype)
    return out
```

```python
import math
from contextlib import ExitStack

import numpy as np
import concourse.bass as bass
from concourse import mybir

F32 = mybir.dt.float32
F32R = mybir.dt.float32r
I32 = mybir.dt.int32
ACT = mybir.ActivationFunctionType
ALU = mybir.AluOpType
AX_X = mybir.AxisListType.X

P = 128
D = 1024
DEPTH = 2
SEQ = 256
TOK = 2 * SEQ
KT = D // P
HEADS = 4
BW = 512
CT = BW // P
DFF = 2816
FT = DFF // P
CHUNK = 64
EPS = 1e-5
ALPHA = (2.0 * DEPTH) ** 0.25
COLS = 512
NBUF = 4
AHEAD = 3
TWO_PI = 2.0 * math.pi
ROUND = 12582912.0


def shape_constants():
    f = np.float32
    out = {"ident": np.eye(P, dtype=f)}
    s, t = np.meshgrid(np.arange(P), np.arange(P), indexing="ij")
    same = s // CHUNK == t // CHUNK
    first = t // CHUNK * CHUNK
    upto = [same & (s <= t), same & (s >= t)]
    ref = [same & (s <= first + CHUNK // 2), same & (s >= first + CHUNK // 2 - 1)]
    after = [same & (s > t), same & (s < t)]
    tau = 1.0 / 16.0
    cums = [np.concatenate([upto[d] * tau, (upto[d].astype(f) - ref[d].astype(f)) * tau], 1) for d in range(2)]
    out["cums"] = np.stack(cums, 1).astype(f).reshape(P, 2 * 256)
    out["tail"] = np.stack([after[d] * tau for d in range(2)], 1).astype(f).reshape(P, 2 * P)
    out["mask"] = np.stack([upto[0], upto[1]], 1).astype(np.int32).reshape(P, 2 * P)
    pos = np.arange(SEQ)
    inv = (10000.0 ** (-np.arange(16, dtype=f) / f(16))).astype(f)
    row, col = (pos // 64).astype(f)[:, None] * inv, (pos % 64).astype(f)[:, None] * inv
    ang = np.concatenate([row, row, col, col], 1)
    sign = np.tile(np.concatenate([-np.ones(16), np.ones(16)]), 2)[None]
    out["rope"] = np.stack([np.cos(ang), np.sin(ang) * sign], 1).astype(f).reshape(2, P, P).transpose(1, 0, 2).reshape(P, 256)
    w = np.pi * (2 * np.arange(256)[None] + 1) * np.arange(256)[:, None] / 512.0
    dft = np.stack([np.cos(w), np.sin(w)])
    out["dft"] = dft.reshape(2, 2, P, 256).transpose(2, 0, 1, 3).astype(f).reshape(P, 1024)
    idft = dft.transpose(0, 2, 1) / 256.0
    out["idft"] = idft.reshape(2, 2, P, 256).transpose(2, 0, 1, 3).astype(f).reshape(P, 1024)
    tt = np.linspace(0.0, 1.0, SEQ, dtype=f)[:, None]
    ww = (f(2.0 * math.pi) * np.arange(SEQ, dtype=f)[:, None] / f(SEQ)).astype(f)
    ff = np.linspace(1e-4, 15, 16, dtype=f)[None, :]
    out["feat"] = np.ascontiguousarray(np.concatenate([tt, np.cos(ff * ww), -np.sin(ff * ww)], 1).T.astype(f))
    lo, hi = math.log(1e-2) / 1.5, math.log(1e-2) / 0.3
    deltas = np.abs(np.linspace(lo, hi, BW, dtype=f))
    decay = np.exp(-tt * deltas).astype(f)
    back = decay.copy()
    back[0] = 0.0
    out["decay"] = np.stack([decay, back]).reshape(2, 2, P, BW).transpose(2, 0, 1, 3).reshape(P, 2048).astype(f)
    return out


class Counts:

    def __init__(self, known=None):
        self.known, self.seen, self.place = known, {}, {}

    def tick(self, stage, *who):
        self.seen[stage] = self.seen.get(stage, 0) + 1
        self.place[(stage, *who)] = self.seen[stage]
        return 1

    def skip(self, stage, n):
        self.seen[stage] = self.seen.get(stage, 0) + n

    def base(self, stage, *who):
        self.place[(stage, "base", *who)] = self.seen.get(stage, 0)
        return self.seen.get(stage, 0)

    def at(self, stage, *who):
        return self.known.place[(stage, *who)] if self.known else 1


def q_tiles(layer):
    return range(4) if layer < DEPTH - 1 else range(2, 4)


def tok0(layer):
    return 0 if layer < DEPTH - 1 else SEQ


class Group:

    def __init__(self, kind, layer, index, turn, n_chunks, tiles, first):
        self.kind, self.layer, self.index, self.turn = kind, layer, index, turn
        self.n, self.tiles, self.first = n_chunks, list(tiles), first
        self.key = (kind, layer, index)


def plan():
    steps, total = [], [0]

    def take(n):
        total[0] += n
        return total[0] - n

    def group(kind, layer, index, turn, n, tiles, between=()):
        g = Group(kind, layer, index, turn, n, tiles, take(n))
        for j in range(n):
            steps.append(("chunk", g, j))
            if j == n - 1:
                steps.append(("evac", g))
            elif between:
                steps.extend(between.pop(0))
        if between:
            steps.extend(between.pop(0))

    def ada(layer, part):
        n_groups = 4 if part == 0 else 8
        steps.append(("ada", layer, part, take(4 * n_groups), n_groups))
        steps.append(("modcols", layer, part))

    steps.append(("start",))
    steps.append(("params", 0))
    ada(0, 0)
    for layer in range(DEPTH):
        last = layer == DEPTH - 1
        qt, every = list(q_tiles(layer)), list(range(4))
        if layer:
            steps.append(("params", layer))
        for s in range(2):
            steps.append(("modulate", layer, 0, s))
        filt = [[("filter", layer, i)] for i in range(4)]
        group("a_q", layer, 0, "T", 4, qt, filt)
        steps.append(("qk_turn", layer, 0))
        group("a_k", layer, 0, "T", 4, every, filt)
        steps.append(("qk_turn", layer, 1))
        group("a_v", layer, 0, "T", 4, every, filt)
        units = [(tt, h) for tt in qt for h in range(HEADS)]
        n_u = len(units)
        mix = []
        for i in range(n_u + 3):
            mix.append([("attend", layer, i, n_u)] if i < n_u + 2 else [])
            if i >= 3 and units[i - 3][1] == HEADS - 1:
                mix[-1].append(("y_turn", layer, 0, units[i - 3][0]))
            if 2 <= i < n_u + 2 and units[i - 2][1] == HEADS - 1:
                mix[-1].append(("head_norm", layer, units[i - 2][0]))
        for j in range(3):
            group("hy", layer, j, "F", 4, range(4), mix)
        group("g_v", layer, 0, "T", 4, every, mix)
        group("g_qk", layer, 0, "F", 4, range(4), mix)
        group("z", layer, 0, "Z", 1, range(1), mix)
        seqs = [0, 1] if not last else [1]
        for s in seqs:
            mix += [[("hy_turn", layer, s)], [("hy_dft", layer, s)], [("hy_idft", layer, s)]]
        for tt in every:
            mix += [[("gla_gate", layer, tt)], [("gla_sum", layer, tt)]]
            if tt in qt:
                mix += [[("gla_att", layer, tt)]]
            mix += [[("gla_state", layer, tt)]]
        mix += [[("gla_scan", layer)]]
        for tt in qt:
            mix += [[("gla_out", layer, tt)]]
        for j in range(5):
            group("gate", layer, j, "F", 4, range(4), mix)
        steps += sum(mix, [])
        del mix[:]
        group("g_r", layer, 0, "T", 4, qt)
        for tt in qt:
            mix.append([("y_turn", layer, 1, tt)])
        group("gate", layer, 5, "F", 4, range(4), mix)
        steps += sum(mix, [])
        if not last:
            ada(layer, 1)
        else:
            steps.append(("modcols", layer, 1))
        steps.append(("y_split", layer))
        for half in range(2):
            for br in range(3):
                group("branch", layer, (half, br), "B", 2, range(4))
        for half in range(2):
            group("out", layer, half, "T", 4, qt)
        steps.append(("post", layer, 0))
        for s in seqs:
            steps.append(("modulate", layer, 1, s))
        steps.append(("up", layer, take(4 * (FT // 2)), FT // 2))
        if not last:
            ada(layer + 1, 0)
            steps.append(("ada", layer + 1, 1, take(32), 8))
        for half in range(2):
            group("down", layer, half, "D", FT // 2, qt)
        steps.append(("post", layer, 1))
    steps.append(("end",))
    return steps, total[0]


def build_program(nc, A, out, known):
    C = Counts(known)
    at, tick = C.at, C.tick
    steps, n_chunks = plan()
    ctx = ExitStack()
    with ctx:
        sems = {}

        def sem(name):
            if name not in sems:
                sems[name] = ctx.enter_context(nc.semaphore(name))
            return sems[name]

        base = (nc.sbuf_base + 31) // 32 * 32
        end = nc.sbuf_usable_end // 32 * 32
        arena = [base]

        def put(name, shape, dt=F32, offset=None):
            size = int(np.prod(shape[1:])) * 4
            if offset is None:
                offset = arena[0]
                arena[0] += (size + 31) // 32 * 32
            assert offset + size <= end, (name, offset + size - end)
            return nc.alloc_sbuf_tensor_at(name, shape, dt, offset=offset)

        stage = put("stage", [P, NBUF, 1024])
        w_hi = put("w_hi", [P, NBUF, 1024], F32R)
        w_lo = put("w_lo", [P, NBUF, 1024], F32R)
        ht_at = arena[0]
        h_hi = put("h_hi", [P, KT, TOK], F32R)
        h_lo = put("h_lo", [P, KT, TOK], F32R)
        ident = put("ident", [P, P])
        cums = put("cums", [P, 2, 256])
        tail = put("tail", [P, 2, P])
        mask = put("mask", [P, 2, P], I32)
        rope = put("rope", [P, 2, 2, 64])
        dft = put("dft", [P, 2, 2, 256])
        idft = put("idft", [P, 2, 2, 256])
        filt_at = arena[0]
        filt = put("filt", [P, 2, 2, BW])
        ada_c = put("ada_c", [P, KT, P], F32R)
        mod_row = put("mod_row", [4, 2, COLS], offset=filt_at + 4096)
        pcol = put("pcol", [P, 228])
        mod_a = put("mod_a", [P, 2, 2, KT])
        mod_b = put("mod_b", [P, 2, 4, KT])
        mrows = put("mrows", [64, 3, P])
        lam = put("lam", [P, 8])
        da_g = put("da_g", [P, P])
        gla_g = put("gla_g", [P, P])
        w_gate = put("w_gate", [33, 2 * 256])
        f_w1 = put("f_w1", [33, 64])
        f_w2 = put("f_w2", [64, 64])
        f_col = put("f_col", [64, 4])
        stat = put("stat", [P, 2, 12])
        moms = put("moms", [P, 4, 4])
        soft = put("soft", [P, 2, 12])
        hn = put("hn", [P, 4, 4])
        dec = put("dec", [P, 2, 8, 2])
        c_act = put("c_act", [P, 16])
        y_at = end - 71680 - 24576
        assert arena[0] <= y_at, arena[0] - y_at
        y = put("y", [P, 3, CT, TOK], offset=y_at)
        t_at = end - 71680

        def tmp(name, kb, shape, dt=F32, at_=t_at):
            return put(name, shape, dt, offset=at_ + int(kb * 1024))

        rows = tmp("rows", 42, [88, 3, P])
        lam_in = tmp("lam_in", 28, [P, 4, 64])
        lam_prod = tmp("lam_prod", 29, [P, 2, 64])
        f_w3 = tmp("f_w3", 66, [64, 2, BW])
        zT = tmp("zT", 40, [33, TOK])
        x_tok = tmp("x_tok", 0, [P, 4, D])
        xn = tmp("xn", 16, [P, 2, D])
        xm = tmp("xm", 24, [P, 4, SEQ])
        qT = tmp("qT", 0, [P, HEADS, TOK])
        kT = tmp("kT", 8, [P, HEADS, TOK])
        v_tok = tmp("v_tok", 16, [P, 4, BW])
        probs = tmp("probs", 24, [P, 2, 2, TOK])
        rope_t = tmp("rope_t", 24, [P, 2, 2, BW])
        qk_tok = tmp("qk_tok", 36, [P, 4, BW])
        attT = tmp("attT", 32, [P, 2, TOK])
        o_sq = tmp("o_sq", 42, [P, BW])
        y_tok = tmp("y_tok", 44, [P, BW])
        f_arg = tmp("f_arg", 46, [64, 2, 256])
        f_h = tmp("f_h", 48, [64, 2, 256])
        decay = tmp("decay", 50, [P, 2, 2, BW])
        f_t = tmp("f_t", 58, [P, 2, BW])
        f_sd = tmp("f_sd", 62, [P, 2, 2, BW])
        feat = put("feat", [33, 256], offset=t_at + 45 * 1024)
        x0T = tmp("x0T", 46, [P, CT, TOK])
        uT = tmp("uT", 54, [P, CT, TOK])
        vvT = tmp("vvT", 62, [P, 2, TOK])
        u_tok = tmp("u_tok", 0, [P, 2, BW])
        spec = tmp("spec", 8, [P, 2, 2, BW])
        spec_t = tmp("spec_t", 16, [P, 2, BW])
        hy_t = tmp("hy_t", 20, [P, 2, SEQ])
        gqk = tmp("gqk", 32, [P, 4, TOK])
        gv = put("gv", [P, 4, BW], offset=y_at + 8192)
        go = tmp("go", 0, [P, 4, BW])
        states = tmp("states", 8, [P, 2, 7, 2, P])
        la = tmp("la", 24, [P, BW])
        eb = tmp("eb", 26, [P, 3, 4, P])
        qe = tmp("qe", 42, [P, 4, P])
        ke = tmp("ke", 44, [P, 4, P])
        att = tmp("att", 46, [P, 2, 4, P])
        ku = tmp("ku", 50, [P, 2, 256])
        ktok = tmp("ktok", 52, [P, 256])
        lg = tmp("lg", 53, [P, BW])
        g_sq = tmp("g_sq", 55, [P, BW])
        rg = tmp("rg", 57, [P, 2, BW])
        etail = tmp("etail", 61, [P, 2, 256])
        sig = tmp("sig", 66, [P, 2, TOK])
        ys_hi = tmp("ys_hi", 0, [P, 3 * CT, TOK], F32R)
        ys_lo = tmp("ys_lo", 24, [P, 3 * CT, TOK], F32R)
        acc = tmp("acc", 48, [P, 4, TOK])
        sig_in = tmp("sig_in", 56, [P, 4, TOK])
        prod = tmp("prod", 64, [P, 2, TOK])
        R = []
        for n, (where, name) in enumerate(((t_at, "r1"), (ht_at, "r2"))):
            R.append(dict(
                x=put(name + "x", [P, 4, D], offset=where),
                g=put(name + "g", [P, 2, D], offset=where + 16384),
                ln=put(name + "ln", [P, 2, D], offset=where + 24576),
            ))
        R[0]["t"] = tmp("r1t", 32, [P, 2, COLS])
        R[1]["t"] = put("r2t", [P, 2, COLS], offset=filt_at)
        act_hi = put("act_hi", [P, FT, TOK], F32R, offset=y_at)
        act_lo = put("act_lo", [P, FT, TOK], F32R, offset=y_at + FT * TOK * 4)
        ffn_t = put("ffn_t", [P, 2, 2, TOK], offset=filt_at)

        ps = ctx.enter_context(nc.psum_tensor("ps", [P, 8, 512], F32))

        def dram(name, shape):
            return nc.dram_tensor(name, shape, F32, kind="Internal").ap()

        d_mod = [dram(f"d_mod{i}", [4, 6 * D]) for i in range(DEPTH)]
        d_gate = [dram(f"d_gate{i}", [2, 4 * D]) for i in range(DEPTH)]
        d_sig = [dram(f"d_sig{i}", [24, P, TOK]) for i in range(DEPTH)]
        d_x = [dram(f"d_x{i}", [4, P, D]) for i in range(2 * DEPTH - 1)]

        W_IN_AT = {"a_q": 0, "a_k": 512, "a_v": 1024, "g_qk": 1536, "g_v": 2048, "g_r": 2560,
                   "z": 3072, "hy": 3104, "gate": 4640}

        def rows_of(w, k0, nk, c0, nc_):
            return w[k0 * P:(k0 + nk) * P, c0:c0 + nc_].rearrange("(k p) n -> p k n", p=P)

        def source(g, j):
            if g.kind == "z":
                return rows_of(A["w_in"][g.layer], 0, KT, W_IN_AT["z"], P)
            if g.kind in W_IN_AT:
                return rows_of(A["w_in"][g.layer], 2 * j, 2, W_IN_AT[g.kind] + g.index * COLS, COLS)
            if g.kind == "branch":
                half, br = g.index
                return rows_of(A["w_branch"][g.layer, br], 2 * j, 2, half * COLS, COLS)
            w = A["w_out"] if g.kind == "out" else A["ffn_w_down"]
            return rows_of(w[g.layer], 2 * j, 2, g.index * COLS, COLS)

        def bc(ap, n):
            return ap.rearrange("(a n) -> a n", a=1).to_broadcast([P, n])

        block = ctx.enter_context(nc.Block())

        @block.sync
        def _(sp):
            def load(c, src, kt=2, cc=None):
                s = c % NBUF
                n = c if cc is None else cc
                if c >= NBUF:
                    sp.wait_ge(sem("lo_ready"), n + (1 - NBUF))
                sp.dma_start(stage[:, s, :].rearrange("p (k n) -> p k n", k=kt), src).then_inc(sem(f"landed{s}"), 32)

            for st in steps:
                if st[0] == "chunk":
                    g, j = st[1], st[2]
                    load(g.first + j, source(g, j), kt=KT if g.kind == "z" else 2)
                elif st[0] == "ada":
                    _, layer, part, c0, n_groups = st
                    w = A["w_ada"][layer]
                    wv = w.rearrange("(k p) (g n) -> p k g n", p=P, n=COLS)
                    g0 = 4 * part

                    def ada_group(i, slot0):
                        for j in range(4):
                            load(c0 + slot0 + j, wv[:, 2 * j:2 * j + 2, bass.ds(i + g0, 1), :].rearrange("p k a n -> p k (a n)"),
                                 cc=c0 + i * 4 + j)
                    first = 1 if c0 == 0 else 0
                    for i in range(first):
                        for j in range(4):
                            load(j, wv[:, 2 * j:2 * j + 2, g0, :])
                    with sp.Fori(first, n_groups) as i:
                        ada_group(i, 4)
                elif st[0] == "up":
                    _, layer, c0, n_groups = st
                    wv = A["ffn_w_up"][layer].rearrange("(k p) (s g n) -> p k s g n", p=P, s=2, n=256)
                    with sp.Fori(0, n_groups) as i:
                        for j in range(4):
                            s = (c0 + j) % NBUF
                            sp.wait_ge(sem("lo_ready"), i * 4 + (c0 + j - NBUF + 1))
                            for a in range(2):
                                dst = stage[:, s, :].rearrange("p (k s n) -> p k s n", k=2, s=2)[:, :, a, :]
                                src = wv[:, 2 * j:2 * j + 2, a, bass.ds(i, 1), :].rearrange("p k a n -> p k (a n)")
                                sp.dma_start(dst, src).then_inc(sem(f"landed{s}"), 16)

        @block.gpsimd
        def _(pool):
            def dma(dst, src, stage_, *who):
                pool.dma_start(dst, src, allow_slow_non_contiguous=True).then_inc(sem(stage_), 16 * tick(stage_, *who))

            def dma_in(n_stage, who, *pairs):
                for n, (dst, src) in enumerate(pairs):
                    dma(dst, src, n_stage, *who, n)

            def start():
                names = [("ident", ident), ("cums", cums), ("tail", tail), ("mask", mask), ("rope", rope),
                         ("dft", dft), ("idft", idft)]
                pool.dma_start(rows[0:8, 0, :], A["c"].rearrange("a (k p) -> (a k) p", p=P)).then_inc(sem("c_in"), 16)
                pool.dma_start(rows[8:16, 0, :], A["c_ctx"].rearrange("(k p) -> k p", p=P)).then_inc(sem("c_in"), 16)
                for name, t in names:
                    flat = {"ident": "", "cums": " a b", "tail": " a b", "mask": " a b", "rope": " a b c",
                            "dft": " a b c", "idft": " a b c"}[name]
                    dst = t[:] if not flat else t[:].rearrange(f"p{flat} -> p ({flat.strip()})")
                    pool.dma_start(dst, A[name]).then_inc(sem("consts_in"), 16)
                for tt in range(4):
                    src = (A["ctx"] if tt < 2 else A["x"])[0, (tt % 2) * P:(tt % 2 + 1) * P, :]
                    dma(x_tok[:, tt, :], src, "x_in", tt)

            def params(layer):
                if layer:
                    pool.wait_ge(sem("post_x"), at("post_x", layer - 1, 1, 3))
                    pool.wait_ge(sem("act_hi"), at("act_hi", "end", layer - 1))
                else:
                    pool.wait_ge(sem("bank_full4"), at("bank_full4", "c"))
                dma_in("params_in", (layer,),
                       (rows[0:36, 0, :], A["hy_conv_w"][layer].rearrange("w (t p) -> (w t) p", p=P)),
                       (rows[36:48, 0, :], A["hy_conv_b"][layer].rearrange("(t p) -> t p", p=P)),
                       (rows[48:52, 0, :], A["hy_skip"][layer].rearrange("(t p) -> t p", p=P)),
                       (rows[0:88, 1, :], A["ffn_conv_w"][layer, 0:2].rearrange("w (t p) -> (w t) p", p=P)),
                       (rows[0:44, 2, :], A["ffn_conv_w"][layer, 2].rearrange("(t p) -> t p", p=P)),
                       (rows[44:88, 2, :], A["ffn_conv_b"][layer].rearrange("(t p) -> t p", p=P)),
                       (lam_in[:].rearrange("p a b -> p (a b)"), bc(A["da_lambda"][layer].rearrange("a b -> (a b)"), 256)),
                       (da_g[:], bc(A["da_norm_g"][layer], P)),
                       (gla_g[:], bc(A["gla_norm_g"][layer], P)),
                       (f_w1[:], A["hy_w1"][layer]), (f_w2[:], A["hy_w2"][layer]),
                       (f_w3[:].rearrange("p a b -> p (a b)"), A["hy_w3"][layer]),
                       (f_col[:, 0:1], A["hy_b1"][layer].rearrange("(p a) -> p a", a=1)),
                       (f_col[:, 1:2], A["hy_freq1"][layer].rearrange("(p a) -> p a", a=1)),
                       (f_col[:, 2:3], A["hy_b2"][layer].rearrange("(p a) -> p a", a=1)),
                       (f_col[:, 3:4], A["hy_freq2"][layer].rearrange("(p a) -> p a", a=1)),
                       (feat[:], A["feat"]),
                       (decay[:].rearrange("p a b c -> p (a b c)"), A["decay"]))
                pool.memset(w_gate[0:32, :], 0.0).then_inc(sem("gate_zero"), tick("gate_zero", layer))
                pool.wait_ge(sem("gate_zero"), at("gate_zero", layer))
                for d in range(2):
                    dma(w_gate[16 * d:16 * d + 16, 256 * d:256 * d + 256], A["gla_w_gate"][layer, d], "params_in", layer, 100 + d)
                dma(w_gate[32:33, :], A["gla_b_gate"][layer].rearrange("d n -> (d n)").rearrange("(a n) -> a n", a=1),
                    "params_in", layer, "last")

            def ada(layer, part, c0, n_groups):
                f0 = [at(f"bank_full{b}", "base", layer, part) for b in range(2)]
                for b in range(2):
                    C.base(f"mod_out{b}", layer, part)
                cols = d_mod[layer].rearrange("r (g n) -> r g n", n=COLS)
                with pool.Fori(0, n_groups // 2) as i:
                    for b in range(2):
                        pool.wait_ge(sem(f"bank_free{b}"), i + (f0[b] + 1))
                        pool.dma_start(cols[:, bass.ds(i * 2 + (4 * part + b), 1), :].rearrange("r a n -> r (a n)"),
                                       mod_row[:, b, :]).then_inc(sem(f"mod_out{b}"), 16)
                for b in range(2):
                    C.skip(f"mod_out{b}", n_groups // 2)
                    C.base(f"mod_out{b}", "end", layer, part)

            def modcols(layer, part):
                n, w0 = (16, 0) if part == 0 else (32, 2 * D)
                for b in range(2):
                    pool.wait_ge(sem(f"mod_out{b}"), 16 * at(f"mod_out{b}", "base", "end", layer, part))
                if (layer, part) != (0, 0):
                    before = (layer, 0) if part else (layer - 1, 1)
                    pool.wait_ge(sem("mod_cols"), at("mod_cols", *before))
                    pool.wait_ge(sem("gate_out"), 16 * at("gate_out", 0)) if layer and not part else None
                for v in range(2):
                    for lo in range(2):
                        dma(mrows[v * n:(v + 1) * n, lo, :],
                            d_mod[layer][2 * lo + v, w0:w0 + n * P].rearrange("(t p) -> t p", p=P), "mod_in", layer, part, v, lo)
                    dma(mrows[v * n:(v + 1) * n, 2, :],
                        A["b_ada"][layer, w0:w0 + n * P].rearrange("(t p) -> t p", p=P), "mod_in", layer, part, v, 2)
                if part:
                    pool.wait_ge(sem("mod_sum"), at("mod_sum", layer, 1))
                    dma(d_gate[layer].rearrange("v (t p) -> (v t) p", p=P), mrows[0:64, 0, :], "gate_out", layer)

            def evac(g):
                layer = g.layer
                if g.kind == "gate":
                    for j in range(4):
                        pool.wait_ge(sem(f"bank_free{j}"), at(f"bank_full{j}", *g.key))
                        o = tok0(layer)
                        dma(d_sig[layer][4 * g.index + j, :, o:TOK], sig[:, j % 2, o:TOK], f"sig_out{j % 2}", layer, g.index, j)

            def y_split(layer):
                for j in range(2):
                    pool.wait_ge(sem(f"sig_out{j}"), 16 * at(f"sig_out{j}", layer, 5, 2 + j))
                pool.wait_ge(sem("bank_free6"), at("bank_full6", "y", layer, 1, 3))

            def chunk(g, j):
                if g.kind == "branch" and j == 0:
                    half, br = g.index
                    o = tok0(g.layer)
                    for n in range(4):
                        if (half, br) != (0, 0):
                            before = (half, br - 1) if br else (half - 1, 2)
                            pool.wait_ge(sem(f"bank_free{n}"), at(f"bank_full{n}", "branch", g.layer, before))
                        dma(sig_in[:, n, o:TOK], d_sig[g.layer][8 * br + 4 * half + n, :, o:TOK], f"sig_in{n}", g.layer, g.index)
                if g.kind in ("out", "down") and g.index == 0 and j == 0:
                    residual_loads(g.layer, 0 if g.kind == "out" else 1)

            def residual_loads(layer, which):
                r = R[which]
                if which == 0:
                    pool.wait_ge(sem("bank_full3"), at("bank_full3", "branch", layer, (1, 2)))
                    if layer:
                        pool.wait_ge(sem("x_out"), 16 * at("x_out", layer - 1, 1, 3))
                else:
                    pool.wait_ge(sem("bank_full3"), at("bank_full3", "base", "up end", layer))
                    pool.wait_ge(sem("x_out"), 16 * at("x_out", layer, 0, 3))
                for tt in q_tiles(layer):
                    if layer == 0 and which == 0:
                        src = (A["ctx"] if tt < 2 else A["x"])[0, (tt % 2) * P:(tt % 2 + 1) * P, :]
                    else:
                        src = d_x[2 * layer + which - 1][tt]
                    dma(r["x"][:, tt, :], src, "res_in", layer, which, tt)
                pool.wait_ge(sem("gate_out"), 16 * at("gate_out", layer))
                for v in range(2):
                    dma(r["g"][:, v, :], bc(d_gate[layer][v, 3 * which * D:(3 * which + 1) * D], D), "res_in", layer, which, "g", v)
                g_, b_ = ("ln1_g", "ln1_b") if which == 0 else ("ln2_g", "ln2_b")
                dma(r["ln"][:, 0, :], bc(A[g_][layer], D), "res_in", layer, which, "ln", 0)
                dma(r["ln"][:, 1, :], bc(A[b_][layer], D), "res_in", layer, which, "last")

            def post(layer, which):
                for tt in q_tiles(layer):
                    pool.wait_ge(sem("post_x"), at("post_x", layer, which, tt))
                    if layer == DEPTH - 1 and which == 1:
                        pool.dma_start(out[0, (tt - 2) * P:(tt - 1) * P, :], x_tok[:, tt, :]).then_inc(sem("stored"), 16)
                    else:
                        dma(d_x[2 * layer + which][tt], x_tok[:, tt, :], "x_out", layer, which, tt)

            def end_():
                pool.wait_ge(sem("stored"), 32)

            fns = dict(start=start, params=params, ada=ada, modcols=modcols, evac=evac, y_split=y_split,
                       chunk=chunk, post=post, end=end_)
            for st in steps:
                if st[0] in fns:
                    fns[st[0]](*st[1:])

        @block.tensor
        def _(pe):
            used = [0] * 8

            def claim(b):
                if used[b]:
                    pe.wait_ge(sem(f"bank_free{b}"), used[b])
                used[b] += 1

            def full(ins, b, *who):
                ins.then_inc(sem(f"bank_full{b}"), tick(f"bank_full{b}", *who))


            def mm(out_, lhsT, rhs, start=True, stop=True):
                return pe.matmul(out_, lhsT, rhs, start=start, stop=stop, skip_group_check=True)

            def three(out_, l_hi, l_lo, r_hi, r_lo, first, last, opens=False):
                ins = mm(out_, l_hi, r_hi, start=first, stop=False)
                if opens:
                    ins.then_inc(sem("chunk_used"), 1)
                mm(out_, l_lo, r_hi, start=False, stop=False)
                return mm(out_, l_hi, r_lo, start=False, stop=last)

            def start():
                pe.wait_ge(sem("c_in"), 32)
                pe.wait_ge(sem("consts_in"), 7 * 16)
                claim(4)
                full(pe.transpose(ps[:, 4, 0:16], rows[0:16, 0, :], ident[0:16, 0:16]), 4, "c")

            def params(layer):
                pe.wait_ge(sem("params_in"), 16 * at("params_in", layer, "last"))
                claim(4)
                pe.transpose(ps[:, 4, 0:52], rows[0:52, 0, :], ident[0:52, 0:52])
                pe.transpose(ps[:, 4, 52:140], rows[0:88, 1, :], ident[0:88, 0:88])
                full(pe.transpose(ps[:, 4, 140:228], rows[0:88, 2, :], ident[0:88, 0:88]), 4, "params", layer)

            def ada(layer, part, c0, n_groups):
                if c0 == 0:
                    pe.wait_ge(sem("ada_lo"), 1)
                u = [used[0], used[1]]
                for b in range(2):
                    C.base(f"bank_full{b}", layer, part)
                with pe.Fori(0, n_groups // 2) as i:
                    for b in range(2):
                        pe.wait_ge(sem(f"bank_free{b}"), i + u[b])
                        for j in range(4):
                            c = c0 + 4 * b + j
                            s = c % NBUF
                            pe.wait_ge(sem("lo_ready"), i * 8 + (c + 1))
                            for kk in range(2):
                                k = 2 * j + kk
                                ins = mm(ps[:, b, :], ada_c[:, k, :], w_hi[:, s, kk * 512:kk * 512 + 512], start=k == 0, stop=False)
                                if k == 0:
                                    ins.then_inc(sem("chunk_used"), 1)
                                ins = mm(ps[:, b, :], ada_c[:, k, :], w_lo[:, s, kk * 512:kk * 512 + 512],
                                         start=False, stop=k == KT - 1)
                            if j < 3:
                                ins.then_inc(sem("chunk_used"), 1)
                            else:
                                ins.then_inc(sem(f"bank_full{b}"), 1)
                for b in range(2):
                    used[b] += n_groups // 2
                    C.skip(f"bank_full{b}", n_groups // 2)

            def modcols(layer, part):
                n = 32 if part == 0 else 64
                pe.wait_ge(sem("mod_sum"), at("mod_sum", layer, part))
                claim(4)
                full(pe.transpose(ps[:, 4, 0:n], mrows[0:n, 0, :], ident[0:n, 0:n]), 4, "mod", layer, part)

            def modulate(layer, which, s):
                for t in range(2):
                    pe.wait_ge(sem("ln_x"), at("ln_x", layer, which, s, t))
                for b in range(4):
                    claim(4 + b)
                    for kk in range(2):
                        for t in range(2):
                            k = 2 * b + kk
                            ins = pe.transpose(ps[:, 4 + b, kk * 256 + t * P:kk * 256 + t * P + P],
                                               xn[:, t, k * P:(k + 1) * P], ident[:])
                    full(ins, 4 + b, "mod_x", layer, which, s)

            def chunk(g, j):
                c = g.first + j
                s = c % NBUF
                layer = g.layer
                pe.wait_ge(sem("lo_ready"), c + 1)
                if j == 0:
                    if g.kind == "a_q":
                        pe.wait_ge(sem("h_ready"), at("h_ready", layer, 0, 1, 3))
                    if g.kind == "branch" and g.index == (0, 0):
                        pe.wait_ge(sem("ys_ready"), at("ys_ready", layer, 3 * CT - 1))
                    if g.kind == "out" and g.index == 0:
                        pe.wait_ge(sem("merged"), at("merged", layer, 7))
                    if g.kind == "down" and g.index == 0:
                        pe.wait_ge(sem("act_lo"), at("act_lo", "base", "end", layer))
                t0 = tok0(layer)
                if g.kind == "a_k" or g.kind == "a_v" or g.kind == "g_v" or g.kind == "z":
                    t0 = 0
                for n in g.tiles:
                    if j == 0:
                        claim(n)
                    if g.turn == "Z":
                        for k in range(KT):
                            ins = three(ps[:, 0, :], w_hi[:, s, k * P:(k + 1) * P], w_lo[:, s, k * P:(k + 1) * P],
                                        h_hi[:, k, :], h_lo[:, k, :], k == 0, k == KT - 1, opens=k == 0)
                    for kk in range(2 if g.turn != "Z" else 0):
                        k = 2 * j + kk
                        first, last = k == 0, k == 2 * g.n - 1
                        opens = first and n == g.tiles[0]
                        if g.turn in "FB":
                            lo_t = 0 if g.kind == "g_qk" and n >= 2 else t0
                            xh, xl = (h_hi, h_lo) if g.turn == "F" else (ys_hi, ys_lo)
                            kx = k if g.turn == "F" else g.index[1] * CT + k
                            cs = slice(kk * 512 + n * P, kk * 512 + n * P + P)
                            ins = three(ps[:, n, lo_t:TOK], w_hi[:, s, cs], w_lo[:, s, cs],
                                        xh[:, kx, lo_t:TOK], xl[:, kx, lo_t:TOK], first, last, opens)
                        else:
                            xh, xl = (act_hi, act_lo) if g.turn == "D" else (h_hi, h_lo)
                            ts_, cs = slice(n * P, n * P + P), slice(kk * 512, kk * 512 + 512)
                            ins = three(ps[:, n, :], xh[:, k, ts_], xl[:, k, ts_], w_hi[:, s, cs], w_lo[:, s, cs], first, last, opens)
                    if j == g.n - 1:
                        full(ins, n, *g.key)
                if j < g.n - 1:
                    ins.then_inc(sem("chunk_used"), 1)

            def qk_turn(layer, w):
                for tt in (q_tiles(layer) if w == 0 else range(4)):
                    if tt < 2:
                        pe.wait_ge(sem(f"bank_free{tt}"), at(f"bank_full{tt}", "a_k" if w else "a_q", layer, 0))
                    else:
                        pe.wait_ge(sem("qk_ready"), at("qk_ready", layer, w, tt))
                    b = 4 + tt
                    claim(b)
                    for h in range(HEADS):
                        ins = pe.transpose(ps[:, b, h * P:(h + 1) * P], qk_tok[:, tt, h * P:(h + 1) * P], ident[:])
                    full(ins, b, "qk", layer, w, tt)

            def filter_(layer, i):
                if i == 0:
                    pe.wait_ge(sem("params_in"), 16 * at("params_in", layer, "last"))
                    claim(4)
                    full(mm(ps[0:64, 4, 0:256], f_w1[:], feat[:]), 4, "filter", layer, 0)
                if i == 1:
                    pe.wait_ge(sem("f_sin"), at("f_sin", layer, 0))
                    claim(4)
                    full(mm(ps[0:64, 4, 0:256], f_w2[:], f_h[:, 0, :]), 4, "filter", layer, 1)
                if i == 2:
                    pe.wait_ge(sem("f_sin"), at("f_sin", layer, 1))
                    for t in range(2):
                        for d in range(2):
                            claim(4 + 2 * t + d)
                            full(mm(ps[:, 4 + 2 * t + d, :], f_h[:, 1, t * P:(t + 1) * P], f_w3[:, d, :]),
                                 4 + 2 * t + d, "filter", layer, 2)
                if i == 3:
                    pe.wait_ge(sem("f_sd"), at("f_sd", layer, 1))
                    for cs in range(2):
                        for kt in range(2):
                            b = 4 + 2 * cs + kt
                            claim(b)
                            for t in range(2):
                                ins = mm(ps[:, b, :], dft[:, cs, t, kt * P:(kt + 1) * P], f_sd[:, cs, t, :], start=t == 0, stop=t == 1)
                            full(ins, b, "filter", layer, 3)

            def units(layer):
                return [(tt, h) for tt in q_tiles(layer) for h in range(HEADS)]

            def attend(layer, i, n_u):
                us = units(layer)
                if i < n_u:
                    tt, h = us[i]
                    nk = SEQ if tt < 2 else TOK
                    if i == 0:
                        pe.wait_ge(sem("bank_free7"), at("bank_full7", "qk", layer, 1, 3))
                        pe.wait_ge(sem("bank_free3"), at("bank_full3", "a_v", layer, 0))
                    for m in range(2):
                        claim(4 + m)
                        full(mm(ps[:, 4 + m, 0:nk], qT[64 * m:64 * m + 64, h, tt * P:(tt + 1) * P],
                                kT[64 * m:64 * m + 64, h, 0:nk]), 4 + m, "scores", layer, i)
                if 1 <= i <= n_u:
                    tt, h = us[i - 1]
                    nk = SEQ if tt < 2 else TOK
                    pe.wait_ge(sem("diff"), at("diff", layer, i - 1))
                    claim(6)
                    for kb in range(nk // P):
                        ins = pe.transpose(ps[:, 6, kb * P:(kb + 1) * P], probs[:, (i - 1) % 2, 0, kb * P:(kb + 1) * P], ident[:])
                    full(ins, 6, "attT", layer, i - 1)
                if i >= 2:
                    tt, h = us[i - 2]
                    nk = SEQ if tt < 2 else TOK
                    pe.wait_ge(sem("bank_free6"), at("bank_full6", "attT", layer, i - 2))
                    if h == 0:
                        claim(7)
                    for kb in range(nk // P):
                        ins = mm(ps[:, 7, h * P:(h + 1) * P], attT[:, i % 2, kb * P:(kb + 1) * P],
                                 v_tok[:, kb, h * P:(h + 1) * P], start=kb == 0, stop=kb == nk // P - 1)
                    if h == HEADS - 1:
                        full(ins, 7, "o", layer, tt)

            def y_turn(layer, br, tt):
                pe.wait_ge(sem("y_tok"), at("y_tok", layer, br, tt))
                src = y_tok[:] if br == 0 else go[:, tt, :]
                claim(6)
                for c in range(CT):
                    ins = pe.transpose(ps[:, 6, c * P:(c + 1) * P], src[:, c * P:(c + 1) * P], ident[:])
                full(ins, 6, "y", layer, br, tt)

            def hy_turn(layer, s):
                pe.wait_ge(sem("u_ready"), at("u_ready", layer, CT - 1))
                for t in range(2):
                    claim(4 + t)
                    for c in range(CT):
                        o = s * SEQ + t * P
                        ins = pe.transpose(ps[:, 4 + t, c * P:(c + 1) * P], uT[:, c, o:o + P], ident[:])
                    full(ins, 4 + t, "u", layer, s)

            def hy_dft(layer, s):
                for t in range(2):
                    pe.wait_ge(sem(f"bank_free{4 + t}"), at(f"bank_full{4 + t}", "u", layer, s))
                for kt in range(2):
                    for cs in range(2):
                        b = 4 + 2 * kt + cs
                        claim(b)
                        for t in range(2):
                            ins = mm(ps[:, b, :], dft[:, cs, t, kt * P:(kt + 1) * P], u_tok[:, t, :], start=t == 0, stop=t == 1)
                        full(ins, b, "U", layer, s)

            def hy_idft(layer, s):
                pe.wait_ge(sem("spec"), at("spec", layer, s, 1))
                for c in range(CT):
                    b = 4 + c // 2
                    if c % 2 == 0:
                        claim(b)
                    n = 0
                    for kt in range(2):
                        for cs in range(2):
                            ins = mm(ps[:, b, (c % 2) * 256:(c % 2) * 256 + 256], spec[:, cs, kt, c * P:(c + 1) * P],
                                     idft[:, cs, kt, :], start=n == 0, stop=n == 3)
                            n += 1
                    if c % 2:
                        full(ins, b, "conv", layer, s)

            def gla_gate(layer, tt):
                if tt == 0:
                    pe.wait_ge(sem("bank_free0"), at("bank_full0", "z", layer, 0))
                    pe.wait_ge(sem("z_one"), at("z_one", layer))
                    pe.wait_ge(sem("bank_free3"), at("bank_full3", "g_qk", layer, 0))
                claim(4)
                full(mm(ps[:, 4, :], zT[0:33, tt * P:(tt + 1) * P], w_gate[0:33, :]), 4, "logit", layer, tt)
                claim(5)
                for p_ in range(2):
                    ins = pe.transpose(ps[:, 5, p_ * P:(p_ + 1) * P], gqk[:, 2 + p_, tt * P:(tt + 1) * P], ident[:])
                full(ins, 5, "ktok", layer, tt)

            def gla_sum(layer, tt):
                pe.wait_ge(sem("bank_free4"), at("bank_full4", "logit", layer, tt))
                for d in range(2):
                    claim(6 + d)
                    for p_ in range(2):
                        ins = mm(ps[:, 6 + d, p_ * 256:p_ * 256 + 256], la[:, (2 * d + p_) * P:(2 * d + p_ + 1) * P], cums[:, d, :])
                    full(ins, 6 + d, "b", layer, tt)
                claim(4)
                for d in range(2):
                    ins = mm(ps[:, 4, d * 256:d * 256 + 256], tail[:, d, :], la[:, d * 256:d * 256 + 256])
                full(ins, 4, "tail", layer, tt)

            def gla_att(layer, tt):
                pe.wait_ge(sem("qke"), at("qke", layer, tt))
                for r in range(2):
                    claim(6 + r)
                    rs = slice(64 * r, 64 * r + 64)
                    for n in range(4):
                        ins = mm(ps[:, 6 + r, n * P:(n + 1) * P], ke[rs, n, :], qe[rs, n, :])
                    full(ins, 6 + r, "att", layer, tt)

            def gla_state(layer, tt):
                pe.wait_ge(sem("ku"), at("ku", layer, tt))
                if tt == 0:
                    pe.wait_ge(sem("bank_free3"), at("bank_full3", "g_v", layer, 0))
                for j in range(2):
                    claim(4 + j)
                    r = slice(64 * j, 64 * j + 64)
                    for d in range(2):
                        for h in range(HEADS):
                            o, p_ = (h % 2) * 64, h // 2
                            ins = mm(ps[o:o + 64, 4 + j, (2 * d + p_) * P:(2 * d + p_ + 1) * P], ku[r, d, h * 64:h * 64 + 64],
                                     gv[r, tt, h * P:(h + 1) * P])
                    full(ins, 4 + j, "u_state", layer, tt)
                if tt in q_tiles(layer):
                    pe.wait_ge(sem("bank_free7"), at("bank_full7", "att", layer, tt))
                    claim(6)
                    for h in range(HEADS):
                        for d in range(2):
                            ins = mm(ps[:, 6, h * P:(h + 1) * P], att[:, h % 2, 2 * d + h // 2, :], gv[:, tt, h * P:(h + 1) * P],
                                     start=d == 0, stop=d == 1)
                    full(ins, 6, "intra", layer, tt)

            def gla_out(layer, tt):
                if tt == q_tiles(layer)[0]:
                    pe.wait_ge(sem("scanned"), at("scanned", layer))
                for r in range(2):
                    claim(4 + r)
                    rs = slice(64 * r, 64 * r + 64)
                    for j in range(2):
                        c = 2 * tt + j
                        ns = [c, (3 - c) if c < 4 else (11 - c)]
                        ds_ = [d for d in range(2) if ns[d] > 0]
                        for p_ in range(2):
                            for d in ds_:
                                ins = mm(ps[64 * j:64 * j + 64, 4 + r, p_ * P:(p_ + 1) * P],
                                         gqk[rs, 2 * d + p_, tt * P + 64 * j:tt * P + 64 * j + 64], states[rs, d, ns[d] - 1, p_, :],
                                         start=d == ds_[0], stop=d == ds_[-1])
                    full(ins, 4 + r, "inter", layer, tt)

            def up(layer, c0, n_groups):
                pe.wait_ge(sem("h_ready"), at("h_ready", layer, 1, 1, 3))
                u = list(used)
                t0 = tok0(layer)
                for b in range(4):
                    C.base(f"bank_full{b}", "up", layer)
                with pe.Fori(0, n_groups) as i:
                    for j in range(4):
                        c = c0 + j
                        s = c % NBUF
                        pe.wait_ge(sem("lo_ready"), i * 4 + (c + 1))
                        for n in range(4):
                            if j == 0:
                                pe.wait_ge(sem(f"bank_free{n}"), i + u[n])
                            for kk in range(2):
                                k = 2 * j + kk
                                cs = slice(kk * 512 + n * P, kk * 512 + n * P + P)
                                ins = three(ps[:, n, t0:TOK], w_hi[:, s, cs], w_lo[:, s, cs],
                                            h_hi[:, k, t0:TOK], h_lo[:, k, t0:TOK], k == 0, k == KT - 1, k == 0 and n == 0)
                            if j == 3:
                                ins.then_inc(sem(f"bank_full{n}"), 1)
                        if j < 3:
                            ins.then_inc(sem("chunk_used"), 1)
                for b in range(4):
                    used[b] += n_groups
                    C.skip(f"bank_full{b}", n_groups)
                C.base("bank_full3", "up end", layer)

            fns = dict(start=start, params=params, ada=ada, modcols=modcols, modulate=modulate, chunk=chunk,
                       qk_turn=qk_turn, filter=filter_, attend=attend, y_turn=y_turn, hy_turn=hy_turn, hy_dft=hy_dft,
                       hy_idft=hy_idft, gla_gate=gla_gate, gla_sum=gla_sum, gla_att=gla_att, gla_state=gla_state,
                       gla_out=gla_out, up=up)
            for st in steps:
                if st[0] in fns:
                    fns[st[0]](*st[1:])

        @block.scalar
        def _(act):
            cursor = [0]

            def split(c):
                s = c % NBUF
                act.wait_ge(sem(f"landed{s}"), 32 * (c // NBUF + 1))
                if c >= NBUF:
                    act.wait_ge(sem("chunk_used"), c - NBUF + 2)
                act.activation(w_hi[:, s, :], stage[:, s, :], ACT.Copy).then_inc(sem("hi_ready"), 1)

            def split_to(c):
                while cursor[0] < min(c, n_chunks):
                    split(cursor[0])
                    cursor[0] += 1

            def bank(b, *who):
                act.wait_ge(sem(f"bank_full{b}"), at(f"bank_full{b}", *who))

            def do(ins, stage_, *who):
                ins.then_inc(sem(stage_), tick(stage_, *who))

            def free(ins, b):
                ins.then_inc(sem(f"bank_free{b}"), 1)

            def freed(b, *who):
                act.wait_ge(sem(f"bank_free{b}"), at(f"bank_full{b}", *who))

            def start():
                bank(4, "c")
                free(act.activation(c_act[:], ps[:, 4, 0:16], ACT.Silu), 4)
                freed(4, "c")
                act.wait_ge(sem("ada_zero"), 1)
                act.activation(ada_c[:, :, 0:2].rearrange("p k v -> p v k"),
                               c_act[:].rearrange("p (v k) -> p v k", v=2), ACT.Copy).then_inc(sem("ada_hi"), 1)
                split_to(AHEAD)

            def params(layer):
                bank(4, "params", layer)
                act.activation(pcol[:], ps[:, 4, 0:228], ACT.Copy).then_inc(sem("bank_free4"), 1)
                act.wait_ge(sem("lam_dot"), at("lam_dot", layer))
                do(act.activation(lam[:, 2:4], lam[:, 0:2], ACT.Exp), "lam_exp", layer)

            def ada(layer, part, c0, n_groups):
                split_to(c0 + AHEAD)
                m0 = [at(f"mod_out{b}", "base", layer, part) for b in range(2)]
                if layer:
                    act.wait_ge(sem("act_lo"), at("act_lo", "base", "end", layer - 1))
                with act.Fori(0, n_groups // 2) as i:
                    for b in range(2):
                        for j in range(4):
                            c = c0 + AHEAD + 4 * b + j
                            s = c % NBUF
                            act.wait_ge(sem(f"landed{s}"), i * 64 + 32 * (c // NBUF + 1))
                            if c >= NBUF:
                                act.wait_ge(sem("chunk_used"), i * 8 + (c - NBUF + 2))
                            else:
                                act.wait_ge(sem("chunk_used"), i * 8)
                            act.activation(w_hi[:, s, :], stage[:, s, :], ACT.Copy).then_inc(sem("hi_ready"), 1)
                        act.wait_ge(sem(f"bank_full{b}"), i + (at(f"bank_full{b}", "base", layer, part) + 1))
                        act.wait_ge(sem(f"mod_out{b}"), i * 16 + 16 * m0[b])
                        act.activation(mod_row[:, b, :], ps[0:4, b, :], ACT.Copy).then_inc(sem(f"bank_free{b}"), 1)
                cursor[0] += 4 * n_groups

            def modcols(layer, part):
                n = 32 if part == 0 else 64
                bank(4, "mod", layer, part)
                dst = (mod_a if part == 0 else mod_b)[:].rearrange("p v w k -> p (v w k)")
                free(act.activation(dst, ps[:, 4, 0:n], ACT.Copy), 4)

            def modulate(layer, which, s):
                for t in range(2):
                    act.wait_ge(sem("ln_var"), at("ln_var", layer, which, s, t))
                    do(act.activation(moms[:, t, 3:4], moms[:, t, 2:3], ACT.Sqrt), "ln_std", layer, which, s, t)
                v = 1 - s
                act.wait_ge(sem("mod_cols"), at("mod_cols", layer, which))
                for b in range(4):
                    bank(4 + b, "mod_x", layer, which, s)
                    if b >= 2:
                        act.wait_ge(sem("h_ready"), at("h_ready", layer, which, s, b - 2))
                    elif (layer, which, s) != (0, 0, 0):
                        prev = (layer, which, 0) if s == 1 and (which, layer) != (1, DEPTH - 1) else \
                            (layer, 0, 1) if which else (layer - 1, 1, 1)
                        act.wait_ge(sem("h_ready"), at("h_ready", *prev, 3))
                    for kk in range(2):
                        k = 2 * b + kk
                        sc = mod_a[:, v, 1, k:k + 1] if which == 0 else mod_b[:, v, 2, k:k + 1]
                        sh = mod_a[:, v, 0, k:k + 1] if which == 0 else mod_b[:, v, 1, k:k + 1]
                        ins = act.activation(xm[:, k % 4, :], ps[:, 4 + b, kk * 256:kk * 256 + 256], ACT.Identity, bias=sh, scale=sc)
                    free(ins, 4 + b)

            def chunk(g, j):
                split_to(g.first + j + 1 + AHEAD)

            def evac(g):
                layer, kind = g.layer, g.kind
                t0 = tok0(layer)
                if kind in ("a_q", "a_k"):
                    w = 0 if kind == "a_q" else 1
                    for tt in g.tiles:
                        if tt < 2:
                            if w == 1:
                                if layer < DEPTH - 1:
                                    act.wait_ge(sem(f"bank_full{4 + tt}"), at(f"bank_full{4 + tt}", "qk", layer, 0, tt))
                            bank(tt, *g.key)
                            free(act.activation(qk_tok[:, tt, :], ps[:, tt, :], ACT.Copy), tt)
                if kind == "a_v":
                    for tt in g.tiles:
                        bank(tt, *g.key)
                        free(act.activation(v_tok[:, tt, :], ps[:, tt, :], ACT.Copy), tt)
                if kind == "hy":
                    part = g.index
                    if part == 0:
                        freed(7, "filter", layer, 3)
                    for n in range(4):
                        t = 4 * part + n
                        bank(n, *g.key)
                        if part == 2 and n >= 2:
                            act.wait_ge(sem("u_ready"), at("u_ready", layer, n - 2))
                        dst = (x0T, uT, vvT)[part][:, n % 2 if part == 2 else n, t0:TOK]
                        do(act.activation(dst, ps[:, n, t0:TOK], ACT.Identity, bias=pcol[:, 36 + t:37 + t],
                                          scale=pcol[:, 12 + t:13 + t]), "conv_mid", layer, part, n)
                if kind == "g_v":
                    for tt in g.tiles:
                        bank(tt, *g.key)
                        free(act.activation(gv[:, tt, :], ps[:, tt, :], ACT.Copy), tt)
                if kind == "g_qk":
                    act.wait_ge(sem("bank_full6"), at("bank_full6", "y", layer, 0, 3))
                    for n in range(4):
                        bank(n, *g.key)
                        lo_t = 0 if n >= 2 else t0
                        free(act.activation(gqk[:, n, lo_t:TOK], ps[:, n, lo_t:TOK], ACT.Copy, scale=0.125 if n < 2 else 1.0), n)
                if kind == "z":
                    bank(0, *g.key)
                    free(act.activation(zT[0:32, :], ps[0:32, 0, :], ACT.Copy), 0)
                if kind == "gate":
                    for j in range(4):
                        bank(j, *g.key)
                        if (g.index, j) >= (0, 2):
                            n = 4 * g.index + j - 2
                            act.wait_ge(sem(f"sig_out{j % 2}"), 16 * at(f"sig_out{j % 2}", layer, n // 4, n % 4))
                        free(act.activation(sig[:, j % 2, t0:TOK], ps[:, j, t0:TOK], ACT.Sigmoid), j)
                if kind == "g_r":
                    for n, tt in enumerate(g.tiles):
                        bank(tt, *g.key)
                        if n >= 2:
                            act.wait_ge(sem("y_tok"), at("y_tok", layer, 1, tt - 2))
                        free(act.activation(rg[:, tt % 2, :], ps[:, tt, :], ACT.Silu), tt)
                if kind == "branch":
                    half, br = g.index
                    if br == 2:
                        for n in range(4):
                            act.wait_ge(sem("gated"), at("gated", layer, g.index, n))
                            do(act.activation(h_hi[:, 4 * half + n, t0:TOK], acc[:, n, t0:TOK], ACT.Copy), "merged_hi", layer, 4 * half + n)

            def qk_turn(layer, w):
                for tt in (q_tiles(layer) if w == 0 else range(4)):
                    b = 4 + tt
                    bank(b, "qk", layer, w, tt)
                    dst = (qT if w == 0 else kT)[:, :, tt * P:(tt + 1) * P]
                    if layer:
                            act.wait_ge(sem("x_out"), 16 * at("x_out", layer - 1, 1, 3))
                    free(act.activation(dst, ps[:, b, :].rearrange("p (h t) -> p h t", h=HEADS), ACT.Copy), b)

            def filter_(layer, i):
                if i < 2:
                    act.wait_ge(sem("f_arg"), at("f_arg", layer, i))
                    do(act.activation(f_h[:, i, :], f_arg[:, 0, :], ACT.Sin), "f_sin", layer, i)
                if i == 3:
                    for b in range(2):
                        act.wait_ge(sem(f"mod_out{b}"), 16 * at(f"mod_out{b}", "base", "end", layer, 1 if layer else 0))
                    for cs in range(2):
                        for kt in range(2):
                            b = 4 + 2 * cs + kt
                            bank(b, "filter", layer, 3)
                            free(act.activation(filt[:, cs, kt, :], ps[:, b, :], ACT.Copy), b)

            def attend(layer, i, n_u):
                us = [(tt, h) for tt in q_tiles(layer) for h in range(HEADS)]
                if i < n_u:
                    nk = SEQ if us[i][0] < 2 else TOK
                    act.wait_ge(sem("neg_max"), at("neg_max", layer, i))
                    for m in range(2):
                        free(act.activation(probs[:, i % 2, m, 0:nk], ps[:, 4 + m, 0:nk], ACT.Exp, bias=soft[:, i % 2, 2 + m:3 + m],
                                            scale=0.125, accum_out=soft[:, i % 2, 4 + m:5 + m]), 4 + m)
                if 1 <= i <= n_u:
                    nk = SEQ if us[i - 1][0] < 2 else TOK
                    bank(6, "attT", layer, i - 1)
                    free(act.activation(attT[:, (i - 1) % 2, 0:nk], ps[:, 6, 0:nk], ACT.Copy), 6)

            def head_norm(layer, tt):
                bank(7, "o", layer, tt)
                do(act.activation(o_sq[:], ps[:, 7, :], ACT.Square), "o_sq", layer, tt)
                act.wait_ge(sem("hn_var"), at("hn_var", layer, 0, tt))
                do(act.activation(hn[:, 1, :], hn[:, 0, :], ACT.Sqrt), "hn_std", layer, 0, tt)

            def y_turn(layer, br, tt):
                bank(6, "y", layer, br, tt)
                free(act.activation(y[:, br, :, tt * P:(tt + 1) * P], ps[:, 6, :].rearrange("p (c t) -> p c t", c=CT), ACT.Copy), 6)

            def hy_turn(layer, s):
                for t in range(2):
                    bank(4 + t, "u", layer, s)
                    free(act.activation(u_tok[:, t, :], ps[:, 4 + t, :], ACT.Copy), 4 + t)

            def gla_gate(layer, tt):
                if tt == 0:
                    act.wait_ge(sem("y_hyena"), at("y_hyena", layer, 1, CT - 1))
                else:
                    freed(4, "logit", layer, tt - 1)
                bank(4, "logit", layer, tt)
                do(act.activation(lg[:], ps[:, 4, :], ACT.Abs), "lg_abs", layer, tt)
                act.wait_ge(sem("lg_abs"), at("lg_abs", layer, tt))
                do(act.activation(lg[:], lg[:], ACT.Exp, scale=-1.0), "lg_exp", layer, tt)
                act.wait_ge(sem("lg_exp"), at("lg_exp", layer, tt))
                do(act.activation(lg[:], lg[:], ACT.Ln, bias=1.0), "lg", layer, tt)
                bank(5, "ktok", layer, tt)
                if tt > 0:
                    act.wait_ge(sem("ku"), at("ku", layer, tt - 1))
                free(act.activation(ktok[:], ps[:, 5, 0:256], ACT.Copy), 5)

            def gla_sum(layer, tt):
                for d in range(2):
                    bank(6 + d, "b", layer, tt)
                src = ps[:, 6:8, :].rearrange("p d (a b t) -> p (d a) b t", a=2, b=2)
                if tt > 0:
                    act.wait_ge(sem("ku"), at("ku", layer, tt - 1))
                    act.wait_ge(sem("dec"), at("dec", layer, tt - 1, 1))
                    if tt - 1 in q_tiles(layer):
                        act.wait_ge(sem("qke"), at("qke", layer, tt - 1))
                ins = act.activation(eb[:, 0, :, :], src[:, :, 0, :], ACT.Exp)
                if tt in q_tiles(layer):
                    act.activation(eb[:, 1, :, :], src[:, :, 1, :], ACT.Exp)
                    ins = act.activation(eb[:, 2, :, :], src[:, :, 1, :], ACT.Exp, scale=-1.0)
                free(ins, 6)
                bank(4, "tail", layer, tt)
                for d, b in ((0, 7), (1, 4)):
                    free(act.activation(etail[:, d, :], ps[:, 4, d * 256:d * 256 + 256], ACT.Exp), b)

            def gla_state(layer, tt):
                for j in range(2):
                    bank(4 + j, "u_state", layer, tt)
                    slots = [((2 * tt + j) if d == 0 else (3 if tt < 2 else 11) - 2 * tt - j, d) for d in range(2)]
                    for n, d in [x for x in slots if x[0] < 7]:
                        ins = act.activation(states[:, d, n, :, :].rearrange("p a v -> p (a v)"),
                                             ps[:, 4 + j, 256 * d:256 * d + 256], ACT.Copy)
                    free(ins, 4 + j)
                if tt in q_tiles(layer):
                    bank(6, "intra", layer, tt)
                    free(act.activation(go[:, tt, :], ps[:, 6, :], ACT.Copy), 6)

            def gla_out(layer, tt):
                freed(5, "inter", layer, tt)
                do(act.activation(g_sq[:], go[:, tt, :], ACT.Square), "g_sq", layer, tt)
                act.wait_ge(sem("hn_var"), at("hn_var", layer, 1, tt))
                do(act.activation(hn[:, 1, :], hn[:, 0, :], ACT.Sqrt), "hn_std", layer, 1, tt)

            def y_split(layer):
                t0 = tok0(layer)
                freed(6, "y", layer, 1, 3)
                act.wait_ge(sem("y_hyena"), at("y_hyena", layer, 1, CT - 1))
                for j in range(2):
                    act.wait_ge(sem(f"sig_out{j}"), 16 * at(f"sig_out{j}", layer, 5, 2 + j))
                for n in range(3 * CT):
                    do(act.activation(ys_hi[:, n, t0:TOK], y[:, n // CT, n % CT, t0:TOK], ACT.Copy), "ys_hi", layer, n)

            def post(layer, which):
                for n, tt in enumerate(q_tiles(layer)):
                    act.wait_ge(sem("post_var"), at("post_var", layer, which, tt))
                    do(act.activation(moms[:, tt, 3:4], moms[:, tt, 2:3], ACT.Sqrt), "post_std", layer, which, tt)

            def up(layer, c0, n_groups):
                split_to(c0 + AHEAD)
                t0 = tok0(layer)
                W0, W1, W2, B = 52, 52 + 44, 140, 184
                e0 = C.base("up_mid", layer)
                b0 = [at(f"bank_full{b}", "base", "up", layer) for b in range(4)]
                l0 = at("act_lo", "base", layer)
                p0 = at("up_prod", "base", layer)
                C.base("up_gelu", layer)
                C.base("act_hi", layer)
                act.wait_ge(sem("x_out"), 16 * at("x_out", layer, 0, 3))
                with act.Fori(0, n_groups) as i:
                    for j in range(4):
                        c = c0 + AHEAD + j
                        s = c % NBUF
                        act.wait_ge(sem(f"landed{s}"), i * 32 + 32 * (c // NBUF + 1))
                        act.wait_ge(sem("chunk_used"), i * 4 + (c - NBUF + 2))
                        act.activation(w_hi[:, s, :], stage[:, s, :], ACT.Copy).then_inc(sem("hi_ready"), 1)
                    for p_ in range(2):
                        act.wait_ge(sem("act_lo"), i * 2 + (l0 + p_ - 1))
                        for a in range(2):
                            b = 2 * a + p_
                            act.wait_ge(sem(f"bank_full{b}"), i + (b0[b] + 1))
                            act.activation(ffn_t[:, p_, a, t0:TOK], ps[:, b, t0:TOK], ACT.Identity,
                                           bias=pcol[:, bass.ds(i * 2 + (B + 22 * a + p_), 1)],
                                           scale=pcol[:, bass.ds(i * 2 + (W1 + 22 * a + p_), 1)]).then_inc(sem("up_mid"), 1)
                    for p_ in range(2):
                        act.wait_ge(sem(f"bank_free{2 + p_}"), i + (b0[2 + p_] + 1))
                        act.activation(ffn_t[:, p_, 1, t0:TOK], ffn_t[:, p_, 1, t0:TOK], ACT.Gelu_apprx_tanh).then_inc(sem("up_gelu"), 1)
                    for p_ in range(2):
                        act.wait_ge(sem("up_prod"), i * 2 + (p0 + p_ + 1))
                        act.activation(act_hi[:, bass.ds(i * 2 + p_, 1), t0:TOK].rearrange("p a t -> p (a t)"),
                                       ffn_t[:, p_, 0, t0:TOK], ACT.Copy).then_inc(sem("act_hi"), 1)
                C.skip("up_mid", 4 * n_groups)
                C.skip("up_gelu", 2 * n_groups)
                C.skip("act_hi", 2 * n_groups)
                C.place[("act_hi", "end", layer)] = C.seen["act_hi"]
                cursor[0] += 4 * n_groups

            fns = dict(start=start, params=params, ada=ada, modcols=modcols, modulate=modulate, chunk=chunk, evac=evac,
                       qk_turn=qk_turn, filter=filter_, attend=attend, head_norm=head_norm, y_turn=y_turn,
                       hy_turn=hy_turn, gla_gate=gla_gate, gla_sum=gla_sum, gla_state=gla_state, gla_out=gla_out, y_split=y_split,
                       post=post, up=up)
            for st in steps:
                if st[0] in fns:
                    fns[st[0]](*st[1:])

        @block.vector
        def _(dve):
            cursor, chain = [0], [0]

            def link(ins):
                chain[0] += 1
                ins.then_inc(sem("dve_chain"), 1)
                dve.wait_ge(sem("dve_chain"), chain[0])

            def split(c):
                s = c % NBUF
                dve.wait_ge(sem("hi_ready"), c + 1)
                dve.tensor_tensor(w_lo[:, s, :], stage[:, s, :], w_hi[:, s, :].bitcast(F32), ALU.subtract)\
                   .then_inc(sem("lo_ready"), 1)

            def split_to(c):
                while cursor[0] < min(c, n_chunks):
                    split(cursor[0])
                    cursor[0] += 1

            def bank(b, *who):
                dve.wait_ge(sem(f"bank_full{b}"), at(f"bank_full{b}", *who))

            def freed(b, *who):
                dve.wait_ge(sem(f"bank_free{b}"), at(f"bank_full{b}", *who))

            def do(ins, stage_, *who):
                ins.then_inc(sem(stage_), tick(stage_, *who))

            def done(stage_, *who):
                dve.wait_ge(sem(stage_), at(stage_, *who))

            def free(ins, b):
                ins.then_inc(sem(f"bank_free{b}"), 1)

            def wide(ap, n, axis=1):
                a = ap.unsqueeze(axis)
                shape = list(a.shape)
                shape[axis] = n
                return a.broadcast_to(shape)

            def start():
                dve.memset(ada_c[:].bitcast(F32), 0.0).then_inc(sem("ada_zero"), 1)
                dve.wait_ge(sem("ada_hi"), 1)
                dve.tensor_tensor(ada_c[:, :, 2:4].rearrange("p k v -> p v k"), c_act[:].rearrange("p (v k) -> p v k", v=2),
                                  ada_c[:, :, 0:2].rearrange("p k v -> p v k").bitcast(F32), ALU.subtract).then_inc(sem("ada_lo"), 1)
                split_to(AHEAD)

            def params(layer):
                lam_init = 0.8 - 0.6 * math.exp(-0.3 * layer)
                dve.wait_ge(sem("params_in"), 16 * at("params_in", layer, "last"))
                lv = lam_in[:].rearrange("p (a b) n -> p a b n", b=2)
                link(dve.tensor_tensor(lam_prod[:], lv[:, :, 0, :], lv[:, :, 1, :], ALU.mult))
                do(dve.tensor_reduce(lam[:, 0:2], lam_prod[:], AX_X, ALU.add), "lam_dot", layer)
                done("lam_exp", layer)
                link(dve.tensor_tensor(lam[:, 4:5], lam[:, 3:4], lam[:, 2:3], ALU.subtract))
                link(dve.tensor_scalar(lam[:, 5:6], lam[:, 4:5], -lam_init, None, ALU.add))
                link(dve.tensor_scalar(da_g[:], da_g[:], 1.0 - lam_init, None, ALU.mult))

            def ada(layer, part, c0, n_groups):
                split_to(c0 + AHEAD)
                with dve.Fori(0, n_groups // 2) as i:
                    for j in range(8):
                        c = c0 + AHEAD + j
                        s = c % NBUF
                        dve.wait_ge(sem("hi_ready"), i * 8 + (c + 1))
                        dve.tensor_tensor(w_lo[:, s, :], stage[:, s, :], w_hi[:, s, :].bitcast(F32), ALU.subtract)\
                           .then_inc(sem("lo_ready"), 1)
                cursor[0] += 4 * n_groups

            def modcols(layer, part):
                n = 32 if part == 0 else 64
                dve.wait_ge(sem("mod_in"), 16 * at("mod_in", layer, part, 1, 2))
                link(dve.tensor_tensor(mrows[0:n, 0, :], mrows[0:n, 0, :], mrows[0:n, 1, :], ALU.add))
                do(dve.tensor_tensor(mrows[0:n, 0, :], mrows[0:n, 0, :], mrows[0:n, 2, :], ALU.add), "mod_sum", layer, part)
                freed(4, "mod", layer, part)
                col = mod_a[:, :, 1, :] if part == 0 else mod_b[:, :, 2, :]
                do(dve.tensor_scalar(col, col, 1.0, None, ALU.add), "mod_cols", layer, part)

            def moments(src, m, st):
                dve.bn_stats(stat[:, st, 0:6], src[:, 0:512])
                link(dve.bn_stats(stat[:, st, 6:12], src[:, 512:1024]))
                link(dve.bn_aggr(moms[:, m, 0:2], stat[:, st, :]))
                return dve.tensor_scalar(moms[:, m, 2:3], moms[:, m, 1:2], EPS, None, ALU.add)

            def modulate(layer, which, s):
                if (layer, which, s) == (0, 0, 0):
                    dve.wait_ge(sem("x_in"), 64)
                for t in range(2):
                    if which or layer:
                        done("post_x", layer if which else layer - 1, 0 if which else 1, 2 * s + t)
                    do(moments(x_tok[:, 2 * s + t, :], t, t), "ln_var", layer, which, s, t)
                for t in range(2):
                    done("ln_std", layer, which, s, t)
                    link(dve.reciprocal(moms[:, t, 2:3], moms[:, t, 3:4]))
                    do(dve.tensor_scalar(xn[:, t, :], x_tok[:, 2 * s + t, :], moms[:, t, 0:1], moms[:, t, 2:3],
                                         ALU.subtract, ALU.mult), "ln_x", layer, which, s, t)
                    done("ln_x", layer, which, s, t)
                cols = slice(s * SEQ, (s + 1) * SEQ)
                for b in range(4):
                    freed(4 + b, "mod_x", layer, which, s)
                    src = xm[:, (2 * b) % 4:(2 * b) % 4 + 2, :]
                    link(dve.tensor_copy(h_hi[:, 2 * b:2 * b + 2, cols], src))
                    do(dve.tensor_tensor(h_lo[:, 2 * b:2 * b + 2, cols], src, h_hi[:, 2 * b:2 * b + 2, cols].bitcast(F32), ALU.subtract),
                       "h_ready", layer, which, s, b)

            def chunk(g, j):
                split_to(g.first + j + 1 + AHEAD)

            def seqs(ap, layer):
                t0 = tok0(layer)
                return ap[:, t0:TOK].rearrange("p (s t) -> p s t", t=SEQ)

            def taps(dst, src, w0, w2):
                first = dve.scalar_tensor_tensor(out=dst[:, :, 1:SEQ], in0=src[:, :, 0:SEQ - 1], scalar=w0, in1=dst[:, :, 1:SEQ],
                                                 op0=ALU.mult, op1=ALU.add)
                link(first)
                return dve.scalar_tensor_tensor(out=dst[:, :, 0:SEQ - 1], in0=src[:, :, 1:SEQ], scalar=w2, in1=dst[:, :, 0:SEQ - 1],
                                                op0=ALU.mult, op1=ALU.add)

            def evac(g):
                layer, kind = g.layer, g.kind
                t0 = tok0(layer)
                if kind in ("a_q", "a_k"):
                    w = 0 if kind == "a_q" else 1
                    for tt in (2, 3):
                        bank(tt, *g.key)
                        if w == 1:
                            bank(4 + tt, "qk", layer, 0, tt)
                            done("qk_ready", layer, 0, tt)
                        src = ps[:, tt, :].rearrange("p (h n) -> p h n", n=64)
                        cos, sin = rope[:, tt - 2, 0, :], rope[:, tt - 2, 1, :]
                        ta, tb = rope_t[:, tt - 2, 0, :], rope_t[:, tt - 2, 1, :]
                        dve.tensor_tensor(ta.rearrange("p (h n) -> p h n", n=64), src, wide(cos, 8), ALU.mult)
                        halves = ps[:, tt, :].rearrange("p (h a n) -> p h a n", a=2, n=16)
                        tv = tb.rearrange("p (h a n) -> p h a n", a=2, n=16)
                        sv = sin.rearrange("p (f a n) -> p f a n", a=2, n=16)
                        for a in range(2):
                            for f in range(2):
                                ins = dve.tensor_tensor(tv.rearrange("p (h f) a n -> p h f a n", f=2)[:, :, f, a, :],
                                                        halves.rearrange("p (h f) a n -> p h f a n", f=2)[:, :, f, 1 - a, :],
                                                        wide(sv[:, f, a, :], 8), ALU.mult)
                        free(ins, tt)
                        freed(tt, *g.key)
                        do(dve.tensor_tensor(qk_tok[:, tt, :], ta, tb, ALU.add), "qk_ready", layer, w, tt)
                if kind == "hy":
                    part = g.index
                    for n in range(4):
                        t = 4 * part + n
                        tile_ = (x0T, uT, vvT)[part][:, n % 2 if part == 2 else n, :]
                        done("conv_mid", layer, part, n)
                        bank(n, *g.key)
                        free(taps(seqs(tile_, layer), seqs(ps[:, n, :], layer), pcol[:, t:t + 1], pcol[:, 24 + t:25 + t]), n)
                        if part == 2:
                            freed(n, *g.key)
                            do(dve.tensor_tensor(uT[:, n, t0:TOK], uT[:, n, t0:TOK], vvT[:, n % 2, t0:TOK], ALU.mult),
                               "u_ready", layer, n)
                if kind == "z":
                    bank(0, *g.key)
                    do(dve.memset(zT[32:33, :], 1.0), "z_one", layer)
                if kind == "g_r":
                    for tt in g.tiles:
                        freed(tt, *g.key)
                        r4 = rg[:, tt % 2, :].rearrange("p (h n) -> p h n", h=HEADS)
                        link(dve.tensor_tensor(r4, r4, wide(gla_g[:], HEADS), ALU.mult))
                        do(dve.tensor_tensor(go[:, tt, :], go[:, tt, :], rg[:, tt % 2, :], ALU.mult), "y_tok", layer, 1, tt)
                if kind == "branch":
                    half, br = g.index
                    for n in range(4):
                        dve.wait_ge(sem(f"sig_in{n}"), 16 * at(f"sig_in{n}", layer, g.index))
                        bank(n, *g.key)
                        if half and br == 0:
                            done("merged", layer, n)
                        if br and (br, n) != (1, 0):
                            prev = ((half, br), n - 2) if n >= 2 else ((half, br - 1), n + 2)
                            if prev[0][1]:
                                done("gated", layer, *prev)
                        dst = acc[:, n, t0:TOK] if br == 0 else prod[:, n % 2, t0:TOK]
                        free(dve.tensor_tensor(dst, ps[:, n, t0:TOK], sig_in[:, n, t0:TOK], ALU.mult), n)
                        if br:
                            freed(n, *g.key)
                            do(dve.tensor_tensor(acc[:, n, t0:TOK], acc[:, n, t0:TOK], dst, ALU.add), "gated", layer, g.index, n)
                    if br == 2:
                        for n in range(4):
                            k = 4 * half + n
                            done("merged_hi", layer, k)
                            do(dve.tensor_tensor(h_lo[:, k, t0:TOK], acc[:, n, t0:TOK], h_hi[:, k, t0:TOK].bitcast(F32), ALU.subtract),
                               "merged", layer, k)
                if kind in ("out", "down"):
                    which = 0 if kind == "out" else 1
                    r, half = R[which], g.index
                    if half == 0:
                        dve.wait_ge(sem("res_in"), 16 * at("res_in", layer, which, "last"))
                    cols = slice(half * COLS, half * COLS + COLS)
                    for tt in g.tiles:
                        bank(tt, *g.key)
                        t = r["t"][:, tt % 2, :]
                        free(dve.tensor_tensor(t, ps[:, tt, :], r["g"][:, 1 if tt < 2 else 0, cols], ALU.mult), tt)
                        freed(tt, *g.key)
                        link(dve.scalar_tensor_tensor(out=r["x"][:, tt, cols], in0=r["x"][:, tt, cols], scalar=ALPHA, in1=t,
                                                      op0=ALU.mult, op1=ALU.add))

            def post(layer, which):
                r = R[which]
                for tt in q_tiles(layer):
                    do(moments(r["x"][:, tt, :], tt, tt % 2), "post_var", layer, which, tt)
                if which and layer < DEPTH - 1:
                    dve.wait_ge(sem("bank_full3"), at("bank_full3", "down", layer, 1))
                for tt in q_tiles(layer):
                    done("post_std", layer, which, tt)
                    link(dve.reciprocal(moms[:, tt, 2:3], moms[:, tt, 3:4]))
                    link(dve.tensor_scalar(x_tok[:, tt, :], r["x"][:, tt, :], moms[:, tt, 0:1], moms[:, tt, 2:3],
                                           ALU.subtract, ALU.mult))
                    link(dve.tensor_tensor(x_tok[:, tt, :], x_tok[:, tt, :], r["ln"][:, 0, :], ALU.mult))
                    do(dve.tensor_tensor(x_tok[:, tt, :], x_tok[:, tt, :], r["ln"][:, 1, :], ALU.add), "post_x", layer, which, tt)
                    done("post_x", layer, which, tt)

            def filter_(layer, i):
                c1 = 6.28125
                c2 = float(np.float32(np.round((TWO_PI - c1) * 2 ** 20) / 2 ** 20))
                c3 = float(np.float32(TWO_PI - c1 - c2))
                if i < 2:
                    bank(4, "filter", layer, i)
                    free(dve.tensor_scalar(f_arg[:, 0, :], ps[0:64, 4, 0:256], f_col[:, 2 * i:2 * i + 1],
                                           f_col[:, 2 * i + 1:2 * i + 2], ALU.add, ALU.mult), 4)
                    freed(4, "filter", layer, i)
                    link(dve.tensor_scalar(f_arg[:, 1, :], f_arg[:, 0, :], 1.0 / TWO_PI, ROUND, ALU.mult, ALU.add))
                    link(dve.tensor_scalar(f_arg[:, 1, :], f_arg[:, 1, :], -ROUND, None, ALU.add))
                    for c in (c1, c2, c3):
                        link(dve.scalar_tensor_tensor(out=f_arg[:, 0, :], in0=f_arg[:, 1, :], scalar=-c, in1=f_arg[:, 0, :],
                                                      op0=ALU.mult, op1=ALU.add))
                    do(dve.tensor_scalar(f_arg[:, 0, :], f_arg[:, 0, :], -3.1415925, 3.1415925, ALU.max, ALU.min), "f_arg", layer, i)
                if i == 2:
                    bank(7, "filter", layer, 2)
                    for t in range(2):
                        for d in range(2):
                            bank(4 + 2 * t + d, "filter", layer, 2)
                            ins = dve.tensor_tensor(f_t[:, d, :], ps[:, 4 + 2 * t + d, :], decay[:, d, t, :], ALU.mult)
                            free(ins, 4 + 2 * t + d)
                        freed(5 + 2 * t, "filter", layer, 2)
                        dve.tensor_tensor(f_sd[:, 0, t, :], f_t[:, 0, :], f_t[:, 1, :], ALU.add)
                        do(dve.tensor_tensor(f_sd[:, 1, t, :], f_t[:, 0, :], f_t[:, 1, :], ALU.subtract), "f_sd", layer, t)
                        done("f_sd", layer, t)

            def attend(layer, i, n_u):
                us = [(tt, h) for tt in q_tiles(layer) for h in range(HEADS)]
                if i >= n_u:
                    return
                nk = SEQ if us[i][0] < 2 else TOK
                s = soft[:, i % 2, :]
                for m in range(2):
                    bank(4 + m, "scores", layer, i)
                if i >= 2:
                    done("diff", layer, i - 2)
                link(dve.tensor_reduce(s[:, 0:2], ps[:, 4:6, 0:nk], AX_X, ALU.max))
                do(dve.tensor_scalar(s[:, 2:4], s[:, 0:2], -0.125, None, ALU.mult), "neg_max", layer, i)
                for m in range(2):
                    freed(4 + m, "scores", layer, i)
                link(dve.reciprocal(s[:, 6:8], s[:, 4:6]))
                link(dve.tensor_tensor(s[:, 8:9], s[:, 7:8], lam[:, 5:6], ALU.mult))
                link(dve.tensor_scalar(probs[:, i % 2, 1, 0:nk], probs[:, i % 2, 1, 0:nk], s[:, 8:9], None, ALU.mult))
                do(dve.scalar_tensor_tensor(out=probs[:, i % 2, 0, 0:nk], in0=probs[:, i % 2, 0, 0:nk], scalar=s[:, 6:7],
                                            in1=probs[:, i % 2, 1, 0:nk], op0=ALU.mult, op1=ALU.add), "diff", layer, i)

            def norms(sq, layer, br, tt):
                link(dve.tensor_reduce(hn[:, 3, :], sq[:].rearrange("p (h n) -> p h n", h=HEADS), AX_X, ALU.add))
                do(dve.tensor_scalar(hn[:, 0, :], hn[:, 3, :], 1.0 / P, EPS, ALU.mult, ALU.add), "hn_var", layer, br, tt)
                done("hn_std", layer, br, tt)
                link(dve.reciprocal(hn[:, 2, :], hn[:, 1, :]))

            def head_norm(layer, tt):
                done("o_sq", layer, tt)
                norms(o_sq, layer, 0, tt)
                bank(7, "o", layer, tt)
                prev = tt - 1
                if prev in q_tiles(layer):
                    bank(6, "y", layer, 0, prev)
                y4 = y_tok[:].rearrange("p (h n) -> p h n", h=HEADS)
                free(dve.tensor_tensor(y4, ps[:, 7, :].rearrange("p (h n) -> p h n", h=HEADS), wide(hn[:, 2, :], P, 2), ALU.mult), 7)
                freed(7, "o", layer, tt)
                do(dve.tensor_tensor(y4, y4, wide(da_g[:], HEADS), ALU.mult), "y_tok", layer, 0, tt)

            def hy_dft(layer, s):
                for kt in range(2):
                    re, im = 4 + 2 * kt, 5 + 2 * kt
                    bank(re, "U", layer, s)
                    bank(im, "U", layer, s)
                    dve.tensor_tensor(spec_t[:, 0, :], ps[:, re, :], filt[:, 0, kt, :], ALU.mult)
                    link(dve.tensor_tensor(spec_t[:, 1, :], ps[:, im, :], filt[:, 1, kt, :], ALU.mult))
                    link(dve.tensor_tensor(spec[:, 0, kt, :], spec_t[:, 0, :], spec_t[:, 1, :], ALU.subtract))
                    free(dve.tensor_tensor(spec_t[:, 0, :], ps[:, re, :], filt[:, 1, kt, :], ALU.mult), re)
                    free(dve.tensor_tensor(spec_t[:, 1, :], ps[:, im, :], filt[:, 0, kt, :], ALU.mult), im)
                    freed(im, "U", layer, s)
                    do(dve.tensor_tensor(spec[:, 1, kt, :], spec_t[:, 0, :], spec_t[:, 1, :], ALU.add), "spec", layer, s, kt)
                    done("spec", layer, s, kt)

            def hy_idft(layer, s):
                cols = slice(s * SEQ, (s + 1) * SEQ)
                for c in range(CT):
                    b = 4 + c // 2
                    bank(b, "conv", layer, s)
                    if c >= 2:
                        done("y_hyena", layer, s, c - 2)
                    ins = dve.scalar_tensor_tensor(out=hy_t[:, c % 2, :], in0=uT[:, c, cols], scalar=pcol[:, 48 + c:49 + c],
                                                   in1=ps[:, b, (c % 2) * 256:(c % 2) * 256 + 256], op0=ALU.mult, op1=ALU.add)
                    if c % 2:
                        free(ins, b)
                        freed(b, "conv", layer, s)
                    else:
                        link(ins)
                    do(dve.tensor_tensor(y[:, 2, c, cols], hy_t[:, c % 2, :], x0T[:, c, cols], ALU.mult), "y_hyena", layer, s, c)

            def gla_gate(layer, tt):
                done("lg", layer, tt)
                if tt > 0:
                    bank(4, "tail", layer, tt - 1)
                if tt == 0:
                    link(dve.memset(att[:], 0.0))
                free(dve.scalar_tensor_tensor(out=la[:], in0=ps[:, 4, :], scalar=0.0, in1=lg[:], op0=ALU.min, op1=ALU.subtract), 4)

            def gla_sum(layer, tt):
                freed(6, "b", layer, tt)
                freed(4, "tail", layer, tt)
                freed(5, "ktok", layer, tt)
                if tt > 0:
                    bank(5, "u_state", layer, tt - 1)
                do(dve.tensor_tensor(ku[:], etail[:], wide(ktok[:], 2), ALU.mult), "ku", layer, tt)
                for j in range(2):
                    c = 2 * tt + j
                    for d in range(2):
                        n = c if d == 0 else (3 - c if c < 4 else 11 - c)
                        t = 64 * j + (63 if d == 0 else 0)
                        do(dve.tensor_copy(dec[:, d, n, :], eb[:, 0, 2 * d:2 * d + 2, t]), "dec", layer, tt, 2 * j + d)
                if tt in q_tiles(layer):
                    if tt > q_tiles(layer)[0]:
                        bank(7, "att", layer, tt - 1)
                    cols = slice(tt * P, (tt + 1) * P)
                    four = lambda ap: ap.rearrange("p (d a) t -> p d a t", d=2)
                    dve.tensor_tensor(four(qe[:]), four(eb[:, 1, :, :]), wide(gqk[:, 0:2, cols], 2), ALU.mult)
                    link(dve.tensor_tensor(four(ke[:]), four(eb[:, 2, :, :]), wide(gqk[:, 2:4, cols], 2), ALU.mult))
                    link(dve.tensor_tensor(gqk[:, 2:4, cols], gqk[:, 0:2, cols], eb[:, 0, 2:4, :], ALU.mult))
                    do(dve.tensor_tensor(gqk[:, 0:2, cols], gqk[:, 0:2, cols], eb[:, 0, 0:2, :], ALU.mult), "qke", layer, tt)

            def gla_att(layer, tt):
                if tt > q_tiles(layer)[0]:
                    bank(6, "intra", layer, tt - 1)
                for r in range(2):
                    bank(6 + r, "att", layer, tt)
                    free(dve.copy_predicated(att[:, r, :, :].rearrange("p (d a) t -> p d a t", d=2), wide(mask[:], 2, 2),
                                             ps[:, 6 + r, :].rearrange("p (d a t) -> p d a t", d=2, a=2)), 6 + r)

            def gla_scan(layer):
                for d in range(2):
                    freed(4 + d, "u_state", layer, 3)
                done("dec", layer, 3, 3)
                for n in range(1, 7):
                    for d in range(2):
                        for p_ in range(2):
                            ins = dve.scalar_tensor_tensor(out=states[:, d, n, p_, :], in0=states[:, d, n - 1, p_, :],
                                                           scalar=dec[:, d, n, p_:p_ + 1], in1=states[:, d, n, p_, :],
                                                           op0=ALU.mult, op1=ALU.add)
                    if n < 6:
                        link(ins)
                do(ins, "scanned", layer)

            def gla_out(layer, tt):
                freed(6, "intra", layer, tt)
                for r in range(2):
                    bank(4 + r, "inter", layer, tt)
                    part = go[:, tt, :].rearrange("p (a r n) -> p a r n", a=2, r=2)[:, :, r, :]
                    free(dve.tensor_tensor(part, part, ps[:, 4 + r, 0:256].rearrange("p (a n) -> p a n", a=2), ALU.add), 4 + r)
                done("g_sq", layer, tt)
                norms(g_sq, layer, 1, tt)
                g4 = go[:, tt, :].rearrange("p (h n) -> p h n", h=HEADS)
                link(dve.tensor_tensor(g4, g4, wide(hn[:, 2, :], P, 2), ALU.mult))

            def y_split(layer):
                t0 = tok0(layer)
                for n in range(3 * CT):
                    done("ys_hi", layer, n)
                    do(dve.tensor_tensor(ys_lo[:, n, t0:TOK], y[:, n // CT, n % CT, t0:TOK], ys_hi[:, n, t0:TOK].bitcast(F32),
                                         ALU.subtract), "ys_ready", layer, n)

            def up(layer, c0, n_groups):
                split_to(c0 + AHEAD)
                t0 = tok0(layer)
                W0, W2 = 52, 140
                if layer == 0:
                    dve.sem_inc(sem("act_lo"), 2)
                    C.skip("act_lo", 2)
                C.base("act_lo", layer)
                C.base("up_prod", layer)
                C.base("up_tap", layer)
                l0 = C.seen.get("up_tap", 0)
                b0 = [at(f"bank_full{b}", "base", "up", layer) for b in range(4)]
                m0, g0, h0 = at("up_mid", "base", layer), at("up_gelu", "base", layer), at("act_hi", "base", layer)
                dve.wait_ge(sem("x_out"), 16 * at("x_out", layer, 0, 3))
                with dve.Fori(0, n_groups) as i:
                    for j in range(4):
                        c = c0 + AHEAD + j
                        s = c % NBUF
                        dve.wait_ge(sem("hi_ready"), i * 4 + (c + 1))
                        dve.tensor_tensor(w_lo[:, s, :], stage[:, s, :], w_hi[:, s, :].bitcast(F32), ALU.subtract)\
                           .then_inc(sem("lo_ready"), 1)
                    for p_ in range(2):
                        for side in range(2):
                            for a in range(2):
                                b = 2 * a + p_
                                dst, src = seqs(ffn_t[:, p_, a, :], layer), seqs(ps[:, b, :], layer)
                                to, of = (slice(1, SEQ), slice(0, SEQ - 1)) if side == 0 else (slice(0, SEQ - 1), slice(1, SEQ))
                                col = pcol[:, bass.ds(i * 2 + ((W0, W2)[side] + 22 * a + p_), 1)]
                                if side == 0:
                                    dve.wait_ge(sem("up_mid"), i * 4 + (m0 + 2 * p_ + a + 1))
                                else:
                                    dve.wait_ge(sem("up_tap"), i * 4 + (l0 + 2 * p_ + a + 1))
                                dve.scalar_tensor_tensor(out=dst[:, :, to], in0=src[:, :, of], scalar=col, in1=dst[:, :, to],
                                                         op0=ALU.mult, op1=ALU.add)\
                                   .then_inc(sem("up_tap") if side == 0 else sem(f"bank_free{b}"), 1)
                    for p_ in range(2):
                        dve.wait_ge(sem("up_gelu"), i * 2 + (g0 + p_ + 1))
                        dve.wait_ge(sem(f"bank_free{p_}"), i + (b0[p_] + 1))
                        dve.tensor_tensor(ffn_t[:, p_, 0, t0:TOK], ffn_t[:, p_, 0, t0:TOK], ffn_t[:, p_, 1, t0:TOK], ALU.mult)\
                           .then_inc(sem("up_prod"), 1)
                    for p_ in range(2):
                        dve.wait_ge(sem("act_hi"), i * 2 + (h0 + p_ + 1))
                        dst = act_lo[:, bass.ds(i * 2 + p_, 1), t0:TOK].rearrange("p a t -> p (a t)")
                        hi = act_hi[:, bass.ds(i * 2 + p_, 1), t0:TOK].rearrange("p a t -> p (a t)").bitcast(F32)
                        dve.tensor_tensor(dst, ffn_t[:, p_, 0, t0:TOK], hi, ALU.subtract).then_inc(sem("act_lo"), 1)
                C.skip("act_lo", 2 * n_groups)
                C.skip("up_prod", 2 * n_groups)
                C.skip("up_tap", 4 * n_groups)
                C.base("act_lo", "end", layer)
                cursor[0] += 4 * n_groups

            fns = dict(start=start, params=params, ada=ada, modcols=modcols, modulate=modulate, chunk=chunk, evac=evac,
                       filter=filter_, attend=attend, head_norm=head_norm, hy_dft=hy_dft, hy_idft=hy_idft,
                       gla_gate=gla_gate, gla_sum=gla_sum, gla_att=gla_att, gla_scan=gla_scan, gla_out=gla_out,
                       y_split=y_split, post=post, up=up)
            for st in steps:
                if st[0] in fns:
                    fns[st[0]](*st[1:])
    return C


INPUTS = ["x", "c", "ctx", "c_ctx", "w_ada", "b_ada", "w_in", "da_lambda", "da_norm_g", "gla_w_gate", "gla_b_gate",
          "gla_norm_g", "hy_conv_w", "hy_conv_b", "hy_w1", "hy_b1", "hy_freq1", "hy_w2", "hy_b2", "hy_freq2", "hy_w3",
          "hy_skip", "w_branch", "w_out", "ln1_g", "ln1_b", "ffn_w_up", "ffn_conv_w", "ffn_conv_b", "ffn_w_down",
          "ln2_g", "ln2_b"]


def kernel(**inputs):
    import concourse.bacc as bacc
    from concourse.bass_utils import run_bass_kernel_spmd

    arrays = {name: np.ascontiguousarray(inputs[name]) for name in INPUTS}
    arrays.update(shape_constants())

    def build(known):
        nc = bacc.Bacc("TRN2", target_bir_lowering=False, num_devices=1)
        args = {n: nc.dram_tensor("in_" + n, a.shape, mybir.dt.from_np(a.dtype), kind="ExternalInput").ap()
                for n, a in arrays.items()}
        out = nc.dram_tensor("out_x", (1, SEQ, D), F32, kind="ExternalOutput").ap()
        return nc, build_program(nc, args, out, known)

    _, counts = build(None)
    nc, _ = build(counts)
    r = run_bass_kernel_spmd(nc, [{"in_" + n: a for n, a in arrays.items()}], core_ids=[0])
    return r.results[0]["out_x"]
```

```python
import math
from contextlib import ExitStack

import numpy as np
import concourse.bass as bass
from concourse import mybir

F32 = mybir.dt.float32
F32R = mybir.dt.float32r
I32 = mybir.dt.int32
ACT = mybir.ActivationFunctionType
ALU = mybir.AluOpType
AX_X = mybir.AxisListType.X

P = 128
D = 1024
DEPTH = 2
SEQ = 256
TOK = 2 * SEQ
KT = D // P
HEADS = 4
BW = 512
CT = BW // P
DFF = 2816
FT = DFF // P
CHUNK = 64
EPS = 1e-5
ALPHA = (2.0 * DEPTH) ** 0.25
COLS = 512
NBUF = 4
AHEAD = 3
TWO_PI = 2.0 * math.pi
ROUND = 12582912.0


def shape_constants():
    f = np.float32
    out = {"ident": np.eye(P, dtype=f)}
    s, t = np.meshgrid(np.arange(P), np.arange(P), indexing="ij")
    same = s // CHUNK == t // CHUNK
    first = t // CHUNK * CHUNK
    upto = [same & (s <= t), same & (s >= t)]
    ref = [same & (s <= first + CHUNK // 2), same & (s >= first + CHUNK // 2 - 1)]
    after = [same & (s > t), same & (s < t)]
    tau = 1.0 / 16.0
    cums = [np.concatenate([upto[d] * tau, (upto[d].astype(f) - ref[d].astype(f)) * tau], 1) for d in range(2)]
    out["cums"] = np.stack(cums, 1).astype(f).reshape(P, 2 * 256)
    out["tail"] = np.stack([after[d] * tau for d in range(2)], 1).astype(f).reshape(P, 2 * P)
    out["mask"] = np.stack([upto[0], upto[1]], 1).astype(np.int32).reshape(P, 2 * P)
    pos = np.arange(SEQ)
    inv = (10000.0 ** (-np.arange(16, dtype=f) / f(16))).astype(f)
    row, col = (pos // 64).astype(f)[:, None] * inv, (pos % 64).astype(f)[:, None] * inv
    ang = np.concatenate([row, row, col, col], 1)
    sign = np.tile(np.concatenate([-np.ones(16), np.ones(16)]), 2)[None]
    out["rope"] = np.stack([np.cos(ang), np.sin(ang) * sign], 1).astype(f).reshape(2, P, P).transpose(1, 0, 2).reshape(P, 256)
    w = np.pi * (2 * np.arange(256)[None] + 1) * np.arange(256)[:, None] / 512.0
    dft = np.stack([np.cos(w), np.sin(w)])
    out["dft"] = dft.reshape(2, 2, P, 256).transpose(2, 0, 1, 3).astype(f).reshape(P, 1024)
    idft = dft.transpose(0, 2, 1) / 256.0
    out["idft"] = idft.reshape(2, 2, P, 256).transpose(2, 0, 1, 3).astype(f).reshape(P, 1024)
    tt = np.linspace(0.0, 1.0, SEQ, dtype=f)[:, None]
    ww = (f(2.0 * math.pi) * np.arange(SEQ, dtype=f)[:, None] / f(SEQ)).astype(f)
    ff = np.linspace(1e-4, 15, 16, dtype=f)[None, :]
    out["feat"] = np.ascontiguousarray(np.concatenate([tt, np.cos(ff * ww), -np.sin(ff * ww)], 1).T.astype(f))
    lo, hi = math.log(1e-2) / 1.5, math.log(1e-2) / 0.3
    deltas = np.abs(np.linspace(lo, hi, BW, dtype=f))
    decay = np.exp(-tt * deltas).astype(f)
    back = decay.copy()
    back[0] = 0.0
    out["decay"] = np.stack([decay, back]).reshape(2, 2, P, BW).transpose(2, 0, 1, 3).reshape(P, 2048).astype(f)
    return out


class Counts:

    def __init__(self, known=None):
        self.known, self.seen, self.place = known, {}, {}

    def tick(self, stage, *who):
        self.seen[stage] = self.seen.get(stage, 0) + 1
        self.place[(stage, *who)] = self.seen[stage]
        return 1

    def skip(self, stage, n):
        self.seen[stage] = self.seen.get(stage, 0) + n

    def base(self, stage, *who):
        self.place[(stage, "base", *who)] = self.seen.get(stage, 0)
        return self.seen.get(stage, 0)

    def at(self, stage, *who):
        return self.known.place[(stage, *who)] if self.known else 1


def q_tiles(layer):
    return range(4) if layer < DEPTH - 1 else range(2, 4)


def tok0(layer):
    return 0 if layer < DEPTH - 1 else SEQ


ADA_GROUPS = (range(0, 4), range(4, 12))
UP_GROUPS = FT // 2


def norms(layer, which, then):
    tiles = list(q_tiles(layer))
    steps = []
    for n, tt in enumerate(tiles):
        steps.append(("post", layer, which, tt))
        if then:
            steps.append(("moments", *then, tt))
            if n:
                steps.append(("normal", *then, tt - 1))
                if tt == 2 and which == 0:
                    steps.append(("modulate", *then, 0))
    if then:
        steps.append(("normal", *then, tiles[-1]))
        if which and tiles[0] == 0:
            steps.append(("modulate", *then, 0))
        steps.append(("modulate", *then, 1))
    return steps


class Group:

    def __init__(self, kind, layer, index, turn, n_chunks, tiles):
        self.kind, self.layer, self.index, self.turn = kind, layer, index, turn
        self.n, self.tiles = n_chunks, list(tiles)
        self.at = []
        self.key = (kind, layer, index)


def plan():
    steps = []

    def group(kind, layer, index, turn, n, tiles, between=()):
        g = Group(kind, layer, index, turn, n, tiles)
        for j in range(n):
            steps.append(("chunk", g, j))
            if j == n - 1:
                steps.append(("evac", g))
            elif between:
                steps.extend(between.pop(0))
        if between:
            steps.extend(between.pop(0))

    def ada(layer, part):
        out = []
        for i in ADA_GROUPS[part]:
            g = Group("ada", layer, i, "A", 4, [4 + i % 2])
            out += [[("chunk", g, j)] for j in range(4)]
            out[-1].append(("evac", g))
        return out

    def spread(slots, chunks, first, per):
        for n, item in enumerate(chunks):
            slots[first + n // per] += item

    steps += [("start",), ("params", 0)]
    steps += sum(ada(0, 0), [])
    steps += [("consts",), ("modload", 0, 0), ("modcols", 0, 0)]
    for s in range(2):
        for tt in (2 * s, 2 * s + 1):
            steps += [("moments", 0, 0, tt)]
        for tt in (2 * s, 2 * s + 1):
            steps += [("normal", 0, 0, tt)]
        steps += [("modulate", 0, 0, s)]
    for layer in range(DEPTH):
        last = layer == DEPTH - 1
        qt, every = list(q_tiles(layer)), list(range(4))
        filt = [[("params_turn", layer), ("filter", layer, 0)]] + [[("filter", layer, i)] for i in range(1, 4)]
        if layer:
            filt.append([("modcols", layer, 1)])
        group("a_q", layer, 0, "T", 4, qt, filt)
        steps.append(("qk_turn", layer, 0))
        group("a_k", layer, 0, "T", 4, every, filt)
        steps.append(("qk_turn", layer, 1))
        group("a_v", layer, 0, "T", 4, every, filt)
        units = [(tt, h) for tt in qt for h in range(HEADS)]
        n_u = len(units)
        mix = []
        for i in range(n_u + 3):
            mix.append([("attend", layer, i, n_u)] if i < n_u + 2 else [])
            if i >= 3 and units[i - 3][1] == HEADS - 1:
                mix[-1].append(("y_turn", layer, 0, units[i - 3][0]))
            if 2 <= i < n_u + 2 and units[i - 2][1] == HEADS - 1:
                mix[-1].append(("head_norm", layer, units[i - 2][0]))
        for j in range(3):
            group("hy", layer, j, "F", 4, range(4), mix)
        group("g_v", layer, 0, "T", 4, every, mix)
        group("g_qk", layer, 0, "F", 4, range(4), mix)
        group("z", layer, 0, "Z", 1, range(1), mix)
        seqs = [0, 1] if not last else [1]
        for s in seqs:
            mix += [[("hy_turn", layer, s)], [("hy_dft", layer, s)], [("hy_idft", layer, s)]]
        mix += [[("gla_gate", layer, 0)], [("gla_sum", layer, 0)]]
        for tt in every:
            if tt < 3:
                mix += [[("gla_gate", layer, tt + 1)]]
            if tt in qt:
                mix += [[("gla_att", layer, tt)]]
            mix += [[("gla_state", layer, tt)]]
            if tt < 3:
                mix += [[("gla_sum", layer, tt + 1)]]
        mix += [[("gla_scan", layer)]]
        for tt in qt:
            mix += [[("gla_out", layer, tt)]]
        for j in range(5):
            group("gate", layer, j, "F", 4, range(4), mix)
        steps += sum(mix, [])
        del mix[:]
        slots = [[] for _ in range(20)]
        for n, tt in enumerate(qt):
            slots[4 + n].append(("y_turn", layer, 1, tt))
        if not last:
            spread(slots, ada(layer, 1), 0, 2)
            slots[16].append(("modload", layer, 1))
            slots[18].append(("modcols", layer, 1))
        group("g_r", layer, 0, "T", 4, qt, slots)
        group("gate", layer, 5, "F", 4, range(4), slots)
        steps.append(("y_split", layer))
        for half in range(2):
            for br in range(3):
                group("branch", layer, (half, br), "B", 2, range(4), slots)
        for half in range(2):
            group("out", layer, half, "T", 4, qt)
        steps += norms(layer, 0, (layer, 1))
        steps.append(["up", layer, None])
        slots = [[] for _ in range(FT)]
        if not last:
            spread(slots, ada(layer + 1, 0), 0, 2)
            slots[10].append(("modload", layer + 1, 0))
            slots[12].append(("modcols", layer + 1, 0))
            spread(slots, ada(layer + 1, 1), 8, 3)
            slots[20].append(("modload", layer + 1, 1))
        for half in range(2):
            group("down", layer, half, "D", FT // 2, qt, slots)
        if not last:
            steps.append(("params", layer + 1))
        steps += norms(layer, 1, None if last else (layer + 1, 0))
    steps.append(("end",))
    total = 0
    for st in steps:
        if st[0] == "chunk":
            st[1].at.append(total)
            total += 1
        elif st[0] == "up":
            st[2] = total
            total += 4 * UP_GROUPS
    return steps, total


def build_program(nc, A, out, known):
    C = Counts(known)
    at, tick = C.at, C.tick
    steps, n_chunks = plan()
    ctx = ExitStack()
    with ctx:
        sems = {}

        def sem(name):
            if name not in sems:
                sems[name] = ctx.enter_context(nc.semaphore(name))
            return sems[name]

        base = (nc.sbuf_base + 31) // 32 * 32
        end = nc.sbuf_usable_end // 32 * 32
        arena = [base]

        def put(name, shape, dt=F32, offset=None):
            size = int(np.prod(shape[1:])) * 4
            if offset is None:
                offset = arena[0]
                arena[0] += (size + 31) // 32 * 32
            assert offset + size <= end, (name, offset + size - end)
            return nc.alloc_sbuf_tensor_at(name, shape, dt, offset=offset)

        stage = put("stage", [P, NBUF, 1024])
        w_hi = put("w_hi", [P, NBUF, 1024], F32R)
        w_lo = put("w_lo", [P, NBUF, 1024], F32R)
        ht_at = arena[0]
        h_hi = put("h_hi", [P, KT, TOK], F32R)
        h_lo = put("h_lo", [P, KT, TOK], F32R)
        ident = put("ident", [P, P])
        cums = put("cums", [P, 2, 256])
        tail = put("tail", [P, 2, P])
        mask = put("mask", [P, 2, P], I32)
        rope = put("rope", [P, 2, 2, 64])
        dft = put("dft", [P, 2, 2, 256])
        idft = put("idft", [P, 2, 2, 256])
        filt_at = arena[0]
        filt = put("filt", [P, 2, 2, BW])
        ada_c = put("ada_c", [P, KT, P], F32R)
        mod_row = put("mod_row", [4, 2, COLS], offset=filt_at + 4096)
        pcol = put("pcol", [P, 228])
        mod_a = put("mod_a", [P, 2, 2, KT])
        mod_b = put("mod_b", [P, 2, 4, KT])
        mrows = put("mrows", [64, 3, P])
        lam = put("lam", [P, 8])
        da_g = put("da_g", [P, P])
        gla_g = put("gla_g", [P, P])
        w_gate = put("w_gate", [33, 2 * 256])
        f_w1 = put("f_w1", [33, 64])
        f_w2 = put("f_w2", [64, 64])
        f_col = put("f_col", [64, 4])
        stat = put("stat", [P, 8, 12])
        moms = put("moms", [P, 8, 5])
        soft = put("soft", [P, 2, 12])
        hn = put("hn", [P, 4, 4])
        dec = put("dec", [P, 2, 8, 2])
        c_act = put("c_act", [P, 16])
        y_at = end - 71680 - 24576
        assert arena[0] <= y_at, arena[0] - y_at
        y = put("y", [P, 3, CT, TOK], offset=y_at)
        t_at = end - 71680

        def tmp(name, kb, shape, dt=F32, at_=t_at):
            return put(name, shape, dt, offset=at_ + int(kb * 1024))

        rows = tmp("rows", 42, [88, 3, P])
        lam_in = tmp("lam_in", 43.5, [P, 4, 64])
        lam_prod = tmp("lam_prod", 44.5, [P, 2, 64])
        f_w3 = tmp("f_w3", 66, [64, 2, BW])
        zT = tmp("zT", 40, [33, TOK])
        x_tok = tmp("x_tok", 0, [P, 4, D])
        xn = [tmp("xn_mix", 16, [P, 4, D]), tmp("xn_ffn", 36, [P, 4, D])]
        xm = tmp("xm", 32, [P, 4, SEQ])
        qT = tmp("qT", 0, [P, HEADS, TOK])
        kT = tmp("kT", 8, [P, HEADS, TOK])
        v_tok = tmp("v_tok", 16, [P, 4, BW])
        probs = tmp("probs", 24, [P, 2, 2, TOK])
        rope_t = tmp("rope_t", 24, [P, 2, 2, BW])
        qk_tok = tmp("qk_tok", 36, [P, 4, BW])
        attT = tmp("attT", 32, [P, 2, TOK])
        o_sq = tmp("o_sq", 42, [P, BW])
        y_tok = tmp("y_tok", 44, [P, BW])
        f_arg = tmp("f_arg", 46, [64, 2, 256])
        f_h = tmp("f_h", 48, [64, 2, 256])
        decay = tmp("decay", 50, [P, 2, 2, BW])
        f_t = tmp("f_t", 58, [P, 2, BW])
        f_sd = tmp("f_sd", 62, [P, 2, 2, BW])
        feat = put("feat", [33, 256], offset=t_at + 45 * 1024)
        x0T = tmp("x0T", 46, [P, CT, TOK])
        uT = tmp("uT", 54, [P, CT, TOK])
        vvT = tmp("vvT", 62, [P, 2, TOK])
        u_tok = tmp("u_tok", 0, [P, 2, BW])
        spec = tmp("spec", 8, [P, 2, 2, BW])
        spec_t = tmp("spec_t", 16, [P, 2, BW])
        hy_t = tmp("hy_t", 20, [P, 2, SEQ])
        gqk = tmp("gqk", 32, [P, 4, TOK])
        gv = put("gv", [P, 4, BW], offset=y_at + 8192)
        go = tmp("go", 0, [P, 4, BW])
        states = tmp("states", 8, [P, 2, 7, 2, P])
        la = tmp("la", 24, [P, BW])
        eb = tmp("eb", 26, [P, 3, 4, P])
        qe = tmp("qe", 42, [P, 4, P])
        ke = tmp("ke", 44, [P, 4, P])
        att = tmp("att", 46, [P, 2, 4, P])
        ku = tmp("ku", 50, [P, 2, 256])
        ktok = tmp("ktok", 52, [P, 256])
        lg = tmp("lg", 53, [P, BW])
        g_sq = tmp("g_sq", 55, [P, BW])
        rg = tmp("rg", 57, [P, 2, BW])
        etail = tmp("etail", 61, [P, 2, 256])
        sig = tmp("sig", 66, [P, 2, TOK])
        ys_hi = tmp("ys_hi", 0, [P, 3 * CT, TOK], F32R)
        ys_lo = tmp("ys_lo", 24, [P, 3 * CT, TOK], F32R)
        acc = tmp("acc", 48, [P, 4, TOK])
        sig_in = tmp("sig_in", 56, [P, 4, TOK])
        prod = tmp("prod", 64, [P, 2, TOK])
        R = []
        for n, (where, name) in enumerate(((t_at, "r1"), (ht_at, "r2"))):
            R.append(dict(
                x=put(name + "x", [P, 4, D], offset=where),
                g=put(name + "g", [P, 2, D], offset=where + 16384),
                ln=put(name + "ln", [P, 2, D], offset=where + 24576),
            ))
        R[0]["t"] = tmp("r1t", 32, [P, 2, COLS])
        R[1]["t"] = put("r2t", [P, 2, COLS], offset=filt_at)
        act_hi = put("act_hi", [P, FT, TOK], F32R, offset=y_at)
        act_lo = put("act_lo", [P, FT, TOK], F32R, offset=y_at + FT * TOK * 4)
        ffn_t = put("ffn_t", [P, 2, 2, TOK], offset=filt_at)

        ps = ctx.enter_context(nc.psum_tensor("ps", [P, 8, 512], F32))

        def dram(name, shape):
            return nc.dram_tensor(name, shape, F32, kind="Internal").ap()

        d_mod = [dram(f"d_mod{i}", [4, 6 * D]) for i in range(DEPTH)]
        d_gate = [dram(f"d_gate{i}", [2, 4 * D]) for i in range(DEPTH)]
        d_sig = [dram(f"d_sig{i}", [24, P, TOK]) for i in range(DEPTH)]
        d_x = [dram(f"d_x{i}", [4, P, D]) for i in range(2 * DEPTH - 1)]

        W_IN_AT = {"a_q": 0, "a_k": 512, "a_v": 1024, "g_qk": 1536, "g_v": 2048, "g_r": 2560,
                   "z": 3072, "hy": 3104, "gate": 4640}

        def rows_of(w, k0, nk, c0, nc_):
            return w[k0 * P:(k0 + nk) * P, c0:c0 + nc_].rearrange("(k p) n -> p k n", p=P)

        def source(g, j):
            if g.kind == "ada":
                return rows_of(A["w_ada"][g.layer], 2 * j, 2, g.index * COLS, COLS)
            if g.kind == "z":
                return rows_of(A["w_in"][g.layer], 0, KT, W_IN_AT["z"], P)
            if g.kind in W_IN_AT:
                return rows_of(A["w_in"][g.layer], 2 * j, 2, W_IN_AT[g.kind] + g.index * COLS, COLS)
            if g.kind == "branch":
                half, br = g.index
                return rows_of(A["w_branch"][g.layer, br], 2 * j, 2, half * COLS, COLS)
            w = A["w_out"] if g.kind == "out" else A["ffn_w_down"]
            return rows_of(w[g.layer], 2 * j, 2, g.index * COLS, COLS)

        def bc(ap, n):
            return ap.rearrange("(a n) -> a n", a=1).to_broadcast([P, n])

        block = ctx.enter_context(nc.Block())

        @block.sync
        def _(sp):
            def load(c, src, kt=2):
                s = c % NBUF
                if c >= NBUF:
                    sp.wait_ge(sem("lo_ready"), c + 1 - NBUF)
                sp.dma_start(stage[:, s, :].rearrange("p (k n) -> p k n", k=kt), src).then_inc(sem(f"landed{s}"), 32)

            for st in steps:
                if st[0] == "start":
                    sp.dma_start(ident[:], A["ident"]).then_inc(sem("ident_in"), 16)
                elif st[0] == "consts":
                    for name, t in (("dft", dft), ("rope", rope), ("idft", idft), ("cums", cums), ("tail", tail), ("mask", mask)):
                        flat = " a b c" if name in ("rope", "dft", "idft") else " a b"
                        sp.dma_start(t[:].rearrange(f"p{flat} -> p ({flat.strip()})"), A[name]).then_inc(sem("consts_in"), 16)
                elif st[0] == "chunk":
                    g, j = st[1], st[2]
                    load(g.at[j], source(g, j), kt=KT if g.kind == "z" else 2)
                elif st[0] == "up":
                    layer, c0, n_groups = st[1], st[2], UP_GROUPS
                    wv = A["ffn_w_up"][layer].rearrange("(k p) (s g n) -> p k s g n", p=P, s=2, n=256)
                    with sp.Fori(0, n_groups) as i:
                        for j in range(4):
                            s = (c0 + j) % NBUF
                            sp.wait_ge(sem("lo_ready"), i * 4 + (c0 + j - NBUF + 1))
                            for a in range(2):
                                dst = stage[:, s, :].rearrange("p (k s n) -> p k s n", k=2, s=2)[:, :, a, :]
                                src = wv[:, 2 * j:2 * j + 2, a, bass.ds(i, 1), :].rearrange("p k a n -> p k (a n)")
                                sp.dma_start(dst, src).then_inc(sem(f"landed{s}"), 16)

        @block.gpsimd
        def _(pool):
            def dma(dst, src, stage_, *who):
                pool.dma_start(dst, src, allow_slow_non_contiguous=True).then_inc(sem(stage_), 16 * tick(stage_, *who))

            def dma_in(n_stage, who, *pairs):
                for n, (dst, src) in enumerate(pairs):
                    dma(dst, src, n_stage, *who, n)

            def start():
                pool.dma_start(rows[0:8, 0, :], A["c"].rearrange("a (k p) -> (a k) p", p=P)).then_inc(sem("c_in"), 16)
                pool.dma_start(rows[8:16, 0, :], A["c_ctx"].rearrange("(k p) -> k p", p=P)).then_inc(sem("c_in"), 16)
            def params(layer):
                if layer:
                    pool.wait_ge(sem("bank_full3"), at("bank_full3", "down", layer - 1, 1))
                    pool.wait_ge(sem("act_hi"), at("act_hi", "end", layer - 1))
                else:
                    pool.wait_ge(sem("bank_full4"), at("bank_full4", "c"))
                dma_in("params_in", (layer,),
                       (rows[0:36, 0, :], A["hy_conv_w"][layer].rearrange("w (t p) -> (w t) p", p=P)),
                       (rows[36:48, 0, :], A["hy_conv_b"][layer].rearrange("(t p) -> t p", p=P)),
                       (rows[48:52, 0, :], A["hy_skip"][layer].rearrange("(t p) -> t p", p=P)),
                       (rows[0:88, 1, :], A["ffn_conv_w"][layer, 0:2].rearrange("w (t p) -> (w t) p", p=P)),
                       (rows[0:44, 2, :], A["ffn_conv_w"][layer, 2].rearrange("(t p) -> t p", p=P)),
                       (rows[44:88, 2, :], A["ffn_conv_b"][layer].rearrange("(t p) -> t p", p=P)),
                       (lam_in[:].rearrange("p a b -> p (a b)"), bc(A["da_lambda"][layer].rearrange("a b -> (a b)"), 256)),
                       (da_g[:], bc(A["da_norm_g"][layer], P)),
                       (gla_g[:], bc(A["gla_norm_g"][layer], P)),
                       (f_w1[:], A["hy_w1"][layer]), (f_w2[:], A["hy_w2"][layer]),
                       (f_w3[:].rearrange("p a b -> p (a b)"), A["hy_w3"][layer]),
                       (f_col[:, 0:1], A["hy_b1"][layer].rearrange("(p a) -> p a", a=1)),
                       (f_col[:, 1:2], A["hy_freq1"][layer].rearrange("(p a) -> p a", a=1)),
                       (f_col[:, 2:3], A["hy_b2"][layer].rearrange("(p a) -> p a", a=1)),
                       (f_col[:, 3:4], A["hy_freq2"][layer].rearrange("(p a) -> p a", a=1)),
                       (feat[:], A["feat"]),
                       (decay[:].rearrange("p a b c -> p (a b c)"), A["decay"]))
                pool.memset(w_gate[0:32, :], 0.0).then_inc(sem("gate_zero"), tick("gate_zero", layer))
                pool.wait_ge(sem("gate_zero"), at("gate_zero", layer))
                for d in range(2):
                    dma(w_gate[16 * d:16 * d + 16, 256 * d:256 * d + 256], A["gla_w_gate"][layer, d], "params_in", layer, 100 + d)
                dma(w_gate[32:33, :], A["gla_b_gate"][layer].rearrange("d n -> (d n)").rearrange("(a n) -> a n", a=1),
                    "params_in", layer, "last")

            def modload(layer, part):
                n, w0 = (16, 0) if part == 0 else (32, 2 * D)
                for b in range(2):
                    pool.wait_ge(sem(f"mod_out{b}"), 16 * at(f"mod_out{b}", layer, ADA_GROUPS[part][-2 + b]))
                if (layer, part) != (0, 0):
                    before = (layer, 0) if part else (layer - 1, 1)
                    pool.wait_ge(sem("mod_cols"), at("mod_cols", *before))
                    pool.wait_ge(sem("gate_out"), 16 * at("gate_out", 0)) if layer and not part else None
                for v in range(2):
                    for lo in range(2):
                        dma(mrows[v * n:(v + 1) * n, lo, :],
                            d_mod[layer][2 * lo + v, w0:w0 + n * P].rearrange("(t p) -> t p", p=P), "mod_in", layer, part, v, lo)
                    dma(mrows[v * n:(v + 1) * n, 2, :],
                        A["b_ada"][layer, w0:w0 + n * P].rearrange("(t p) -> t p", p=P), "mod_in", layer, part, v, 2)
            def modcols(layer, part):
                if part:
                    pool.wait_ge(sem("mod_sum"), at("mod_sum", layer, 1))
                    dma(d_gate[layer].rearrange("v (t p) -> (v t) p", p=P), mrows[0:64, 0, :], "gate_out", layer)

            def evac(g):
                layer = g.layer
                if g.kind == "ada":
                    b = g.index % 2
                    pool.wait_ge(sem(f"bank_free{4 + b}"), at(f"bank_full{4 + b}", *g.key))
                    dma(d_mod[layer][:, g.index * COLS:(g.index + 1) * COLS], mod_row[:, b, :], f"mod_out{b}", layer, g.index)
                if g.kind == "gate":
                    for j in range(4):
                        pool.wait_ge(sem(f"bank_free{j}"), at(f"bank_full{j}", *g.key))
                        o = tok0(layer)
                        dma(d_sig[layer][4 * g.index + j, :, o:TOK], sig[:, j % 2, o:TOK], f"sig_out{j % 2}", layer, g.index, j)

            def y_split(layer):
                for j in range(2):
                    pool.wait_ge(sem(f"sig_out{j}"), 16 * at(f"sig_out{j}", layer, 5, 2 + j))
                pool.wait_ge(sem("bank_free6"), at("bank_full6", "y", layer, 1, 3))

            def chunk(g, j):
                if g.kind == "branch" and j == 0:
                    half, br = g.index
                    o = tok0(g.layer)
                    for n in range(4):
                        if (half, br) != (0, 0):
                            before = (half, br - 1) if br else (half - 1, 2)
                            pool.wait_ge(sem(f"bank_free{n}"), at(f"bank_full{n}", "branch", g.layer, before))
                        dma(sig_in[:, n, o:TOK], d_sig[g.layer][8 * br + 4 * half + n, :, o:TOK], f"sig_in{n}", g.layer, g.index)
                if g.kind in ("out", "down") and g.index == 0 and j == 0:
                    residual_loads(g.layer, 0 if g.kind == "out" else 1)

            def residual_loads(layer, which):
                r = R[which]
                if which == 0:
                    pool.wait_ge(sem("bank_full3"), at("bank_full3", "branch", layer, (1, 2)))
                    if layer:
                        pool.wait_ge(sem("x_out"), 16 * at("x_out", layer - 1, 1, 3))
                else:
                    pool.wait_ge(sem("bank_full3"), at("bank_full3", "base", "up end", layer))
                    pool.wait_ge(sem("x_out"), 16 * at("x_out", layer, 0, 3))
                for tt in q_tiles(layer):
                    if layer == 0 and which == 0:
                        src = (A["ctx"] if tt < 2 else A["x"])[0, (tt % 2) * P:(tt % 2 + 1) * P, :]
                    else:
                        src = d_x[2 * layer + which - 1][tt]
                    dma(r["x"][:, tt, :], src, "res_in", layer, which, tt)
                pool.wait_ge(sem("gate_out"), 16 * at("gate_out", layer))
                for v in range(2):
                    dma(r["g"][:, v, :], bc(d_gate[layer][v, 3 * which * D:(3 * which + 1) * D], D), "res_in", layer, which, "g", v)
                g_, b_ = ("ln1_g", "ln1_b") if which == 0 else ("ln2_g", "ln2_b")
                dma(r["ln"][:, 0, :], bc(A[g_][layer], D), "res_in", layer, which, "ln", 0)
                dma(r["ln"][:, 1, :], bc(A[b_][layer], D), "res_in", layer, which, "last")

            def post(layer, which, tt):
                pool.wait_ge(sem("post_x"), at("post_x", layer, which, tt))
                if layer == DEPTH - 1 and which == 1:
                    pool.dma_start(out[0, (tt - 2) * P:(tt - 1) * P, :], x_tok[:, tt, :]).then_inc(sem("stored"), 16)
                else:
                    dma(d_x[2 * layer + which][tt], x_tok[:, tt, :], "x_out", layer, which, tt)

            def end_():
                pool.wait_ge(sem("stored"), 32)

            fns = dict(start=start, params=params, modload=modload, modcols=modcols, evac=evac, y_split=y_split,
                       chunk=chunk, post=post, end=end_)
            for st in steps:
                if st[0] in fns:
                    fns[st[0]](*st[1:])

        @block.tensor
        def _(pe):
            used = [0] * 8
            owed = [True]

            def claim(b):
                if used[b]:
                    pe.wait_ge(sem(f"bank_free{b}"), used[b])
                used[b] += 1

            def full(ins, b, *who):
                ins.then_inc(sem(f"bank_full{b}"), tick(f"bank_full{b}", *who))


            def mm(out_, lhsT, rhs, start=True, stop=True):
                return pe.matmul(out_, lhsT, rhs, start=start, stop=stop, skip_group_check=True)

            def pay(ins):
                if owed[0]:
                    ins.then_inc(sem("chunk_used"), 1)
                    owed[0] = False

            def three(out_, l_hi, l_lo, r_hi, r_lo, first, last):
                pay(mm(out_, l_hi, r_hi, start=first, stop=False))
                mm(out_, l_lo, r_hi, start=False, stop=False)
                return mm(out_, l_hi, r_lo, start=False, stop=last)

            def start():
                pe.wait_ge(sem("c_in"), 32)
                pe.wait_ge(sem("ident_in"), 16)
                claim(4)
                full(pe.transpose(ps[:, 4, 0:16], rows[0:16, 0, :], ident[0:16, 0:16]), 4, "c")

            def params_turn(layer):
                pe.wait_ge(sem("params_in"), 16 * at("params_in", layer, "last"))
                pe.wait_ge(sem("consts_in"), 6 * 16)
                claim(4)
                pe.transpose(ps[:, 4, 0:52], rows[0:52, 0, :], ident[0:52, 0:52])
                pe.transpose(ps[:, 4, 52:140], rows[0:88, 1, :], ident[0:88, 0:88])
                full(pe.transpose(ps[:, 4, 140:228], rows[0:88, 2, :], ident[0:88, 0:88]), 4, "params", layer)

            def ada(layer, part, c0, n_groups):
                if c0 == 0:
                    pe.wait_ge(sem("ada_lo"), 1)
                u = [used[0], used[1]]
                for b in range(2):
                    C.base(f"bank_full{b}", layer, part)
                with pe.Fori(0, n_groups // 2) as i:
                    for b in range(2):
                        pe.wait_ge(sem(f"bank_free{b}"), i + u[b])
                        for j in range(4):
                            c = c0 + 4 * b + j
                            s = c % NBUF
                            pe.wait_ge(sem("lo_ready"), i * 8 + (c + 1))
                            for kk in range(2):
                                k = 2 * j + kk
                                ins = mm(ps[:, b, :], ada_c[:, k, :], w_hi[:, s, kk * 512:kk * 512 + 512], start=k == 0, stop=False)
                                if k == 0:
                                    ins.then_inc(sem("chunk_used"), 1)
                                ins = mm(ps[:, b, :], ada_c[:, k, :], w_lo[:, s, kk * 512:kk * 512 + 512],
                                         start=False, stop=k == KT - 1)
                            if j < 3:
                                ins.then_inc(sem("chunk_used"), 1)
                            else:
                                ins.then_inc(sem(f"bank_full{b}"), 1)
                for b in range(2):
                    used[b] += n_groups // 2
                    C.skip(f"bank_full{b}", n_groups // 2)

            def ada_chunk(g, j, c):
                b, s = g.tiles[0], c % NBUF
                if c == 0:
                    pe.wait_ge(sem("ada_lo"), 1)
                if j == 0:
                    claim(b)
                for k in (2 * j, 2 * j + 1):
                    cs = slice(k % 2 * COLS, k % 2 * COLS + COLS)
                    pay(mm(ps[:, b, :], ada_c[:, k, :], w_hi[:, s, cs], start=k == 0, stop=False))
                    ins = mm(ps[:, b, :], ada_c[:, k, :], w_lo[:, s, cs], start=False, stop=k == KT - 1)
                return ins

            def modcols(layer, part):
                n = 32 if part == 0 else 64
                pe.wait_ge(sem("mod_sum"), at("mod_sum", layer, part))
                claim(4)
                full(pe.transpose(ps[:, 4, 0:n], mrows[0:n, 0, :], ident[0:n, 0:n]), 4, "mod", layer, part)

            def modulate(layer, which, s):
                for t in range(2):
                    pe.wait_ge(sem("ln_x"), at("ln_x", layer, which, 2 * s + t))
                for b in range(4):
                    q = 4 * (1 - s) + b
                    claim(q)
                    for kk in range(2):
                        for t in range(2):
                            k = 2 * b + kk
                            ins = pe.transpose(ps[:, q, kk * 256 + t * P:kk * 256 + t * P + P],
                                               xn[which][:, 2 * s + t, k * P:(k + 1) * P], ident[:])
                    full(ins, q, "mod_x", layer, which, s)

            def chunk(g, j):
                c = g.at[j]
                s = c % NBUF
                layer = g.layer
                pe.wait_ge(sem("lo_ready"), c + 1)
                if g.kind == "a_q":
                    pe.wait_ge(sem("h_ready"), at("h_ready", layer, 0, 1, j))
                if j == 0:
                    if g.kind == "branch" and g.index == (0, 0):
                        pe.wait_ge(sem("ys_ready"), at("ys_ready", layer, 3 * CT - 1))
                    if g.kind == "out" and g.index == 0:
                        pe.wait_ge(sem("merged"), at("merged", layer, 7))
                    if g.kind == "down" and g.index == 0:
                        pe.wait_ge(sem("act_lo"), at("act_lo", "base", "end", layer))
                t0 = tok0(layer)
                if g.kind == "a_k" or g.kind == "a_v" or g.kind == "g_v" or g.kind == "z":
                    t0 = 0
                for n in g.tiles:
                    if g.turn == "A":
                        ins = ada_chunk(g, j, c)
                    elif j == 0:
                        claim(n)
                    if g.turn == "Z":
                        for k in range(KT):
                            ins = three(ps[:, 0, :], w_hi[:, s, k * P:(k + 1) * P], w_lo[:, s, k * P:(k + 1) * P],
                                        h_hi[:, k, :], h_lo[:, k, :], k == 0, k == KT - 1)
                    for kk in range(2 if g.turn not in "AZ" else 0):
                        k = 2 * j + kk
                        first, last = k == 0, k == 2 * g.n - 1
                        if g.turn in "FB":
                            lo_t = 0 if g.kind == "g_qk" and n >= 2 else t0
                            xh, xl = (h_hi, h_lo) if g.turn == "F" else (ys_hi, ys_lo)
                            kx = k if g.turn == "F" else g.index[1] * CT + k
                            cs = slice(kk * 512 + n * P, kk * 512 + n * P + P)
                            ins = three(ps[:, n, lo_t:TOK], w_hi[:, s, cs], w_lo[:, s, cs],
                                        xh[:, kx, lo_t:TOK], xl[:, kx, lo_t:TOK], first, last)
                        else:
                            xh, xl = (act_hi, act_lo) if g.turn == "D" else (h_hi, h_lo)
                            ts_, cs = slice(n * P, n * P + P), slice(kk * 512, kk * 512 + 512)
                            ins = three(ps[:, n, :], xh[:, k, ts_], xl[:, k, ts_], w_hi[:, s, cs], w_lo[:, s, cs], first, last)
                    if j == g.n - 1:
                        full(ins, n, *g.key)
                if j < g.n - 1:
                    ins.then_inc(sem("chunk_used"), 1)
                else:
                    owed[0] = True

            def qk_turn(layer, w):
                for tt in (q_tiles(layer) if w == 0 else range(4)):
                    if tt < 2:
                        pe.wait_ge(sem(f"bank_free{tt}"), at(f"bank_full{tt}", "a_k" if w else "a_q", layer, 0))
                    else:
                        pe.wait_ge(sem("qk_ready"), at("qk_ready", layer, w, tt))
                    b = 4 + tt
                    claim(b)
                    for h in range(HEADS):
                        ins = pe.transpose(ps[:, b, h * P:(h + 1) * P], qk_tok[:, tt, h * P:(h + 1) * P], ident[:])
                    full(ins, b, "qk", layer, w, tt)

            def filter_(layer, i):
                if i == 0:
                    claim(4)
                    full(mm(ps[0:64, 4, 0:256], f_w1[:], feat[:]), 4, "filter", layer, 0)
                if i == 1:
                    pe.wait_ge(sem("f_sin"), at("f_sin", layer, 0))
                    claim(4)
                    full(mm(ps[0:64, 4, 0:256], f_w2[:], f_h[:, 0, :]), 4, "filter", layer, 1)
                if i == 2:
                    pe.wait_ge(sem("f_sin"), at("f_sin", layer, 1))
                    for t in range(2):
                        for d in range(2):
                            claim(4 + 2 * t + d)
                            full(mm(ps[:, 4 + 2 * t + d, :], f_h[:, 1, t * P:(t + 1) * P], f_w3[:, d, :]),
                                 4 + 2 * t + d, "filter", layer, 2)
                if i == 3:
                    pe.wait_ge(sem("f_sd"), at("f_sd", layer, 1))
                    for cs in range(2):
                        for kt in range(2):
                            b = 4 + 2 * cs + kt
                            claim(b)
                            for t in range(2):
                                ins = mm(ps[:, b, :], dft[:, cs, t, kt * P:(kt + 1) * P], f_sd[:, cs, t, :], start=t == 0, stop=t == 1)
                            full(ins, b, "filter", layer, 3)

            def units(layer):
                return [(tt, h) for tt in q_tiles(layer) for h in range(HEADS)]

            def attend(layer, i, n_u):
                us = units(layer)
                if i < n_u:
                    tt, h = us[i]
                    nk = SEQ if tt < 2 else TOK
                    if i == 0:
                        pe.wait_ge(sem("bank_free7"), at("bank_full7", "qk", layer, 1, 3))
                        pe.wait_ge(sem("bank_free3"), at("bank_full3", "a_v", layer, 0))
                    for m in range(2):
                        claim(4 + m)
                        full(mm(ps[:, 4 + m, 0:nk], qT[64 * m:64 * m + 64, h, tt * P:(tt + 1) * P],
                                kT[64 * m:64 * m + 64, h, 0:nk]), 4 + m, "scores", layer, i)
                if 1 <= i <= n_u:
                    tt, h = us[i - 1]
                    nk = SEQ if tt < 2 else TOK
                    pe.wait_ge(sem("diff"), at("diff", layer, i - 1))
                    claim(6)
                    for kb in range(nk // P):
                        ins = pe.transpose(ps[:, 6, kb * P:(kb + 1) * P], probs[:, (i - 1) % 2, 0, kb * P:(kb + 1) * P], ident[:])
                    full(ins, 6, "attT", layer, i - 1)
                if i >= 2:
                    tt, h = us[i - 2]
                    nk = SEQ if tt < 2 else TOK
                    pe.wait_ge(sem("bank_free6"), at("bank_full6", "attT", layer, i - 2))
                    if h == 0:
                        claim(7)
                    for kb in range(nk // P):
                        ins = mm(ps[:, 7, h * P:(h + 1) * P], attT[:, i % 2, kb * P:(kb + 1) * P],
                                 v_tok[:, kb, h * P:(h + 1) * P], start=kb == 0, stop=kb == nk // P - 1)
                    if h == HEADS - 1:
                        full(ins, 7, "o", layer, tt)

            def y_turn(layer, br, tt):
                pe.wait_ge(sem("y_tok"), at("y_tok", layer, br, tt))
                src = y_tok[:] if br == 0 else go[:, tt, :]
                claim(6)
                for c in range(CT):
                    ins = pe.transpose(ps[:, 6, c * P:(c + 1) * P], src[:, c * P:(c + 1) * P], ident[:])
                full(ins, 6, "y", layer, br, tt)

            def hy_turn(layer, s):
                pe.wait_ge(sem("u_ready"), at("u_ready", layer, CT - 1))
                for t in range(2):
                    claim(4 + t)
                    for c in range(CT):
                        o = s * SEQ + t * P
                        ins = pe.transpose(ps[:, 4 + t, c * P:(c + 1) * P], uT[:, c, o:o + P], ident[:])
                    full(ins, 4 + t, "u", layer, s)

            def hy_dft(layer, s):
                for t in range(2):
                    pe.wait_ge(sem(f"bank_free{4 + t}"), at(f"bank_full{4 + t}", "u", layer, s))
                for kt in range(2):
                    for cs in range(2):
                        b = 4 + 2 * kt + cs
                        claim(b)
                        for t in range(2):
                            ins = mm(ps[:, b, :], dft[:, cs, t, kt * P:(kt + 1) * P], u_tok[:, t, :], start=t == 0, stop=t == 1)
                        full(ins, b, "U", layer, s)

            def hy_idft(layer, s):
                pe.wait_ge(sem("spec"), at("spec", layer, s, 1))
                for c in range(CT):
                    b = 4 + c // 2
                    if c % 2 == 0:
                        claim(b)
                    n = 0
                    for kt in range(2):
                        for cs in range(2):
                            ins = mm(ps[:, b, (c % 2) * 256:(c % 2) * 256 + 256], spec[:, cs, kt, c * P:(c + 1) * P],
                                     idft[:, cs, kt, :], start=n == 0, stop=n == 3)
                            n += 1
                    if c % 2:
                        full(ins, b, "conv", layer, s)

            def gla_gate(layer, tt):
                if tt == 0:
                    pe.wait_ge(sem("bank_free0"), at("bank_full0", "z", layer, 0))
                    pe.wait_ge(sem("z_one"), at("z_one", layer))
                    pe.wait_ge(sem("bank_free3"), at("bank_full3", "g_qk", layer, 0))
                claim(4)
                full(mm(ps[:, 4, :], zT[0:33, tt * P:(tt + 1) * P], w_gate[0:33, :]), 4, "logit", layer, tt)
                claim(5)
                for p_ in range(2):
                    ins = pe.transpose(ps[:, 5, p_ * P:(p_ + 1) * P], gqk[:, 2 + p_, tt * P:(tt + 1) * P], ident[:])
                full(ins, 5, "ktok", layer, tt)

            def gla_sum(layer, tt):
                pe.wait_ge(sem("bank_free4"), at("bank_full4", "logit", layer, tt))
                for d in range(2):
                    claim(6 + d)
                    for p_ in range(2):
                        ins = mm(ps[:, 6 + d, p_ * 256:p_ * 256 + 256], la[:, (2 * d + p_) * P:(2 * d + p_ + 1) * P], cums[:, d, :])
                    full(ins, 6 + d, "b", layer, tt)
                claim(4)
                for d in range(2):
                    ins = mm(ps[:, 4, d * 256:d * 256 + 256], tail[:, d, :], la[:, d * 256:d * 256 + 256])
                full(ins, 4, "tail", layer, tt)

            def gla_att(layer, tt):
                pe.wait_ge(sem("qke"), at("qke", layer, tt))
                for r in range(2):
                    claim(6 + r)
                    rs = slice(64 * r, 64 * r + 64)
                    for n in range(4):
                        ins = mm(ps[:, 6 + r, n * P:(n + 1) * P], ke[rs, n, :], qe[rs, n, :])
                    full(ins, 6 + r, "att", layer, tt)

            def gla_state(layer, tt):
                pe.wait_ge(sem("ku"), at("ku", layer, tt))
                if tt == 0:
                    pe.wait_ge(sem("bank_free3"), at("bank_full3", "g_v", layer, 0))
                for j in range(2):
                    claim(4 + j)
                    r = slice(64 * j, 64 * j + 64)
                    for d in range(2):
                        for h in range(HEADS):
                            o, p_ = (h % 2) * 64, h // 2
                            ins = mm(ps[o:o + 64, 4 + j, (2 * d + p_) * P:(2 * d + p_ + 1) * P], ku[r, d, h * 64:h * 64 + 64],
                                     gv[r, tt, h * P:(h + 1) * P])
                    full(ins, 4 + j, "u_state", layer, tt)
                if tt in q_tiles(layer):
                    pe.wait_ge(sem("bank_free7"), at("bank_full7", "att", layer, tt))
                    claim(6)
                    for h in range(HEADS):
                        for d in range(2):
                            ins = mm(ps[:, 6, h * P:(h + 1) * P], att[:, h % 2, 2 * d + h // 2, :], gv[:, tt, h * P:(h + 1) * P],
                                     start=d == 0, stop=d == 1)
                    full(ins, 6, "intra", layer, tt)

            def gla_out(layer, tt):
                if tt == q_tiles(layer)[0]:
                    pe.wait_ge(sem("scanned"), at("scanned", layer))
                for r in range(2):
                    claim(4 + r)
                    rs = slice(64 * r, 64 * r + 64)
                    for j in range(2):
                        c = 2 * tt + j
                        ns = [c, (3 - c) if c < 4 else (11 - c)]
                        ds_ = [d for d in range(2) if ns[d] > 0]
                        for p_ in range(2):
                            for d in ds_:
                                ins = mm(ps[64 * j:64 * j + 64, 4 + r, p_ * P:(p_ + 1) * P],
                                         gqk[rs, 2 * d + p_, tt * P + 64 * j:tt * P + 64 * j + 64], states[rs, d, ns[d] - 1, p_, :],
                                         start=d == ds_[0], stop=d == ds_[-1])
                    full(ins, 4 + r, "inter", layer, tt)

            def up(layer, c0):
                u = list(used)
                t0 = tok0(layer)
                for b in range(8):
                    C.base(f"bank_full{b}", "up", layer)

                def up_group(i, h):
                    for j in range(4):
                        c = c0 + 4 * h + j
                        s = c % NBUF
                        pe.wait_ge(sem("lo_ready"), i * 8 + (c + 1))
                        pe.wait_ge(sem("h_ready"), at("h_ready", layer, 1, 1, j))
                        for n in range(4):
                            b = 4 * h + n
                            if j == 0:
                                pe.wait_ge(sem(f"bank_free{b}"), i + u[b])
                            for kk in range(2):
                                k = 2 * j + kk
                                cs = slice(kk * 512 + n * P, kk * 512 + n * P + P)
                                ins = three(ps[:, b, t0:TOK], w_hi[:, s, cs], w_lo[:, s, cs],
                                            h_hi[:, k, t0:TOK], h_lo[:, k, t0:TOK], k == 0, k == KT - 1)
                            if j == 3:
                                ins.then_inc(sem(f"bank_full{b}"), 1)
                        if j < 3:
                            ins.then_inc(sem("chunk_used"), 1)
                        else:
                            owed[0] = True

                with pe.Fori(0, UP_GROUPS // 2) as i:
                    for h in range(2):
                        up_group(i, h)
                up_group(UP_GROUPS // 2, 0)
                for b in range(8):
                    n = UP_GROUPS // 2 + (1 if b < 4 else 0)
                    used[b] += n
                    C.skip(f"bank_full{b}", n)
                C.base("bank_full3", "up end", layer)

            fns = dict(start=start, params_turn=params_turn, modcols=modcols, modulate=modulate, chunk=chunk,
                       qk_turn=qk_turn, filter=filter_, attend=attend, y_turn=y_turn, hy_turn=hy_turn, hy_dft=hy_dft,
                       hy_idft=hy_idft, gla_gate=gla_gate, gla_sum=gla_sum, gla_att=gla_att, gla_state=gla_state,
                       gla_out=gla_out, up=up)
            for st in steps:
                if st[0] in fns:
                    fns[st[0]](*st[1:])

        @block.scalar
        def _(act):
            cursor = [0]

            def split(c):
                s = c % NBUF
                act.wait_ge(sem(f"landed{s}"), 32 * (c // NBUF + 1))
                if c >= NBUF:
                    act.wait_ge(sem("chunk_used"), c - NBUF + 2)
                act.activation(w_hi[:, s, :], stage[:, s, :], ACT.Copy).then_inc(sem("hi_ready"), 1)

            def split_to(c):
                while cursor[0] < min(c, n_chunks):
                    split(cursor[0])
                    cursor[0] += 1

            def bank(b, *who):
                act.wait_ge(sem(f"bank_full{b}"), at(f"bank_full{b}", *who))

            def do(ins, stage_, *who):
                ins.then_inc(sem(stage_), tick(stage_, *who))

            def free(ins, b):
                ins.then_inc(sem(f"bank_free{b}"), 1)

            def freed(b, *who):
                act.wait_ge(sem(f"bank_free{b}"), at(f"bank_full{b}", *who))

            def start():
                for tt in range(4):
                    src = (A["ctx"] if tt < 2 else A["x"])[0, (tt % 2) * P:(tt % 2 + 1) * P, :]
                    act.dma_start(x_tok[:, tt, :], src).then_inc(sem("x_in"), 16)
                bank(4, "c")
                free(act.activation(c_act[:], ps[:, 4, 0:16], ACT.Silu), 4)
                freed(4, "c")
                act.wait_ge(sem("ada_zero"), 1)
                act.activation(ada_c[:, :, 0:2].rearrange("p k v -> p v k"),
                               c_act[:].rearrange("p (v k) -> p v k", v=2), ACT.Copy).then_inc(sem("ada_hi"), 1)
                split_to(AHEAD)

            def params_turn(layer):
                bank(4, "params", layer)
                act.activation(pcol[:], ps[:, 4, 0:228], ACT.Copy).then_inc(sem("bank_free4"), 1)
                act.wait_ge(sem("lam_dot"), at("lam_dot", layer))
                do(act.activation(lam[:, 2:4], lam[:, 0:2], ACT.Exp), "lam_exp", layer)



            def modcols(layer, part):
                n = 32 if part == 0 else 64
                bank(4, "mod", layer, part)
                dst = (mod_a if part == 0 else mod_b)[:].rearrange("p v w k -> p (v w k)")
                free(act.activation(dst, ps[:, 4, 0:n], ACT.Copy), 4)

            def moments(layer, which, tt):
                act.wait_ge(sem("ln_var"), at("ln_var", layer, which, tt))
                do(act.activation(moms[:, 4 + tt, 3:4], moms[:, 4 + tt, 2:3], ACT.Sqrt), "ln_std", layer, which, tt)

            def normal(layer, which, tt):
                act.wait_ge(sem("ln_scale"), at("ln_scale", layer, which, tt))
                do(act.activation(xn[which][:, tt, :], x_tok[:, tt, :], ACT.Identity, bias=moms[:, 4 + tt, 4:5],
                                  scale=moms[:, 4 + tt, 2:3]), "ln_x", layer, which, tt)

            def modulate(layer, which, s):
                v = 1 - s
                act.wait_ge(sem("mod_cols"), at("mod_cols", layer, which))
                for b in range(4):
                    q = 4 * (1 - s) + b
                    bank(q, "mod_x", layer, which, s)
                    if b >= 2:
                        act.wait_ge(sem("h_ready"), at("h_ready", layer, which, s, b - 2))
                    elif (layer, which, s) != (0, 0, 0):
                        prev = (layer, which, 0) if s == 1 and (which, layer) != (1, DEPTH - 1) else \
                            (layer, 0, 1) if which else (layer - 1, 1, 1)
                        act.wait_ge(sem("h_ready"), at("h_ready", *prev, 3))
                    for kk in range(2):
                        k = 2 * b + kk
                        sc = mod_a[:, v, 1, k:k + 1] if which == 0 else mod_b[:, v, 2, k:k + 1]
                        sh = mod_a[:, v, 0, k:k + 1] if which == 0 else mod_b[:, v, 1, k:k + 1]
                        ins = act.activation(xm[:, k % 4, :], ps[:, q, kk * 256:kk * 256 + 256], ACT.Identity, bias=sh, scale=sc)
                    free(ins, q)

            def chunk(g, j):
                split_to(g.at[j] + 1 + AHEAD)

            def evac(g):
                layer, kind = g.layer, g.kind
                t0 = tok0(layer)
                if kind == "ada":
                    b, i = g.index % 2, g.index
                    if (layer, i) == (0, ADA_GROUPS[1][0]):
                        freed(7, "U", layer, 1)
                    if (layer, i) == (1, 0):
                        act.wait_ge(sem("act_lo"), at("act_lo", "base", "end", 0))
                    if (layer, i) > (0, 1):
                        before = (layer, i - 2) if i >= 2 else (layer - 1, i + 10)
                        act.wait_ge(sem(f"mod_out{b}"), 16 * at(f"mod_out{b}", *before))
                    bank(4 + b, *g.key)
                    free(act.activation(mod_row[:, b, :], ps[0:4, 4 + b, :], ACT.Copy), 4 + b)
                if kind in ("out", "down") and g.index == 1:
                    which = 0 if kind == "out" else 1
                    for tt in g.tiles:
                        act.wait_ge(sem("post_var"), at("post_var", layer, which, tt))
                        do(act.activation(moms[:, tt, 3:4], moms[:, tt, 2:3], ACT.Sqrt), "post_std", layer, which, tt)
                if kind in ("a_q", "a_k"):
                    w = 0 if kind == "a_q" else 1
                    for tt in g.tiles:
                        if tt < 2:
                            if w == 1:
                                if layer < DEPTH - 1:
                                    act.wait_ge(sem(f"bank_full{4 + tt}"), at(f"bank_full{4 + tt}", "qk", layer, 0, tt))
                            bank(tt, *g.key)
                            free(act.activation(qk_tok[:, tt, :], ps[:, tt, :], ACT.Copy), tt)
                if kind == "a_v":
                    for tt in g.tiles:
                        bank(tt, *g.key)
                        free(act.activation(v_tok[:, tt, :], ps[:, tt, :], ACT.Copy), tt)
                if kind == "hy":
                    part = g.index
                    if part == 0:
                        freed(7, "filter", layer, 3)
                    for n in range(4):
                        t = 4 * part + n
                        bank(n, *g.key)
                        if part == 2 and n >= 2:
                            act.wait_ge(sem("u_ready"), at("u_ready", layer, n - 2))
                        dst = (x0T, uT, vvT)[part][:, n % 2 if part == 2 else n, t0:TOK]
                        do(act.activation(dst, ps[:, n, t0:TOK], ACT.Identity, bias=pcol[:, 36 + t:37 + t],
                                          scale=pcol[:, 12 + t:13 + t]), "conv_mid", layer, part, n)
                if kind == "g_v":
                    for tt in g.tiles:
                        bank(tt, *g.key)
                        free(act.activation(gv[:, tt, :], ps[:, tt, :], ACT.Copy), tt)
                if kind == "g_qk":
                    act.wait_ge(sem("bank_full6"), at("bank_full6", "y", layer, 0, 3))
                    for n in range(4):
                        bank(n, *g.key)
                        lo_t = 0 if n >= 2 else t0
                        free(act.activation(gqk[:, n, lo_t:TOK], ps[:, n, lo_t:TOK], ACT.Copy, scale=0.125 if n < 2 else 1.0), n)
                if kind == "z":
                    bank(0, *g.key)
                    free(act.activation(zT[0:32, :], ps[0:32, 0, :], ACT.Copy), 0)
                if kind == "gate":
                    for j in range(4):
                        bank(j, *g.key)
                        if (g.index, j) >= (0, 2):
                            n = 4 * g.index + j - 2
                            act.wait_ge(sem(f"sig_out{j % 2}"), 16 * at(f"sig_out{j % 2}", layer, n // 4, n % 4))
                        free(act.activation(sig[:, j % 2, t0:TOK], ps[:, j, t0:TOK], ACT.Sigmoid), j)
                if kind == "g_r":
                    for n, tt in enumerate(g.tiles):
                        bank(tt, *g.key)
                        if n >= 2:
                            act.wait_ge(sem("y_tok"), at("y_tok", layer, 1, tt - 2))
                        free(act.activation(rg[:, tt % 2, :], ps[:, tt, :], ACT.Silu), tt)
                if kind == "branch":
                    half, br = g.index
                    if br == 2:
                        for n in range(4):
                            act.wait_ge(sem("gated"), at("gated", layer, g.index, n))
                            do(act.activation(h_hi[:, 4 * half + n, t0:TOK], acc[:, n, t0:TOK], ACT.Copy), "merged_hi", layer, 4 * half + n)

            def qk_turn(layer, w):
                for tt in (q_tiles(layer) if w == 0 else range(4)):
                    b = 4 + tt
                    bank(b, "qk", layer, w, tt)
                    dst = (qT if w == 0 else kT)[:, :, tt * P:(tt + 1) * P]
                    if layer:
                            act.wait_ge(sem("x_out"), 16 * at("x_out", layer - 1, 1, 3))
                    free(act.activation(dst, ps[:, b, :].rearrange("p (h t) -> p h t", h=HEADS), ACT.Copy), b)

            def filter_(layer, i):
                if i < 2:
                    act.wait_ge(sem("f_arg"), at("f_arg", layer, i))
                    do(act.activation(f_h[:, i, :], f_arg[:, 0, :], ACT.Sin), "f_sin", layer, i)
                if i == 3:
                    for b in range(2):
                        act.wait_ge(sem(f"mod_out{b}"), 16 * at(f"mod_out{b}", layer, ADA_GROUPS[1 if layer else 0][-2 + b]))
                    for cs in range(2):
                        for kt in range(2):
                            b = 4 + 2 * cs + kt
                            bank(b, "filter", layer, 3)
                            free(act.activation(filt[:, cs, kt, :], ps[:, b, :], ACT.Copy), b)

            def attend(layer, i, n_u):
                us = [(tt, h) for tt in q_tiles(layer) for h in range(HEADS)]
                if i < n_u:
                    nk = SEQ if us[i][0] < 2 else TOK
                    act.wait_ge(sem("neg_max"), at("neg_max", layer, i))
                    for m in range(2):
                        free(act.activation(probs[:, i % 2, m, 0:nk], ps[:, 4 + m, 0:nk], ACT.Exp, bias=soft[:, i % 2, 2 + m:3 + m],
                                            scale=0.125, accum_out=soft[:, i % 2, 4 + m:5 + m]), 4 + m)
                if 1 <= i <= n_u:
                    nk = SEQ if us[i - 1][0] < 2 else TOK
                    bank(6, "attT", layer, i - 1)
                    free(act.activation(attT[:, (i - 1) % 2, 0:nk], ps[:, 6, 0:nk], ACT.Copy), 6)

            def head_norm(layer, tt):
                bank(7, "o", layer, tt)
                do(act.activation(o_sq[:], ps[:, 7, :], ACT.Square), "o_sq", layer, tt)
                act.wait_ge(sem("hn_var"), at("hn_var", layer, 0, tt))
                do(act.activation(hn[:, 1, :], hn[:, 0, :], ACT.Sqrt), "hn_std", layer, 0, tt)

            def y_turn(layer, br, tt):
                bank(6, "y", layer, br, tt)
                free(act.activation(y[:, br, :, tt * P:(tt + 1) * P], ps[:, 6, :].rearrange("p (c t) -> p c t", c=CT), ACT.Copy), 6)

            def hy_turn(layer, s):
                for t in range(2):
                    bank(4 + t, "u", layer, s)
                    free(act.activation(u_tok[:, t, :], ps[:, 4 + t, :], ACT.Copy), 4 + t)

            def gla_gate(layer, tt):
                if tt == 0:
                    act.wait_ge(sem("y_hyena"), at("y_hyena", layer, 1, CT - 1))
                else:
                    freed(4, "logit", layer, tt - 1)
                bank(4, "logit", layer, tt)
                do(act.activation(lg[:], ps[:, 4, :], ACT.Abs), "lg_abs", layer, tt)
                act.wait_ge(sem("lg_abs"), at("lg_abs", layer, tt))
                do(act.activation(lg[:], lg[:], ACT.Exp, scale=-1.0), "lg_exp", layer, tt)
                act.wait_ge(sem("lg_exp"), at("lg_exp", layer, tt))
                do(act.activation(lg[:], lg[:], ACT.Ln, bias=1.0), "lg", layer, tt)
                bank(5, "ktok", layer, tt)
                if tt > 0:
                    act.wait_ge(sem("ku"), at("ku", layer, tt - 1))
                free(act.activation(ktok[:], ps[:, 5, 0:256], ACT.Copy), 5)

            def gla_sum(layer, tt):
                for d in range(2):
                    bank(6 + d, "b", layer, tt)
                src = ps[:, 6:8, :].rearrange("p d (a b t) -> p (d a) b t", a=2, b=2)
                if tt > 0:
                    act.wait_ge(sem("ku"), at("ku", layer, tt - 1))
                    act.wait_ge(sem("dec"), at("dec", layer, tt - 1, 1))
                    if tt - 1 in q_tiles(layer):
                        act.wait_ge(sem("qke"), at("qke", layer, tt - 1))
                ins = act.activation(eb[:, 0, :, :], src[:, :, 0, :], ACT.Exp)
                if tt in q_tiles(layer):
                    act.activation(eb[:, 1, :, :], src[:, :, 1, :], ACT.Exp)
                    ins = act.activation(eb[:, 2, :, :], src[:, :, 1, :], ACT.Exp, scale=-1.0)
                free(ins, 6)
                bank(4, "tail", layer, tt)
                for d, b in ((0, 7), (1, 4)):
                    free(act.activation(etail[:, d, :], ps[:, 4, d * 256:d * 256 + 256], ACT.Exp), b)

            def gla_state(layer, tt):
                for j in range(2):
                    bank(4 + j, "u_state", layer, tt)
                    slots = [((2 * tt + j) if d == 0 else (3 if tt < 2 else 11) - 2 * tt - j, d) for d in range(2)]
                    for n, d in [x for x in slots if x[0] < 7]:
                        ins = act.activation(states[:, d, n, :, :].rearrange("p a v -> p (a v)"),
                                             ps[:, 4 + j, 256 * d:256 * d + 256], ACT.Copy)
                    free(ins, 4 + j)
                if tt in q_tiles(layer):
                    bank(6, "intra", layer, tt)
                    free(act.activation(go[:, tt, :], ps[:, 6, :], ACT.Copy), 6)

            def gla_out(layer, tt):
                freed(5, "inter", layer, tt)
                do(act.activation(g_sq[:], go[:, tt, :], ACT.Square), "g_sq", layer, tt)
                act.wait_ge(sem("hn_var"), at("hn_var", layer, 1, tt))
                do(act.activation(hn[:, 1, :], hn[:, 0, :], ACT.Sqrt), "hn_std", layer, 1, tt)

            def y_split(layer):
                t0 = tok0(layer)
                freed(6, "y", layer, 1, 3)
                act.wait_ge(sem("y_hyena"), at("y_hyena", layer, 1, CT - 1))
                for j in range(2):
                    act.wait_ge(sem(f"sig_out{j}"), 16 * at(f"sig_out{j}", layer, 5, 2 + j))
                for n in range(3 * CT):
                    do(act.activation(ys_hi[:, n, t0:TOK], y[:, n // CT, n % CT, t0:TOK], ACT.Copy), "ys_hi", layer, n)

            def up(layer, c0):
                split_to(c0 + AHEAD)
                t0 = tok0(layer)
                W0, W1, W2, B = 52, 52 + 44, 140, 184
                e0 = C.base("up_mid", layer)
                b0 = [at(f"bank_full{b}", "base", "up", layer) for b in range(8)]
                l0 = at("act_lo", "base", layer)
                p0 = at("up_prod", "base", layer)
                n_groups = UP_GROUPS
                C.base("up_gelu", layer)
                C.base("act_hi", layer)
                act.wait_ge(sem("x_out"), 16 * at("x_out", layer, 0, 3))
                def up_group(i, h):
                    for j in range(4):
                        c = c0 + AHEAD + 4 * h + j
                        s = c % NBUF
                        act.wait_ge(sem(f"landed{s}"), i * 64 + 32 * (c // NBUF + 1))
                        act.wait_ge(sem("chunk_used"), i * 8 + (c - NBUF + 2))
                        act.activation(w_hi[:, s, :], stage[:, s, :], ACT.Copy).then_inc(sem("hi_ready"), 1)
                    for p_ in range(2):
                        act.wait_ge(sem("act_lo"), i * 4 + (l0 + 2 * h + p_ - 1))
                        for a in range(2):
                            b = 4 * h + 2 * a + p_
                            act.wait_ge(sem(f"bank_full{b}"), i + (b0[b] + 1))
                            act.activation(ffn_t[:, p_, a, t0:TOK], ps[:, b, t0:TOK], ACT.Identity,
                                           bias=pcol[:, bass.ds(i * 4 + (B + 22 * a + 2 * h + p_), 1)],
                                           scale=pcol[:, bass.ds(i * 4 + (W1 + 22 * a + 2 * h + p_), 1)]).then_inc(sem("up_mid"), 1)
                    for p_ in range(2):
                        b = 4 * h + 2 + p_
                        act.wait_ge(sem(f"bank_free{b}"), i + (b0[b] + 1))
                        act.activation(ffn_t[:, p_, 1, t0:TOK], ffn_t[:, p_, 1, t0:TOK], ACT.Gelu_apprx_tanh).then_inc(sem("up_gelu"), 1)
                    for p_ in range(2):
                        act.wait_ge(sem("up_prod"), i * 4 + (p0 + 2 * h + p_ + 1))
                        act.activation(act_hi[:, bass.ds(i * 4 + (2 * h + p_), 1), t0:TOK].rearrange("p a t -> p (a t)"),
                                       ffn_t[:, p_, 0, t0:TOK], ACT.Copy).then_inc(sem("act_hi"), 1)

                with act.Fori(0, UP_GROUPS // 2) as i:
                    for h in range(2):
                        up_group(i, h)
                up_group(UP_GROUPS // 2, 0)
                C.skip("up_mid", 4 * n_groups)
                C.skip("up_gelu", 2 * n_groups)
                C.skip("act_hi", 2 * n_groups)
                C.place[("act_hi", "end", layer)] = C.seen["act_hi"]
                cursor[0] += 4 * n_groups

            fns = dict(start=start, params_turn=params_turn, modcols=modcols, moments=moments, normal=normal,
                       modulate=modulate, chunk=chunk, evac=evac, qk_turn=qk_turn, filter=filter_, attend=attend, head_norm=head_norm, y_turn=y_turn,
                       hy_turn=hy_turn, gla_gate=gla_gate, gla_sum=gla_sum, gla_state=gla_state, gla_out=gla_out, y_split=y_split,
                       up=up)
            for st in steps:
                if st[0] in fns:
                    fns[st[0]](*st[1:])

        @block.vector
        def _(dve):
            cursor, chain = [0], [0]

            def link(ins):
                chain[0] += 1
                ins.then_inc(sem("dve_chain"), 1)
                dve.wait_ge(sem("dve_chain"), chain[0])

            def split(c):
                s = c % NBUF
                dve.wait_ge(sem("hi_ready"), c + 1)
                dve.tensor_tensor(w_lo[:, s, :], stage[:, s, :], w_hi[:, s, :].bitcast(F32), ALU.subtract)\
                   .then_inc(sem("lo_ready"), 1)

            def split_to(c):
                while cursor[0] < min(c, n_chunks):
                    split(cursor[0])
                    cursor[0] += 1

            def bank(b, *who):
                dve.wait_ge(sem(f"bank_full{b}"), at(f"bank_full{b}", *who))

            def freed(b, *who):
                dve.wait_ge(sem(f"bank_free{b}"), at(f"bank_full{b}", *who))

            def do(ins, stage_, *who):
                ins.then_inc(sem(stage_), tick(stage_, *who))

            def done(stage_, *who):
                dve.wait_ge(sem(stage_), at(stage_, *who))

            def free(ins, b):
                ins.then_inc(sem(f"bank_free{b}"), 1)

            def wide(ap, n, axis=1):
                a = ap.unsqueeze(axis)
                shape = list(a.shape)
                shape[axis] = n
                return a.broadcast_to(shape)

            def start():

                dve.memset(ada_c[:].bitcast(F32), 0.0).then_inc(sem("ada_zero"), 1)
                dve.wait_ge(sem("ada_hi"), 1)
                dve.tensor_tensor(ada_c[:, :, 2:4].rearrange("p k v -> p v k"), c_act[:].rearrange("p (v k) -> p v k", v=2),
                                  ada_c[:, :, 0:2].rearrange("p k v -> p v k").bitcast(F32), ALU.subtract).then_inc(sem("ada_lo"), 1)
                split_to(AHEAD)

            def params_turn(layer):
                lam_init = 0.8 - 0.6 * math.exp(-0.3 * layer)
                dve.wait_ge(sem("params_in"), 16 * at("params_in", layer, "last"))
                dve.wait_ge(sem("consts_in"), 6 * 16)
                lv = lam_in[:].rearrange("p (a b) n -> p a b n", b=2)
                link(dve.tensor_tensor(lam_prod[:], lv[:, :, 0, :], lv[:, :, 1, :], ALU.mult))
                do(dve.tensor_reduce(lam[:, 0:2], lam_prod[:], AX_X, ALU.add), "lam_dot", layer)
                done("lam_exp", layer)
                link(dve.tensor_tensor(lam[:, 4:5], lam[:, 3:4], lam[:, 2:3], ALU.subtract))
                link(dve.tensor_scalar(lam[:, 5:6], lam[:, 4:5], -lam_init, None, ALU.add))
                link(dve.tensor_scalar(da_g[:], da_g[:], 1.0 - lam_init, None, ALU.mult))



            def modcols(layer, part):
                n = 32 if part == 0 else 64
                dve.wait_ge(sem("mod_in"), 16 * at("mod_in", layer, part, 1, 2))
                link(dve.tensor_tensor(mrows[0:n, 0, :], mrows[0:n, 0, :], mrows[0:n, 1, :], ALU.add))
                do(dve.tensor_tensor(mrows[0:n, 0, :], mrows[0:n, 0, :], mrows[0:n, 2, :], ALU.add), "mod_sum", layer, part)
                freed(4, "mod", layer, part)
                col = mod_a[:, :, 1, :] if part == 0 else mod_b[:, :, 2, :]
                do(dve.tensor_scalar(col, col, 1.0, None, ALU.add), "mod_cols", layer, part)

            def half_moments(src, m, half):
                return dve.bn_stats(stat[:, m, 6 * half:6 * half + 6], src[:, half * 512:half * 512 + 512])

            def whole_moments(m):
                link(dve.bn_aggr(moms[:, m, 0:2], stat[:, m, :]))
                return dve.tensor_scalar(moms[:, m, 2:3], moms[:, m, 1:2], EPS, None, ALU.add)

            def moments(layer, which, tt):
                if (layer, which, tt) == (0, 0, 0):
                    dve.wait_ge(sem("x_in"), 64)
                half_moments(x_tok[:, tt, :], 4 + tt, 0)
                link(half_moments(x_tok[:, tt, :], 4 + tt, 1))
                do(whole_moments(4 + tt), "ln_var", layer, which, tt)

            def normal(layer, which, tt):
                done("ln_std", layer, which, tt)
                m = moms[:, 4 + tt, :]
                link(dve.reciprocal(m[:, 2:3], m[:, 3:4]))
                do(dve.scalar_tensor_tensor(out=m[:, 4:5], in0=m[:, 0:1], scalar=-1.0, in1=m[:, 2:3], op0=ALU.mult, op1=ALU.mult),
                   "ln_scale", layer, which, tt)

            def modulate(layer, which, s):
                cols = slice(s * SEQ, (s + 1) * SEQ)
                for b in range(4):
                    freed(4 * (1 - s) + b, "mod_x", layer, which, s)
                    src = xm[:, (2 * b) % 4:(2 * b) % 4 + 2, :]
                    link(dve.tensor_copy(h_hi[:, 2 * b:2 * b + 2, cols], src))
                    do(dve.tensor_tensor(h_lo[:, 2 * b:2 * b + 2, cols], src, h_hi[:, 2 * b:2 * b + 2, cols].bitcast(F32), ALU.subtract),
                       "h_ready", layer, which, s, b)

            def chunk(g, j):
                split_to(g.at[j] + 1 + AHEAD)

            def seqs(ap, layer):
                t0 = tok0(layer)
                return ap[:, t0:TOK].rearrange("p (s t) -> p s t", t=SEQ)

            def taps(dst, src, w0, w2):
                first = dve.scalar_tensor_tensor(out=dst[:, :, 1:SEQ], in0=src[:, :, 0:SEQ - 1], scalar=w0, in1=dst[:, :, 1:SEQ],
                                                 op0=ALU.mult, op1=ALU.add)
                link(first)
                return dve.scalar_tensor_tensor(out=dst[:, :, 0:SEQ - 1], in0=src[:, :, 1:SEQ], scalar=w2, in1=dst[:, :, 0:SEQ - 1],
                                                op0=ALU.mult, op1=ALU.add)

            def evac(g):
                layer, kind = g.layer, g.kind
                t0 = tok0(layer)
                if kind in ("a_q", "a_k"):
                    w = 0 if kind == "a_q" else 1
                    for tt in (2, 3):
                        bank(tt, *g.key)
                        if w == 1:
                            bank(4 + tt, "qk", layer, 0, tt)
                            done("qk_ready", layer, 0, tt)
                        src = ps[:, tt, :].rearrange("p (h n) -> p h n", n=64)
                        cos, sin = rope[:, tt - 2, 0, :], rope[:, tt - 2, 1, :]
                        ta, tb = rope_t[:, tt - 2, 0, :], rope_t[:, tt - 2, 1, :]
                        dve.tensor_tensor(ta.rearrange("p (h n) -> p h n", n=64), src, wide(cos, 8), ALU.mult)
                        halves = ps[:, tt, :].rearrange("p (h a n) -> p h a n", a=2, n=16)
                        tv = tb.rearrange("p (h a n) -> p h a n", a=2, n=16)
                        sv = sin.rearrange("p (f a n) -> p f a n", a=2, n=16)
                        for a in range(2):
                            for f in range(2):
                                ins = dve.tensor_tensor(tv.rearrange("p (h f) a n -> p h f a n", f=2)[:, :, f, a, :],
                                                        halves.rearrange("p (h f) a n -> p h f a n", f=2)[:, :, f, 1 - a, :],
                                                        wide(sv[:, f, a, :], 8), ALU.mult)
                        free(ins, tt)
                        freed(tt, *g.key)
                        do(dve.tensor_tensor(qk_tok[:, tt, :], ta, tb, ALU.add), "qk_ready", layer, w, tt)
                if kind == "hy":
                    part = g.index
                    for n in range(4):
                        t = 4 * part + n
                        tile_ = (x0T, uT, vvT)[part][:, n % 2 if part == 2 else n, :]
                        done("conv_mid", layer, part, n)
                        bank(n, *g.key)
                        free(taps(seqs(tile_, layer), seqs(ps[:, n, :], layer), pcol[:, t:t + 1], pcol[:, 24 + t:25 + t]), n)
                        if part == 2:
                            freed(n, *g.key)
                            do(dve.tensor_tensor(uT[:, n, t0:TOK], uT[:, n, t0:TOK], vvT[:, n % 2, t0:TOK], ALU.mult),
                               "u_ready", layer, n)
                if kind == "z":
                    bank(0, *g.key)
                    do(dve.memset(zT[32:33, :], 1.0), "z_one", layer)
                if kind == "g_r":
                    for tt in g.tiles:
                        freed(tt, *g.key)
                        r4 = rg[:, tt % 2, :].rearrange("p (h n) -> p h n", h=HEADS)
                        link(dve.tensor_tensor(r4, r4, wide(gla_g[:], HEADS), ALU.mult))
                        do(dve.tensor_tensor(go[:, tt, :], go[:, tt, :], rg[:, tt % 2, :], ALU.mult), "y_tok", layer, 1, tt)
                if kind == "branch":
                    half, br = g.index
                    for n in range(4):
                        dve.wait_ge(sem(f"sig_in{n}"), 16 * at(f"sig_in{n}", layer, g.index))
                        bank(n, *g.key)
                        if half and br == 0:
                            done("merged", layer, n)
                        if br and (br, n) != (1, 0):
                            prev = ((half, br), n - 2) if n >= 2 else ((half, br - 1), n + 2)
                            if prev[0][1]:
                                done("gated", layer, *prev)
                        dst = acc[:, n, t0:TOK] if br == 0 else prod[:, n % 2, t0:TOK]
                        free(dve.tensor_tensor(dst, ps[:, n, t0:TOK], sig_in[:, n, t0:TOK], ALU.mult), n)
                        if br:
                            freed(n, *g.key)
                            do(dve.tensor_tensor(acc[:, n, t0:TOK], acc[:, n, t0:TOK], dst, ALU.add), "gated", layer, g.index, n)
                    if br == 2:
                        for n in range(4):
                            k = 4 * half + n
                            done("merged_hi", layer, k)
                            do(dve.tensor_tensor(h_lo[:, k, t0:TOK], acc[:, n, t0:TOK], h_hi[:, k, t0:TOK].bitcast(F32), ALU.subtract),
                               "merged", layer, k)
                if kind in ("out", "down"):
                    which = 0 if kind == "out" else 1
                    r, half = R[which], g.index
                    if half == 0:
                        dve.wait_ge(sem("res_in"), 16 * at("res_in", layer, which, "last"))
                    cols = slice(half * COLS, half * COLS + COLS)
                    for tt in g.tiles:
                        bank(tt, *g.key)
                        t = r["t"][:, tt % 2, :]
                        free(dve.tensor_tensor(t, ps[:, tt, :], r["g"][:, 1 if tt < 2 else 0, cols], ALU.mult), tt)
                        freed(tt, *g.key)
                        link(dve.scalar_tensor_tensor(out=r["x"][:, tt, cols], in0=r["x"][:, tt, cols], scalar=ALPHA, in1=t,
                                                      op0=ALU.mult, op1=ALU.add))
                        link(half_moments(r["x"][:, tt, :], tt, half))
                        if half:
                            do(whole_moments(tt), "post_var", layer, which, tt)

            def post(layer, which, tt):
                r = R[which]
                done("post_std", layer, which, tt)
                link(dve.reciprocal(moms[:, tt, 2:3], moms[:, tt, 3:4]))
                link(dve.scalar_tensor_tensor(out=x_tok[:, tt, :], in0=r["x"][:, tt, :], scalar=moms[:, tt, 0:1],
                                              in1=r["ln"][:, 0, :], op0=ALU.subtract, op1=ALU.mult))
                do(dve.scalar_tensor_tensor(out=x_tok[:, tt, :], in0=x_tok[:, tt, :], scalar=moms[:, tt, 2:3],
                                            in1=r["ln"][:, 1, :], op0=ALU.mult, op1=ALU.add), "post_x", layer, which, tt)
                done("post_x", layer, which, tt)

            def filter_(layer, i):
                c1 = 6.28125
                c2 = float(np.float32(np.round((TWO_PI - c1) * 2 ** 20) / 2 ** 20))
                c3 = float(np.float32(TWO_PI - c1 - c2))
                if i < 2:
                    bank(4, "filter", layer, i)
                    free(dve.tensor_scalar(f_arg[:, 0, :], ps[0:64, 4, 0:256], f_col[:, 2 * i:2 * i + 1],
                                           f_col[:, 2 * i + 1:2 * i + 2], ALU.add, ALU.mult), 4)
                    freed(4, "filter", layer, i)
                    link(dve.tensor_scalar(f_arg[:, 1, :], f_arg[:, 0, :], 1.0 / TWO_PI, ROUND, ALU.mult, ALU.add))
                    link(dve.tensor_scalar(f_arg[:, 1, :], f_arg[:, 1, :], -ROUND, None, ALU.add))
                    for c in (c1, c2, c3):
                        link(dve.scalar_tensor_tensor(out=f_arg[:, 0, :], in0=f_arg[:, 1, :], scalar=-c, in1=f_arg[:, 0, :],
                                                      op0=ALU.mult, op1=ALU.add))
                    do(dve.tensor_scalar(f_arg[:, 0, :], f_arg[:, 0, :], -3.1415925, 3.1415925, ALU.max, ALU.min), "f_arg", layer, i)
                if i == 2:
                    bank(7, "filter", layer, 2)
                    for t in range(2):
                        for d in range(2):
                            bank(4 + 2 * t + d, "filter", layer, 2)
                            ins = dve.tensor_tensor(f_t[:, d, :], ps[:, 4 + 2 * t + d, :], decay[:, d, t, :], ALU.mult)
                            free(ins, 4 + 2 * t + d)
                        freed(5 + 2 * t, "filter", layer, 2)
                        dve.tensor_tensor(f_sd[:, 0, t, :], f_t[:, 0, :], f_t[:, 1, :], ALU.add)
                        do(dve.tensor_tensor(f_sd[:, 1, t, :], f_t[:, 0, :], f_t[:, 1, :], ALU.subtract), "f_sd", layer, t)
                        done("f_sd", layer, t)

            def attend(layer, i, n_u):
                us = [(tt, h) for tt in q_tiles(layer) for h in range(HEADS)]
                if i >= n_u:
                    return
                nk = SEQ if us[i][0] < 2 else TOK
                s = soft[:, i % 2, :]
                for m in range(2):
                    bank(4 + m, "scores", layer, i)
                if i >= 2:
                    done("diff", layer, i - 2)
                link(dve.tensor_reduce(s[:, 0:2], ps[:, 4:6, 0:nk], AX_X, ALU.max))
                do(dve.tensor_scalar(s[:, 2:4], s[:, 0:2], -0.125, None, ALU.mult), "neg_max", layer, i)
                for m in range(2):
                    freed(4 + m, "scores", layer, i)
                link(dve.reciprocal(s[:, 6:8], s[:, 4:6]))
                link(dve.tensor_tensor(s[:, 8:9], s[:, 7:8], lam[:, 5:6], ALU.mult))
                link(dve.tensor_scalar(probs[:, i % 2, 1, 0:nk], probs[:, i % 2, 1, 0:nk], s[:, 8:9], None, ALU.mult))
                do(dve.scalar_tensor_tensor(out=probs[:, i % 2, 0, 0:nk], in0=probs[:, i % 2, 0, 0:nk], scalar=s[:, 6:7],
                                            in1=probs[:, i % 2, 1, 0:nk], op0=ALU.mult, op1=ALU.add), "diff", layer, i)

            def norms(sq, layer, br, tt):
                link(dve.tensor_reduce(hn[:, 3, :], sq[:].rearrange("p (h n) -> p h n", h=HEADS), AX_X, ALU.add))
                do(dve.tensor_scalar(hn[:, 0, :], hn[:, 3, :], 1.0 / P, EPS, ALU.mult, ALU.add), "hn_var", layer, br, tt)
                done("hn_std", layer, br, tt)
                link(dve.reciprocal(hn[:, 2, :], hn[:, 1, :]))

            def head_norm(layer, tt):
                done("o_sq", layer, tt)
                norms(o_sq, layer, 0, tt)
                bank(7, "o", layer, tt)
                prev = tt - 1
                if prev in q_tiles(layer):
                    bank(6, "y", layer, 0, prev)
                y4 = y_tok[:].rearrange("p (h n) -> p h n", h=HEADS)
                free(dve.tensor_tensor(y4, ps[:, 7, :].rearrange("p (h n) -> p h n", h=HEADS), wide(hn[:, 2, :], P, 2), ALU.mult), 7)
                freed(7, "o", layer, tt)
                do(dve.tensor_tensor(y4, y4, wide(da_g[:], HEADS), ALU.mult), "y_tok", layer, 0, tt)

            def hy_dft(layer, s):
                for kt in range(2):
                    re, im = 4 + 2 * kt, 5 + 2 * kt
                    bank(re, "U", layer, s)
                    bank(im, "U", layer, s)
                    dve.tensor_tensor(spec_t[:, 0, :], ps[:, re, :], filt[:, 0, kt, :], ALU.mult)
                    link(dve.tensor_tensor(spec_t[:, 1, :], ps[:, im, :], filt[:, 1, kt, :], ALU.mult))
                    link(dve.tensor_tensor(spec[:, 0, kt, :], spec_t[:, 0, :], spec_t[:, 1, :], ALU.subtract))
                    free(dve.tensor_tensor(spec_t[:, 0, :], ps[:, re, :], filt[:, 1, kt, :], ALU.mult), re)
                    free(dve.tensor_tensor(spec_t[:, 1, :], ps[:, im, :], filt[:, 0, kt, :], ALU.mult), im)
                    freed(im, "U", layer, s)
                    do(dve.tensor_tensor(spec[:, 1, kt, :], spec_t[:, 0, :], spec_t[:, 1, :], ALU.add), "spec", layer, s, kt)
                    done("spec", layer, s, kt)

            def hy_idft(layer, s):
                cols = slice(s * SEQ, (s + 1) * SEQ)
                for c in range(CT):
                    b = 4 + c // 2
                    bank(b, "conv", layer, s)
                    if c >= 2:
                        done("y_hyena", layer, s, c - 2)
                    ins = dve.scalar_tensor_tensor(out=hy_t[:, c % 2, :], in0=uT[:, c, cols], scalar=pcol[:, 48 + c:49 + c],
                                                   in1=ps[:, b, (c % 2) * 256:(c % 2) * 256 + 256], op0=ALU.mult, op1=ALU.add)
                    if c % 2:
                        free(ins, b)
                        freed(b, "conv", layer, s)
                    else:
                        link(ins)
                    do(dve.tensor_tensor(y[:, 2, c, cols], hy_t[:, c % 2, :], x0T[:, c, cols], ALU.mult), "y_hyena", layer, s, c)

            def gla_gate(layer, tt):
                done("lg", layer, tt)
                if tt > 0:
                    bank(4, "tail", layer, tt - 1)
                if tt == 0:
                    link(dve.memset(att[:], 0.0))
                free(dve.scalar_tensor_tensor(out=la[:], in0=ps[:, 4, :], scalar=0.0, in1=lg[:], op0=ALU.min, op1=ALU.subtract), 4)

            def gla_sum(layer, tt):
                freed(6, "b", layer, tt)
                freed(4, "tail", layer, tt)
                freed(5, "ktok", layer, tt)
                if tt > 0:
                    bank(5, "u_state", layer, tt - 1)
                do(dve.tensor_tensor(ku[:], etail[:], wide(ktok[:], 2), ALU.mult), "ku", layer, tt)
                for j in range(2):
                    c = 2 * tt + j
                    for d in range(2):
                        n = c if d == 0 else (3 - c if c < 4 else 11 - c)
                        t = 64 * j + (63 if d == 0 else 0)
                        do(dve.tensor_copy(dec[:, d, n, :], eb[:, 0, 2 * d:2 * d + 2, t]), "dec", layer, tt, 2 * j + d)
                if tt in q_tiles(layer):
                    if tt > q_tiles(layer)[0]:
                        bank(7, "att", layer, tt - 1)
                    cols = slice(tt * P, (tt + 1) * P)
                    four = lambda ap: ap.rearrange("p (d a) t -> p d a t", d=2)
                    dve.tensor_tensor(four(qe[:]), four(eb[:, 1, :, :]), wide(gqk[:, 0:2, cols], 2), ALU.mult)
                    link(dve.tensor_tensor(four(ke[:]), four(eb[:, 2, :, :]), wide(gqk[:, 2:4, cols], 2), ALU.mult))
                    link(dve.tensor_tensor(gqk[:, 2:4, cols], gqk[:, 0:2, cols], eb[:, 0, 2:4, :], ALU.mult))
                    do(dve.tensor_tensor(gqk[:, 0:2, cols], gqk[:, 0:2, cols], eb[:, 0, 0:2, :], ALU.mult), "qke", layer, tt)

            def gla_att(layer, tt):
                if tt > q_tiles(layer)[0]:
                    bank(6, "intra", layer, tt - 1)
                for r in range(2):
                    bank(6 + r, "att", layer, tt)
                    free(dve.copy_predicated(att[:, r, :, :].rearrange("p (d a) t -> p d a t", d=2), wide(mask[:], 2, 2),
                                             ps[:, 6 + r, :].rearrange("p (d a t) -> p d a t", d=2, a=2)), 6 + r)

            def gla_scan(layer):
                for d in range(2):
                    freed(4 + d, "u_state", layer, 3)
                done("dec", layer, 3, 3)
                for n in range(1, 7):
                    for d in range(2):
                        for p_ in range(2):
                            ins = dve.scalar_tensor_tensor(out=states[:, d, n, p_, :], in0=states[:, d, n - 1, p_, :],
                                                           scalar=dec[:, d, n, p_:p_ + 1], in1=states[:, d, n, p_, :],
                                                           op0=ALU.mult, op1=ALU.add)
                    if n < 6:
                        link(ins)
                do(ins, "scanned", layer)

            def gla_out(layer, tt):
                freed(6, "intra", layer, tt)
                for r in range(2):
                    bank(4 + r, "inter", layer, tt)
                    part = go[:, tt, :].rearrange("p (a r n) -> p a r n", a=2, r=2)[:, :, r, :]
                    free(dve.tensor_tensor(part, part, ps[:, 4 + r, 0:256].rearrange("p (a n) -> p a n", a=2), ALU.add), 4 + r)
                done("g_sq", layer, tt)
                norms(g_sq, layer, 1, tt)
                g4 = go[:, tt, :].rearrange("p (h n) -> p h n", h=HEADS)
                link(dve.tensor_tensor(g4, g4, wide(hn[:, 2, :], P, 2), ALU.mult))

            def y_split(layer):
                t0 = tok0(layer)
                for n in range(3 * CT):
                    done("ys_hi", layer, n)
                    do(dve.tensor_tensor(ys_lo[:, n, t0:TOK], y[:, n // CT, n % CT, t0:TOK], ys_hi[:, n, t0:TOK].bitcast(F32),
                                         ALU.subtract), "ys_ready", layer, n)

            def up(layer, c0):
                split_to(c0 + AHEAD)
                t0 = tok0(layer)
                n_groups = UP_GROUPS
                W0, W2 = 52, 140
                if layer == 0:
                    dve.sem_inc(sem("act_lo"), 2)
                    C.skip("act_lo", 2)
                C.base("act_lo", layer)
                C.base("up_prod", layer)
                C.base("up_tap", layer)
                l0 = C.seen.get("up_tap", 0)
                b0 = [at(f"bank_full{b}", "base", "up", layer) for b in range(8)]
                m0, g0, h0 = at("up_mid", "base", layer), at("up_gelu", "base", layer), at("act_hi", "base", layer)
                dve.wait_ge(sem("x_out"), 16 * at("x_out", layer, 0, 3))
                def up_group(i, h):
                    for j in range(4):
                        c = c0 + AHEAD + 4 * h + j
                        s = c % NBUF
                        dve.wait_ge(sem("hi_ready"), i * 8 + (c + 1))
                        dve.tensor_tensor(w_lo[:, s, :], stage[:, s, :], w_hi[:, s, :].bitcast(F32), ALU.subtract)\
                           .then_inc(sem("lo_ready"), 1)
                    for p_ in range(2):
                        for side in range(2):
                            for a in range(2):
                                b = 4 * h + 2 * a + p_
                                dst, src = seqs(ffn_t[:, p_, a, :], layer), seqs(ps[:, b, :], layer)
                                to, of = (slice(1, SEQ), slice(0, SEQ - 1)) if side == 0 else (slice(0, SEQ - 1), slice(1, SEQ))
                                col = pcol[:, bass.ds(i * 4 + ((W0, W2)[side] + 22 * a + 2 * h + p_), 1)]
                                if side == 0:
                                    dve.wait_ge(sem("up_mid"), i * 8 + (m0 + 4 * h + 2 * p_ + a + 1))
                                else:
                                    dve.wait_ge(sem("up_tap"), i * 8 + (l0 + 4 * h + 2 * p_ + a + 1))
                                dve.scalar_tensor_tensor(out=dst[:, :, to], in0=src[:, :, of], scalar=col, in1=dst[:, :, to],
                                                         op0=ALU.mult, op1=ALU.add)\
                                   .then_inc(sem("up_tap") if side == 0 else sem(f"bank_free{b}"), 1)
                    for p_ in range(2):
                        dve.wait_ge(sem("up_gelu"), i * 4 + (g0 + 2 * h + p_ + 1))
                        dve.wait_ge(sem(f"bank_free{4 * h + p_}"), i + (b0[4 * h + p_] + 1))
                        dve.tensor_tensor(ffn_t[:, p_, 0, t0:TOK], ffn_t[:, p_, 0, t0:TOK], ffn_t[:, p_, 1, t0:TOK], ALU.mult)\
                           .then_inc(sem("up_prod"), 1)
                    for p_ in range(2):
                        dve.wait_ge(sem("act_hi"), i * 4 + (h0 + 2 * h + p_ + 1))
                        dst = act_lo[:, bass.ds(i * 4 + (2 * h + p_), 1), t0:TOK].rearrange("p a t -> p (a t)")
                        hi = act_hi[:, bass.ds(i * 4 + (2 * h + p_), 1), t0:TOK].rearrange("p a t -> p (a t)").bitcast(F32)
                        dve.tensor_tensor(dst, ffn_t[:, p_, 0, t0:TOK], hi, ALU.subtract).then_inc(sem("act_lo"), 1)

                with dve.Fori(0, UP_GROUPS // 2) as i:
                    for h in range(2):
                        up_group(i, h)
                up_group(UP_GROUPS // 2, 0)
                C.skip("act_lo", 2 * n_groups)
                C.skip("up_prod", 2 * n_groups)
                C.skip("up_tap", 4 * n_groups)
                C.base("act_lo", "end", layer)
                cursor[0] += 4 * n_groups

            fns = dict(start=start, params_turn=params_turn, modcols=modcols, moments=moments, normal=normal,
                       modulate=modulate, chunk=chunk, evac=evac, filter=filter_, attend=attend, head_norm=head_norm, hy_dft=hy_dft, hy_idft=hy_idft,
                       gla_gate=gla_gate, gla_sum=gla_sum, gla_att=gla_att, gla_scan=gla_scan, gla_out=gla_out,
                       y_split=y_split, post=post, up=up)
            for st in steps:
                if st[0] in fns:
                    fns[st[0]](*st[1:])
    return C


INPUTS = ["x", "c", "ctx", "c_ctx", "w_ada", "b_ada", "w_in", "da_lambda", "da_norm_g", "gla_w_gate", "gla_b_gate",
          "gla_norm_g", "hy_conv_w", "hy_conv_b", "hy_w1", "hy_b1", "hy_freq1", "hy_w2", "hy_b2", "hy_freq2", "hy_w3",
          "hy_skip", "w_branch", "w_out", "ln1_g", "ln1_b", "ffn_w_up", "ffn_conv_w", "ffn_conv_b", "ffn_w_down",
          "ln2_g", "ln2_b"]


def kernel(**inputs):
    import concourse.bacc as bacc
    from concourse.bass_utils import run_bass_kernel_spmd

    arrays = {name: np.ascontiguousarray(inputs[name]) for name in INPUTS}
    arrays.update(shape_constants())

    def build(known):
        nc = bacc.Bacc("TRN2", target_bir_lowering=False, num_devices=1)
        args = {n: nc.dram_tensor("in_" + n, a.shape, mybir.dt.from_np(a.dtype), kind="ExternalInput").ap()
                for n, a in arrays.items()}
        out = nc.dram_tensor("out_x", (1, SEQ, D), F32, kind="ExternalOutput").ap()
        return nc, build_program(nc, args, out, known)

    _, counts = build(None)
    nc, _ = build(counts)
    r = run_bass_kernel_spmd(nc, [{"in_" + n: a for n, a in arrays.items()}], core_ids=[0])
    return r.results[0]["out_x"]
```

```python
import math
from contextlib import ExitStack

import numpy as np
import concourse.bass as bass
from concourse import mybir

F32 = mybir.dt.float32
F32R = mybir.dt.float32r
I32 = mybir.dt.int32
ACT = mybir.ActivationFunctionType
ALU = mybir.AluOpType
AX_X = mybir.AxisListType.X

P = 128
D = 1024
DEPTH = 2
SEQ = 256
TOK = 2 * SEQ
KT = D // P
HEADS = 4
BW = 512
CT = BW // P
DFF = 2816
FT = DFF // P
CHUNK = 64
EPS = 1e-5
ALPHA = (2.0 * DEPTH) ** 0.25
COLS = 512
NBUF = 4
AHEAD = 3
TWO_PI = 2.0 * math.pi
ROUND = 12582912.0


def shape_constants():
    f = np.float32
    out = {"ident": np.eye(P, dtype=f)}
    s, t = np.meshgrid(np.arange(P), np.arange(P), indexing="ij")
    same = s // CHUNK == t // CHUNK
    first = t // CHUNK * CHUNK
    upto = [same & (s <= t), same & (s >= t)]
    ref = [same & (s <= first + CHUNK // 2), same & (s >= first + CHUNK // 2 - 1)]
    after = [same & (s > t), same & (s < t)]
    tau = 1.0 / 16.0
    cums = [np.concatenate([upto[d] * tau, (upto[d].astype(f) - ref[d].astype(f)) * tau], 1) for d in range(2)]
    out["cums"] = np.stack(cums, 1).astype(f).reshape(P, 2 * 256)
    out["tail"] = np.stack([after[d] * tau for d in range(2)], 1).astype(f).reshape(P, 2 * P)
    out["mask"] = np.stack([upto[0], upto[1]], 1).astype(np.int32).reshape(P, 2 * P)
    pos = np.arange(SEQ)
    inv = (10000.0 ** (-np.arange(16, dtype=f) / f(16))).astype(f)
    row, col = (pos // 64).astype(f)[:, None] * inv, (pos % 64).astype(f)[:, None] * inv
    ang = np.concatenate([row, row, col, col], 1)
    sign = np.tile(np.concatenate([-np.ones(16), np.ones(16)]), 2)[None]
    out["rope"] = np.stack([np.cos(ang), np.sin(ang) * sign], 1).astype(f).reshape(2, P, P).transpose(1, 0, 2).reshape(P, 256)
    w = np.pi * (2 * np.arange(256)[None] + 1) * np.arange(256)[:, None] / 512.0
    dft = np.stack([np.cos(w), np.sin(w)])
    out["dft"] = dft.reshape(2, 2, P, 256).transpose(2, 0, 1, 3).astype(f).reshape(P, 1024)
    idft = dft.transpose(0, 2, 1) / 256.0
    out["idft"] = idft.reshape(2, 2, P, 256).transpose(2, 0, 1, 3).astype(f).reshape(P, 1024)
    tt = np.linspace(0.0, 1.0, SEQ, dtype=f)[:, None]
    ww = (f(2.0 * math.pi) * np.arange(SEQ, dtype=f)[:, None] / f(SEQ)).astype(f)
    ff = np.linspace(1e-4, 15, 16, dtype=f)[None, :]
    out["feat"] = np.ascontiguousarray(np.concatenate([tt, np.cos(ff * ww), -np.sin(ff * ww)], 1).T.astype(f))
    lo, hi = math.log(1e-2) / 1.5, math.log(1e-2) / 0.3
    deltas = np.abs(np.linspace(lo, hi, BW, dtype=f))
    decay = np.exp(-tt * deltas).astype(f)
    back = decay.copy()
    back[0] = 0.0
    out["decay"] = np.stack([decay, back]).reshape(2, 2, P, BW).transpose(2, 0, 1, 3).reshape(P, 2048).astype(f)
    return out


class Counts:

    def __init__(self, known=None):
        self.known, self.seen, self.place = known, {}, {}

    def tick(self, stage, *who):
        self.seen[stage] = self.seen.get(stage, 0) + 1
        self.place[(stage, *who)] = self.seen[stage]
        return 1

    def skip(self, stage, n):
        self.seen[stage] = self.seen.get(stage, 0) + n

    def base(self, stage, *who):
        self.place[(stage, "base", *who)] = self.seen.get(stage, 0)
        return self.seen.get(stage, 0)

    def at(self, stage, *who):
        return self.known.place[(stage, *who)] if self.known else 1


def q_tiles(layer):
    return range(4) if layer < DEPTH - 1 else range(2, 4)


def tok0(layer):
    return 0 if layer < DEPTH - 1 else SEQ


ADA_GROUPS = (range(0, 4), range(4, 12))
UP_GROUPS = FT // 2


def norms(layer, which, then, tiles):
    slots = []
    for n, tt in enumerate(tiles):
        slots.append([("post", layer, which, tt)])
        if then:
            slots[-1] += [("moments", *then, tt), ("deviation", *then, tt)]
            if n:
                slots[-1].append(("normal", *then, tt - 1))
                if n == 2:
                    slots[-1].append(("turn", *then, 0))
    if then:
        slots.append([("normal", *then, tiles[-1]), ("turn", *then, 1)])
        latents_only = then == (DEPTH - 1, 0)
        slots.append([("modulate", *then, s, b) for b in range(4) for s in range(1 if latents_only else tiles[0] // 2, 2)])
    return slots


class Group:

    def __init__(self, kind, layer, index, turn, n_chunks, tiles, bank0=0, pair=False):
        self.kind, self.layer, self.index, self.turn = kind, layer, index, turn
        self.n, self.tiles = n_chunks, list(tiles)
        self.key = (kind, layer, index)
        self.late = pair or kind in ("a_q", "a_k", "a_v", "hy", "g_v", "g_qk") or self.key == ("ada", 0, 3)
        self.at = []
        self.bank0 = bank0
        self.pair = pair



def plan():
    steps = []

    def group(kind, layer, index, turn, n, tiles, between=(), bank0=0, pair=False):
        g = Group(kind, layer, index, turn, n, tiles, bank0, pair)
        for j in range(n):
            steps.append(("chunk", g, j))
            if j == n - 1:
                steps.append(("evac", g))
            elif between:
                steps.extend(between.pop(0))
        if between:
            steps.extend(between.pop(0))

    def ada(layer, groups, bank0=4):
        out = []
        for i in groups:
            g = Group("ada", layer, i, "A", 4, [i % 2], bank0)
            out += [[("chunk", g, j)] for j in range(4)]
            out[-1].append(("evac", g))
        return out

    def spread(slots, chunks, first, per):
        for n, item in enumerate(chunks):
            slots[first + n // per] += item

    steps += [("start",), ("modbias", 0, 0)]
    slots = ada(0, ADA_GROUPS[0])
    for tt in range(4):
        slots[9 + tt].append(("moments", 0, 0, tt))
    steps += sum(slots, [])
    steps += [("modload", 0, 0), ("params", 0)]
    steps += [("deviation", 0, 0, tt) for tt in range(4)] + [("normal", 0, 0, tt) for tt in range(4)]
    steps += [("turn", 0, 0, 0), ("modcols", 0, 0), ("turn", 0, 0, 1)]
    steps += [("modulate", 0, 0, s, b) for b in range(4) for s in range(2)]
    for layer in range(DEPTH):
        last = layer == DEPTH - 1
        qt, every = list(q_tiles(layer)), list(range(4))
        filt = [[] for _ in range(12)]
        if last:
            filt[0] += [("modulate", layer, 0, 0, b) for b in range(4)]
            filt[8].append(("modcols", layer, 1))
        else:
            filt[1].append(("consts",))
        filt[1 if last else 2].append(("params_turn", layer))
        for n in range(2):
            filt[4 + 4 * n].append(("qk_turn", layer, n))
        for n in range(4):
            filt[4 + n].append(("filter", layer, n))
        group("a_q", layer, 0, "T", 4, qt, filt)

        group("a_k", layer, 0, "T", 4, every, filt)

        group("a_v", layer, 0, "T", 4, every, filt)
        units = [(tt, h) for tt in qt for h in range(HEADS)]
        n_u = len(units)
        mix = []
        for i in range(n_u + 3):
            mix.append([("attend", layer, i, n_u)] if i < n_u + 2 else [])
            if i >= 3 and units[i - 3][1] == HEADS - 1:
                mix[-1].append(("y_turn", layer, 0, units[i - 3][0]))
            if 2 <= i < n_u + 2 and units[i - 2][1] == HEADS - 1:
                mix[-1].append(("head_norm", layer, units[i - 2][0]))
        for j in range(3):
            group("hy", layer, j, "F", 4, range(4), mix)
        group("g_v", layer, 0, "T", 4, every, mix)
        group("g_qk", layer, 0, "F", 4, range(4), mix)
        group("z", layer, 0, "Z", 1, range(1), mix)
        seqs = [0, 1] if not last else [1]
        for s in seqs:
            mix += [[("hy_turn", layer, s)], [("hy_dft", layer, s)], [("hy_idft", layer, s)]]
        mix += [[("gla_gate", layer, 0)], [("gla_sum", layer, 0)]]
        for tt in every:
            if tt < 3:
                mix += [[("gla_gate", layer, tt + 1)]]
            if tt in qt:
                mix += [[("gla_att", layer, tt)]]
            mix += [[("gla_state", layer, tt)]]
            if tt < 3:
                mix += [[("gla_sum", layer, tt + 1)]]
        mix += [[("gla_scan", layer)]]
        for tt in qt:
            mix += [[("gla_out", layer, tt)]]
        for j in range(5):
            group("gate", layer, j, "F", 4, range(4), mix)
        steps += sum(mix, [])
        del mix[:]
        slots = [[] for _ in range(20)]
        for n, tt in enumerate(qt):
            slots[4 + n].append(("y_turn", layer, 1, tt))
        slots[6 if last else 7].append(("y_split", layer, 1))
        if not last:
            slots[0].append(("modbias", layer, 1))
            spread(slots, ada(layer, ADA_GROUPS[1]), 0, 2)
            slots[15].append(("modload", layer, 1))


        slots[0].append(("y_split", layer, 0))
        slots[2].append(("y_split", layer, 2))
        group("g_r", layer, 0, "T", 4, qt, slots)
        group("gate", layer, 5, "F", 4, range(4), slots)
        steps.append(("gates_out", layer))
        for half in range(2):
            for br in range(3):
                group("branch", layer, (half, br), "B", 2, range(4), slots, pair=(half, br) == (1, 2))
        slots = [[], [("modcols", layer, 1)] if not last else [], [("gate_rows", layer, 0)], [],
                 [("residual", layer, 0)], [], [], []]
        for half in range(2):
            group("out", layer, half, "T", 4, qt, slots, bank0=4 * half, pair=half == 1)
        steps += sum(norms(layer, 0, (layer, 1), qt), [])
        steps.append(["up", layer, None])
        slots = [[] for _ in range(FT)]
        slots[8] += [("gate_rows", layer, 1), ("residual", layer, 1)]
        if not last:

            slots[0].append(("modbias", layer + 1, 0))
            spread(slots, ada(layer + 1, range(0, 8)), 0, 3)
            slots[6].append(("modload", layer + 1, 0))
            slots[8].append(("modcols", layer + 1, 0))
            spread(slots, ada(layer + 1, range(8, 12), 0), 12, 2)
            slots[12].append(("modbias", layer + 1, 1))
            slots[20].append(("modload", layer + 1, 1))
        for half in range(2):
            group("down", layer, half, "D", FT // 2, qt, slots, bank0=4 * half, pair=half == 1)
        if not last:
            steps.append(("params", layer + 1))
        steps += sum(norms(layer, 1, None if last else (layer + 1, 0), qt), [])
    steps.append(("end",))
    total = 0
    for st in steps:
        if st[0] == "chunk":
            st[1].at.append(total)
            total += 1
        elif st[0] == "up":
            st[2] = total
            total += 4 * UP_GROUPS
    return steps, total


def act_moments(layer, which, tt):
    return (layer, which) != (0, 0) and tt < 3


def turn_bank(layer, which, s, b):
    return 4 * (1 - s) + (b + (2 if (layer, which) == (DEPTH - 1, 0) else 0)) % 4


def mod_bank(layer, part):
    return 3 if (layer, part) == (0, 0) else 6


def build_program(nc, A, out, known):
    C = Counts(known)
    at, tick = C.at, C.tick
    steps, n_chunks = plan()
    ctx = ExitStack()
    with ctx:
        sems = {}

        def sem(name):
            if name not in sems:
                sems[name] = ctx.enter_context(nc.semaphore(name))
            return sems[name]

        base = (nc.sbuf_base + 31) // 32 * 32
        end = nc.sbuf_usable_end // 32 * 32
        arena = [base]

        def put(name, shape, dt=F32, offset=None):
            size = int(np.prod(shape[1:])) * 4
            if offset is None:
                offset = arena[0]
                arena[0] += (size + 31) // 32 * 32
            assert offset + size <= end, (name, offset + size - end)
            return nc.alloc_sbuf_tensor_at(name, shape, dt, offset=offset)

        stage = put("stage", [P, NBUF, 1024])
        w_hi = put("w_hi", [P, NBUF, 1024], F32R)
        w_lo = put("w_lo", [P, NBUF, 1024], F32R)
        ht_at = arena[0]
        h_hi = put("h_hi", [P, KT, TOK], F32R)
        h_lo = put("h_lo", [P, KT, TOK], F32R)
        ident = put("ident", [P, P])
        cums = put("cums", [P, 2, 256])
        tail = put("tail", [P, 2, P])
        mask = put("mask", [P, 2, P], I32)
        rope = put("rope", [P, 2, 2, 64])
        dft = put("dft", [P, 2, 2, 256])
        idft = put("idft", [P, 2, 2, 256])
        filt_at = arena[0]
        filt = put("filt", [P, 2, 2, BW])
        ada_c = put("ada_c", [P, KT, P], F32R)
        mod_row = put("mod_row", [4, 2, COLS], offset=filt_at + 4096)
        pcol = put("pcol", [P, 228])
        mod_a = put("mod_a", [P, 2, 2, KT])
        mod_b = put("mod_b", [P, 2, 4, KT])
        mrows = put("mrows", [64, 3, P])
        lam = put("lam", [P, 8])
        da_g = put("da_g", [P, P])
        gla_g = put("gla_g", [P, P])
        w_gate = put("w_gate", [33, 2 * 256])
        f_w1 = put("f_w1", [33, 64])
        f_w2 = put("f_w2", [64, 64])
        f_col = put("f_col", [64, 4])
        stat = put("stat", [P, 8, 12])
        moms = put("moms", [P, 8, 5])
        soft = put("soft", [P, 2, 12])
        hn = put("hn", [P, 4, 4])
        dec = put("dec", [P, 2, 8, 2])
        c_act = put("c_act", [P, 16])
        eps_col = put("eps_col", [P, 1])
        y_at = end - 71680 - 24576
        assert arena[0] <= y_at, arena[0] - y_at
        y = put("y", [P, 3, CT, TOK], offset=y_at)
        t_at = end - 71680

        def tmp(name, kb, shape, dt=F32, at_=t_at):
            return put(name, shape, dt, offset=at_ + int(kb * 1024))

        rows = tmp("rows", 42, [88, 3, P])
        lam_in = tmp("lam_in", 43.5, [P, 4, 64])
        lam_prod = tmp("lam_prod", 44.5, [P, 2, 64])
        f_w3 = tmp("f_w3", 66, [64, 2, BW])
        zT = tmp("zT", 40, [33, TOK])
        x_tok = tmp("x_tok", 0, [P, 4, D])
        xn = [tmp("xn_mix", 16, [P, 4, D]), tmp("xn_ffn", 36, [P, 4, D])]
        xm = tmp("xm", 32, [P, 4, SEQ])
        qT = tmp("qT", 0, [P, HEADS, TOK])
        kT = tmp("kT", 8, [P, HEADS, TOK])
        v_tok = tmp("v_tok", 16, [P, 4, BW])
        probs = tmp("probs", 24, [P, 2, 2, TOK])
        rope_t = tmp("rope_t", 24, [P, 2, 2, BW])
        qk_tok = tmp("qk_tok", 36, [P, 4, BW])
        attT = tmp("attT", 32, [P, 2, TOK])
        o_sq = tmp("o_sq", 42, [P, BW])
        y_tok = tmp("y_tok", 44, [P, BW])
        f_arg = tmp("f_arg", 46, [64, 2, 256])
        f_h = tmp("f_h", 48, [64, 2, 256])
        decay = tmp("decay", 50, [P, 2, 2, BW])
        f_t = tmp("f_t", 58, [P, 2, BW])
        f_sd = tmp("f_sd", 62, [P, 2, 2, BW])
        feat = put("feat", [33, 256], offset=t_at + 45 * 1024)
        x0T = tmp("x0T", 46, [P, CT, TOK])
        uT = tmp("uT", 54, [P, CT, TOK])
        vvT = tmp("vvT", 62, [P, 2, TOK])
        u_tok = tmp("u_tok", 0, [P, 2, BW])
        spec = tmp("spec", 8, [P, 2, 2, BW])
        spec_t = tmp("spec_t", 16, [P, 2, BW])
        hy_t = tmp("hy_t", 20, [P, 2, SEQ])
        gqk = tmp("gqk", 32, [P, 4, TOK])
        gv = put("gv", [P, 4, BW], offset=y_at + 8192)
        go = tmp("go", 0, [P, 4, BW])
        states = tmp("states", 8, [P, 2, 7, 2, P])
        la = tmp("la", 24, [P, BW])
        eb = tmp("eb", 26, [P, 3, 4, P])
        qe = tmp("qe", 42, [P, 4, P])
        ke = tmp("ke", 44, [P, 4, P])
        att = tmp("att", 46, [P, 2, 4, P])
        ku = tmp("ku", 50, [P, 2, 256])
        ktok = tmp("ktok", 52, [P, 256])
        lg = tmp("lg", 53, [P, BW])
        g_sq = tmp("g_sq", 55, [P, BW])
        rg = tmp("rg", 57, [P, 2, BW])
        etail = tmp("etail", 61, [P, 2, 256])
        sig = tmp("sig", 66, [P, 2, TOK])
        ys_hi = tmp("ys_hi", 0, [P, 3 * CT, TOK], F32R)
        ys_lo = tmp("ys_lo", 24, [P, 3 * CT, TOK], F32R)
        ys_at = (CT, 0, 2 * CT)
        acc = tmp("acc", 48, [P, 4, TOK])
        sig_in = tmp("sig_in", 56, [P, 4, TOK])
        prod = tmp("prod", 64, [P, 2, TOK])
        R = []
        for n, (where, name) in enumerate(((t_at, "r1"), (ht_at, "r2"))):
            R.append(dict(
                x=put(name + "x", [P, 4, D], offset=where),
                g=put(name + "g", [P, 2, D], offset=where + 16384),
                ln=put(name + "ln", [P, 2, D], offset=where + 24576),
            ))
        R[0]["t"] = R[1]["t"] = put("res_t", [P, 2, COLS], offset=filt_at)
        act_hi = put("act_hi", [P, FT, TOK], F32R, offset=y_at)
        act_lo = put("act_lo", [P, FT, TOK], F32R, offset=y_at + FT * TOK * 4)
        ffn_t = put("ffn_t", [P, 2, 2, TOK], offset=filt_at)

        ps = ctx.enter_context(nc.psum_tensor("ps", [P, 8, 512], F32))

        def dram(name, shape):
            return nc.dram_tensor(name, shape, F32, kind="Internal").ap()

        d_mod = [[dram(f"d_mod{i}{part}", [4, len(ADA_GROUPS[part]) * COLS]) for part in range(2)] for i in range(DEPTH)]
        d_gate = [dram(f"d_gate{i}", [2, 4 * D]) for i in range(DEPTH)]
        d_sig = [dram(f"d_sig{i}", [24, P, TOK]) for i in range(DEPTH)]
        d_x = [dram(f"d_x{i}", [4, P, D]) for i in range(2 * DEPTH - 1)]

        W_IN_AT = {"a_q": 0, "a_k": 512, "a_v": 1024, "g_qk": 1536, "g_v": 2048, "g_r": 2560,
                   "z": 3072, "hy": 3104, "gate": 4640}

        def rows_of(w, k0, nk, c0, nc_):
            return w[k0 * P:(k0 + nk) * P, c0:c0 + nc_].rearrange("(k p) n -> p k n", p=P)

        def source(g, j):
            if g.kind == "ada":
                return rows_of(A["w_ada"][g.layer], 2 * j, 2, g.index * COLS, COLS)
            if g.kind == "z":
                return rows_of(A["w_in"][g.layer], 0, KT, W_IN_AT["z"], P)
            if g.kind in W_IN_AT:
                return rows_of(A["w_in"][g.layer], 2 * j, 2, W_IN_AT[g.kind] + g.index * COLS, COLS)
            if g.kind == "branch":
                half, br = g.index
                return rows_of(A["w_branch"][g.layer, br], 2 * j, 2, half * COLS, COLS)
            w = A["w_out"] if g.kind == "out" else A["ffn_w_down"]
            return rows_of(w[g.layer], 2 * j, 2, g.index * COLS, COLS)

        def bc(ap, n):
            return ap.rearrange("(a n) -> a n", a=1).to_broadcast([P, n])

        block = ctx.enter_context(nc.Block())

        @block.sync
        def _(sp):
            def residual(layer, which):
                r = R[which]
                if which == 0:
                    sp.wait_ge(sem("bank_full3"), at("bank_full3", "branch", layer, (1, 2)))
                    if layer:
                        sp.wait_ge(sem("x_out"), 16 * at("x_out", layer - 1, 1, 3))
                else:
                    sp.wait_ge(sem("bank_full3"), at("bank_full3", "base", "up end", layer))
                    sp.wait_ge(sem("x_out"), 16 * at("x_out", layer, 0, 3))
                for tt in q_tiles(layer):
                    if layer == 0 and which == 0:
                        src = (A["ctx"] if tt < 2 else A["x"])[0, (tt % 2) * P:(tt % 2 + 1) * P, :]
                    else:
                        src = d_x[2 * layer + which - 1][tt]
                    sp.dma_start(r["x"][:, tt, :], src).then_inc(sem(f"res_x{tt // 2}"), 16 * tick(f"res_x{tt // 2}", layer, which, tt % 2))
                for n, name in enumerate((("ln1_g", "ln1_b"), ("ln2_g", "ln2_b"))[which]):
                    sp.dma_start(r["ln"][:, n, :], bc(A[name][layer], D)).then_inc(sem("res_ln"), 16 * tick("res_ln", layer, which, n))

            def load(c, src, kt=2):
                s = c % NBUF
                if c >= NBUF:
                    sp.wait_ge(sem("lo_ready"), c + 1 - NBUF)
                sp.dma_start(stage[:, s, :].rearrange("p (k n) -> p k n", k=kt), src).then_inc(sem(f"landed{s}"), 32)

            for st in steps:
                if st[0] == "residual":
                    residual(*st[1:])
                elif st[0] == "start":
                    sp.dma_start(rows[0:8, 0, :], A["c"].rearrange("a (k p) -> (a k) p", p=P)).then_inc(sem("c_in"), 16)
                    sp.dma_start(rows[8:16, 0, :], A["c_ctx"].rearrange("(k p) -> k p", p=P)).then_inc(sem("c_in"), 16)
                    sp.dma_start(ident[:], A["ident"]).then_inc(sem("ident_in"), 16)
                elif st[0] == "consts":
                    for name, t in (("dft", dft), ("rope", rope), ("idft", idft), ("cums", cums), ("tail", tail), ("mask", mask)):
                        flat = " a b c" if name in ("rope", "dft", "idft") else " a b"
                        sp.dma_start(t[:].rearrange(f"p{flat} -> p ({flat.strip()})"), A[name]).then_inc(sem("consts_in"), 16)
                elif st[0] == "chunk":
                    g, j = st[1], st[2]
                    load(g.at[j], source(g, j), kt=KT if g.kind == "z" else 2)
                elif st[0] == "up":
                    layer, c0, n_groups = st[1], st[2], UP_GROUPS
                    wv = A["ffn_w_up"][layer].rearrange("(k p) (s g n) -> p k s g n", p=P, s=2, n=256)
                    with sp.Fori(0, n_groups) as i:
                        for j in range(4):
                            s = (c0 + j) % NBUF
                            sp.wait_ge(sem("lo_ready"), i * 4 + (c0 + j - NBUF + 1))
                            for a in range(2):
                                dst = stage[:, s, :].rearrange("p (k s n) -> p k s n", k=2, s=2)[:, :, a, :]
                                src = wv[:, 2 * j:2 * j + 2, a, bass.ds(i, 1), :].rearrange("p k a n -> p k (a n)")
                                sp.dma_start(dst, src).then_inc(sem(f"landed{s}"), 16)

        @block.gpsimd
        def _(pool):
            def dma(dst, src, stage_, *who):
                pool.dma_start(dst, src, allow_slow_non_contiguous=True).then_inc(sem(stage_), 16 * tick(stage_, *who))

            def dma_in(n_stage, who, *pairs):
                for n, (dst, src) in enumerate(pairs):
                    dma(dst, src, n_stage, *who, n)


            def params(layer):
                if layer:
                    pool.wait_ge(sem("bank_full7"), at("bank_full7", "down", layer - 1, 1))
                    pool.wait_ge(sem("act_hi"), at("act_hi", "end", layer - 1))
                else:
                    pool.wait_ge(sem("bank_full4"), at("bank_full4", "c"))
                dma_in("params_in", (layer,),
                       (rows[0:36, 0, :], A["hy_conv_w"][layer].rearrange("w (t p) -> (w t) p", p=P)),
                       (rows[36:48, 0, :], A["hy_conv_b"][layer].rearrange("(t p) -> t p", p=P)),
                       (rows[48:52, 0, :], A["hy_skip"][layer].rearrange("(t p) -> t p", p=P)),
                       (rows[0:88, 1, :], A["ffn_conv_w"][layer, 0:2].rearrange("w (t p) -> (w t) p", p=P)),
                       (rows[0:44, 2, :], A["ffn_conv_w"][layer, 2].rearrange("(t p) -> t p", p=P)),
                       (rows[44:88, 2, :], A["ffn_conv_b"][layer].rearrange("(t p) -> t p", p=P)),
                       (lam_in[:].rearrange("p a b -> p (a b)"), bc(A["da_lambda"][layer].rearrange("a b -> (a b)"), 256)),
                       (da_g[:], bc(A["da_norm_g"][layer], P)),
                       (gla_g[:], bc(A["gla_norm_g"][layer], P)),
                       (f_w1[:], A["hy_w1"][layer]), (f_w2[:], A["hy_w2"][layer]),
                       (f_w3[:].rearrange("p a b -> p (a b)"), A["hy_w3"][layer]),
                       (f_col[:, 0:1], A["hy_b1"][layer].rearrange("(p a) -> p a", a=1)),
                       (f_col[:, 1:2], A["hy_freq1"][layer].rearrange("(p a) -> p a", a=1)),
                       (f_col[:, 2:3], A["hy_b2"][layer].rearrange("(p a) -> p a", a=1)),
                       (f_col[:, 3:4], A["hy_freq2"][layer].rearrange("(p a) -> p a", a=1)),
                       (feat[:], A["feat"]),
                       (decay[:].rearrange("p a b c -> p (a b c)"), A["decay"]))
                pool.memset(w_gate[0:32, :], 0.0).then_inc(sem("gate_zero"), tick("gate_zero", layer))
                pool.wait_ge(sem("gate_zero"), at("gate_zero", layer))
                for d in range(2):
                    dma(w_gate[16 * d:16 * d + 16, 256 * d:256 * d + 256], A["gla_w_gate"][layer, d], "params_in", layer, 100 + d)
                dma(w_gate[32:33, :], A["gla_b_gate"][layer].rearrange("d n -> (d n)").rearrange("(a n) -> a n", a=1),
                    "params_in", layer, "last")

            def modbias(layer, part):
                n, w0 = (16, 0) if part == 0 else (32, 2 * D)
                if (layer, part) != (0, 0):
                    before = (layer, 0) if part else (layer - 1, 1)
                    pool.wait_ge(sem("mod_cols"), at("mod_cols", *before))
                    pool.wait_ge(sem("gate_out"), 16 * at("gate_out", 0)) if layer and not part else None
                for v in range(2):
                    dma(mrows[v * n:(v + 1) * n, 2, :],
                        A["b_ada"][layer, w0:w0 + n * P].rearrange("(t p) -> t p", p=P), "mod_in", layer, part, "bias", v)

            def modload(layer, part):
                n = 16 if part == 0 else 32
                for b in range(2):
                    pool.wait_ge(sem(f"mod_out{b}"), 16 * at(f"mod_out{b}", layer, ADA_GROUPS[part][-2 + b]))
                for lo in range(2):
                    dma(mrows[0:2 * n, lo, :], d_mod[layer][part][2 * lo:2 * lo + 2, :].rearrange("v (t p) -> (v t) p", p=P),
                        "mod_in", layer, part, lo)
            def modcols(layer, part):
                if part:
                    pool.wait_ge(sem("mod_sum"), at("mod_sum", layer, 1))
                    dma(d_gate[layer].rearrange("v (t p) -> (v t) p", p=P), mrows[0:64, 0, :], "gate_out", layer)

            def evac(g):
                layer = g.layer
                if g.kind == "ada":
                    b, q = g.index % 2, g.bank0 + g.index % 2
                    part = 0 if g.index in ADA_GROUPS[0] else 1
                    n = g.index - ADA_GROUPS[part][0]
                    pool.wait_ge(sem(f"bank_free{q}"), at(f"bank_full{q}", *g.key))
                    dma(d_mod[layer][part][:, n * COLS:(n + 1) * COLS], mod_row[:, b, :], f"mod_out{b}", layer, g.index)
                if g.kind == "gate":
                    for j in range(4):
                        pool.wait_ge(sem(f"bank_free{j}"), at(f"bank_full{j}", *g.key))
                        o = tok0(layer)
                        dma(d_sig[layer][4 * g.index + j, :, o:TOK], sig[:, j % 2, o:TOK], f"sig_out{j % 2}", layer, g.index, j)

            def gates_out(layer):
                for j in range(2):
                    pool.wait_ge(sem(f"sig_out{j}"), 16 * at(f"sig_out{j}", layer, 5, 2 + j))
                pool.wait_ge(sem("bank_free6"), at("bank_full6", "y", layer, 1, 3))

            def chunk(g, j):
                if g.kind == "branch" and j == 0:
                    half, br = g.index
                    o = tok0(g.layer)
                    for n in range(4):
                        if (half, br) != (0, 0):
                            before = (half, br - 1) if br else (half - 1, 2)
                            pool.wait_ge(sem(f"bank_free{n}"), at(f"bank_full{n}", "branch", g.layer, before))
                        dma(sig_in[:, n, o:TOK], d_sig[g.layer][8 * br + 4 * half + n, :, o:TOK], f"sig_in{n}", g.layer, g.index)


            def gate_rows(layer, which):
                what = ("branch", layer, (1, 2)) if which == 0 else ("base", "up end", layer)
                pool.wait_ge(sem("bank_full3"), at("bank_full3", *what))
                pool.wait_ge(sem("gate_out"), 16 * at("gate_out", layer))
                for s in range(tok0(layer) // SEQ, 2):
                    v = 1 - s
                    dma(R[which]["g"][:, v, :], bc(d_gate[layer][v, 3 * which * D:(3 * which + 1) * D], D), f"gates_in{s}", layer, which)

            def post(layer, which, tt):
                pool.wait_ge(sem("post_x"), at("post_x", layer, which, tt))
                if layer == DEPTH - 1 and which == 1:
                    pool.dma_start(out[0, (tt - 2) * P:(tt - 1) * P, :], x_tok[:, tt, :]).then_inc(sem("stored"), 16)
                else:
                    dma(d_x[2 * layer + which][tt], x_tok[:, tt, :], "x_out", layer, which, tt)

            def end_():
                pool.wait_ge(sem("stored"), 32)

            fns = dict(gate_rows=gate_rows, gates_out=gates_out, modbias=modbias, params=params, modload=modload, modcols=modcols, evac=evac,
                       chunk=chunk, post=post, end=end_)
            for st in steps:
                if st[0] in fns:
                    fns[st[0]](*st[1:])

        @block.tensor
        def _(pe):
            used = [0] * 8
            owed = [True]

            def claim(b):
                if used[b]:
                    pe.wait_ge(sem(f"bank_free{b}"), used[b])
                used[b] += 1

            def full(ins, b, *who):
                ins.then_inc(sem(f"bank_full{b}"), tick(f"bank_full{b}", *who))


            def mm(out_, lhsT, rhs, start=True, stop=True):
                return pe.matmul(out_, lhsT, rhs, start=start, stop=stop, skip_group_check=True)

            def pay(ins):
                if owed[0]:
                    ins.then_inc(sem("chunk_used"), 1)
                    owed[0] = False

            def three(out_, l_hi, l_lo, r_hi, r_lo, first, last):
                pay(mm(out_, l_hi, r_hi, start=first, stop=False))
                mm(out_, l_lo, r_hi, start=False, stop=False)
                return mm(out_, l_hi, r_lo, start=False, stop=last)

            def start():
                pe.wait_ge(sem("c_in"), 32)
                pe.wait_ge(sem("ident_in"), 16)
                claim(4)
                full(pe.transpose(ps[:, 4, 0:16], rows[0:16, 0, :], ident[0:16, 0:16]), 4, "c")

            def params_turn(layer):
                pe.wait_ge(sem("params_in"), 16 * at("params_in", layer, "last"))
                pe.wait_ge(sem("consts_in"), 6 * 16)
                claim(4)
                pe.transpose(ps[:, 4, 0:52], rows[0:52, 0, :], ident[0:52, 0:52])
                pe.transpose(ps[:, 4, 52:140], rows[0:88, 1, :], ident[0:88, 0:88])
                full(pe.transpose(ps[:, 4, 140:228], rows[0:88, 2, :], ident[0:88, 0:88]), 4, "params", layer)

            def ada(layer, part, c0, n_groups):
                if c0 == 0:
                    pe.wait_ge(sem("ada_lo"), 1)
                u = [used[0], used[1]]
                for b in range(2):
                    C.base(f"bank_full{b}", layer, part)
                with pe.Fori(0, n_groups // 2) as i:
                    for b in range(2):
                        pe.wait_ge(sem(f"bank_free{b}"), i + u[b])
                        for j in range(4):
                            c = c0 + 4 * b + j
                            s = c % NBUF
                            pe.wait_ge(sem("lo_ready"), i * 8 + (c + 1))
                            for kk in range(2):
                                k = 2 * j + kk
                                ins = mm(ps[:, b, :], ada_c[:, k, :], w_hi[:, s, kk * 512:kk * 512 + 512], start=k == 0, stop=False)
                                if k == 0:
                                    ins.then_inc(sem("chunk_used"), 1)
                                ins = mm(ps[:, b, :], ada_c[:, k, :], w_lo[:, s, kk * 512:kk * 512 + 512],
                                         start=False, stop=k == KT - 1)
                            if j < 3:
                                ins.then_inc(sem("chunk_used"), 1)
                            else:
                                ins.then_inc(sem(f"bank_full{b}"), 1)
                for b in range(2):
                    used[b] += n_groups // 2
                    C.skip(f"bank_full{b}", n_groups // 2)

            def ada_chunk(g, j, c):
                b, s = g.bank0 + g.tiles[0], c % NBUF
                if c == 0:
                    pe.wait_ge(sem("ada_lo"), 1)
                if j == 0:
                    claim(b)
                for k in (2 * j, 2 * j + 1):
                    cs = slice(k % 2 * COLS, k % 2 * COLS + COLS)
                    pay(mm(ps[:, b, :], ada_c[:, k, :], w_hi[:, s, cs], start=k == 0, stop=False))
                    ins = mm(ps[:, b, :], ada_c[:, k, :], w_lo[:, s, cs], start=False, stop=k == KT - 1)
                return ins

            def modcols(layer, part):
                n = 32 if part == 0 else 64
                b = mod_bank(layer, part)
                pe.wait_ge(sem("mod_sum"), at("mod_sum", layer, part))
                claim(b)
                full(pe.transpose(ps[:, b, 0:n], mrows[0:n, 0, :], ident[0:n, 0:n]), b, "mod", layer, part)

            def turn(layer, which, s):
                for t in range(2):
                    pe.wait_ge(sem("ln_x"), at("ln_x", layer, which, 2 * s + t))
                for b in range(4):
                    q = turn_bank(layer, which, s, b)
                    claim(q)
                    for kk in range(2):
                        for t in range(2):
                            k = 2 * b + kk
                            ins = pe.transpose(ps[:, q, kk * 256 + t * P:kk * 256 + t * P + P],
                                               xn[which][:, 2 * s + t, k * P:(k + 1) * P], ident[:])
                    full(ins, q, "mod_x", layer, which, s)

            def chunk(g, j):
                layer = g.layer
                if g.pair and j == g.n - 2:
                    return
                js = (j - 1, j) if g.pair and j == g.n - 1 else (j,)
                assert g.at[j] - g.at[js[0]] == len(js) - 1
                pe.wait_ge(sem("lo_ready"), g.at[j] + 1)
                if g.kind == "a_q":
                    pe.wait_ge(sem("h_ready"), at("h_ready", layer, 0, 1, j))
                if g.kind == "a_k" and layer == DEPTH - 1:
                    pe.wait_ge(sem("h_ready"), at("h_ready", layer, 0, 0, j))
                if g.kind == "branch" and g.index[0] == 0:
                    pe.wait_ge(sem("ys_ready"), at("ys_ready", layer, g.index[1], 2 * j + 1))
                if g.kind == "out" and g.index == 0:
                    pe.wait_ge(sem("merged"), at("merged", layer, 2 * j + 1))
                if g.kind == "down" and g.index == 0:
                    pe.wait_ge(sem("act_lo"), at("act_lo", "base", "end", layer) - FT + 2 * j + 2)
                t0 = tok0(layer)
                if g.kind == "a_k" or g.kind == "a_v" or g.kind == "g_v" or g.kind == "z":
                    t0 = 0
                for n, j in [(n, j) for n in g.tiles for j in js]:
                    c, b = g.at[j], g.bank0 + n
                    s = c % NBUF
                    if g.turn == "A":
                        ins = ada_chunk(g, j, c)
                    elif j == 0:
                        claim(b)
                    if g.turn == "Z":
                        for k in range(KT):
                            ins = three(ps[:, 0, :], w_hi[:, s, k * P:(k + 1) * P], w_lo[:, s, k * P:(k + 1) * P],
                                        h_hi[:, k, :], h_lo[:, k, :], k == 0, k == KT - 1)
                    for kk in range(2 if g.turn not in "AZ" else 0):
                        k = 2 * j + kk
                        first, last = k == 0, k == 2 * g.n - 1
                        if g.turn in "FB":
                            lo_t = 0 if g.kind == "g_qk" and n >= 2 else t0
                            xh, xl = (h_hi, h_lo) if g.turn == "F" else (ys_hi, ys_lo)
                            kx = k if g.turn == "F" else ys_at[g.index[1]] + k
                            cs = slice(kk * 512 + n * P, kk * 512 + n * P + P)
                            ins = three(ps[:, b, lo_t:TOK], w_hi[:, s, cs], w_lo[:, s, cs],
                                        xh[:, kx, lo_t:TOK], xl[:, kx, lo_t:TOK], first, last)
                        else:
                            xh, xl = (act_hi, act_lo) if g.turn == "D" else (h_hi, h_lo)
                            ts_, cs = slice(n * P, n * P + P), slice(kk * 512, kk * 512 + 512)
                            ins = three(ps[:, b, :], xh[:, k, ts_], xl[:, k, ts_], w_hi[:, s, cs], w_lo[:, s, cs], first, last)
                    if j == g.n - 1:
                        full(ins, b, *g.key)
                        owed[0] = n == g.tiles[-1]
                    elif n == g.tiles[-1]:
                        ins.then_inc(sem("chunk_used"), 1)

            def qk_turn(layer, w):
                for tt in (q_tiles(layer) if w == 0 else range(4)):
                    if tt < 2:
                        pe.wait_ge(sem(f"bank_free{tt}"), at(f"bank_full{tt}", "a_k" if w else "a_q", layer, 0))
                    else:
                        pe.wait_ge(sem("qk_ready"), at("qk_ready", layer, w, tt))
                    b = 4 + tt
                    claim(b)
                    for h in range(HEADS):
                        ins = pe.transpose(ps[:, b, h * P:(h + 1) * P], qk_tok[:, tt, h * P:(h + 1) * P], ident[:])
                    full(ins, b, "qk", layer, w, tt)

            def filter_(layer, i):
                if i == 0:
                    claim(4)
                    full(mm(ps[0:64, 4, 0:256], f_w1[:], feat[:]), 4, "filter", layer, 0)
                if i == 1:
                    pe.wait_ge(sem("f_sin"), at("f_sin", layer, 0))
                    claim(4)
                    full(mm(ps[0:64, 4, 0:256], f_w2[:], f_h[:, 0, :]), 4, "filter", layer, 1)
                if i == 2:
                    pe.wait_ge(sem("f_sin"), at("f_sin", layer, 1))
                    for t in range(2):
                        for d in range(2):
                            claim(4 + 2 * t + d)
                            full(mm(ps[:, 4 + 2 * t + d, :], f_h[:, 1, t * P:(t + 1) * P], f_w3[:, d, :]),
                                 4 + 2 * t + d, "filter", layer, 2)
                if i == 3:
                    pe.wait_ge(sem("f_sd"), at("f_sd", layer, 1))
                    for cs in range(2):
                        for kt in range(2):
                            b = 4 + 2 * cs + kt
                            claim(b)
                            for t in range(2):
                                ins = mm(ps[:, b, :], dft[:, cs, t, kt * P:(kt + 1) * P], f_sd[:, cs, t, :], start=t == 0, stop=t == 1)
                            full(ins, b, "filter", layer, 3)

            def units(layer):
                return [(tt, h) for tt in q_tiles(layer) for h in range(HEADS)]

            def attend(layer, i, n_u):
                us = units(layer)
                if i < n_u:
                    tt, h = us[i]
                    nk = SEQ if tt < 2 else TOK
                    if i == 0:
                        pe.wait_ge(sem("bank_free7"), at("bank_full7", "qk", layer, 1, 3))
                        pe.wait_ge(sem("bank_free3"), at("bank_full3", "a_v", layer, 0))
                    for m in range(2):
                        claim(4 + m)
                        full(mm(ps[:, 4 + m, 0:nk], qT[64 * m:64 * m + 64, h, tt * P:(tt + 1) * P],
                                kT[64 * m:64 * m + 64, h, 0:nk]), 4 + m, "scores", layer, i)
                if 1 <= i <= n_u:
                    tt, h = us[i - 1]
                    nk = SEQ if tt < 2 else TOK
                    pe.wait_ge(sem("diff"), at("diff", layer, i - 1))
                    claim(6)
                    for kb in range(nk // P):
                        ins = pe.transpose(ps[:, 6, kb * P:(kb + 1) * P], probs[:, (i - 1) % 2, 0, kb * P:(kb + 1) * P], ident[:])
                    full(ins, 6, "attT", layer, i - 1)
                if i >= 2:
                    tt, h = us[i - 2]
                    nk = SEQ if tt < 2 else TOK
                    pe.wait_ge(sem("bank_free6"), at("bank_full6", "attT", layer, i - 2))
                    if h == 0:
                        claim(7)
                    for kb in range(nk // P):
                        ins = mm(ps[:, 7, h * P:(h + 1) * P], attT[:, i % 2, kb * P:(kb + 1) * P],
                                 v_tok[:, kb, h * P:(h + 1) * P], start=kb == 0, stop=kb == nk // P - 1)
                    if h == HEADS - 1:
                        full(ins, 7, "o", layer, tt)

            def y_turn(layer, br, tt):
                pe.wait_ge(sem("y_tok"), at("y_tok", layer, br, tt))
                src = y_tok[:] if br == 0 else go[:, tt, :]
                claim(6)
                for c in range(CT):
                    ins = pe.transpose(ps[:, 6, c * P:(c + 1) * P], src[:, c * P:(c + 1) * P], ident[:])
                full(ins, 6, "y", layer, br, tt)

            def hy_turn(layer, s):
                pe.wait_ge(sem("u_ready"), at("u_ready", layer, CT - 1))
                for t in range(2):
                    claim(4 + t)
                    for c in range(CT):
                        o = s * SEQ + t * P
                        ins = pe.transpose(ps[:, 4 + t, c * P:(c + 1) * P], uT[:, c, o:o + P], ident[:])
                    full(ins, 4 + t, "u", layer, s)

            def hy_dft(layer, s):
                for t in range(2):
                    pe.wait_ge(sem(f"bank_free{4 + t}"), at(f"bank_full{4 + t}", "u", layer, s))
                for kt in range(2):
                    for cs in range(2):
                        b = 4 + 2 * kt + cs
                        claim(b)
                        for t in range(2):
                            ins = mm(ps[:, b, :], dft[:, cs, t, kt * P:(kt + 1) * P], u_tok[:, t, :], start=t == 0, stop=t == 1)
                        full(ins, b, "U", layer, s)

            def hy_idft(layer, s):
                pe.wait_ge(sem("spec"), at("spec", layer, s, 1))
                for c in range(CT):
                    b = 4 + c // 2
                    if c % 2 == 0:
                        claim(b)
                    n = 0
                    for kt in range(2):
                        for cs in range(2):
                            ins = mm(ps[:, b, (c % 2) * 256:(c % 2) * 256 + 256], spec[:, cs, kt, c * P:(c + 1) * P],
                                     idft[:, cs, kt, :], start=n == 0, stop=n == 3)
                            n += 1
                    if c % 2:
                        full(ins, b, "conv", layer, s)

            def gla_gate(layer, tt):
                if tt == 0:
                    pe.wait_ge(sem("bank_free0"), at("bank_full0", "z", layer, 0))
                    pe.wait_ge(sem("z_one"), at("z_one", layer))
                    pe.wait_ge(sem("bank_free3"), at("bank_full3", "g_qk", layer, 0))
                claim(4)
                full(mm(ps[:, 4, :], zT[0:33, tt * P:(tt + 1) * P], w_gate[0:33, :]), 4, "logit", layer, tt)
                claim(5)
                for p_ in range(2):
                    ins = pe.transpose(ps[:, 5, p_ * P:(p_ + 1) * P], gqk[:, 2 + p_, tt * P:(tt + 1) * P], ident[:])
                full(ins, 5, "ktok", layer, tt)

            def gla_sum(layer, tt):
                pe.wait_ge(sem("bank_free4"), at("bank_full4", "logit", layer, tt))
                for d in range(2):
                    claim(6 + d)
                    for p_ in range(2):
                        ins = mm(ps[:, 6 + d, p_ * 256:p_ * 256 + 256], la[:, (2 * d + p_) * P:(2 * d + p_ + 1) * P], cums[:, d, :])
                    full(ins, 6 + d, "b", layer, tt)
                claim(4)
                for d in range(2):
                    ins = mm(ps[:, 4, d * 256:d * 256 + 256], tail[:, d, :], la[:, d * 256:d * 256 + 256])
                full(ins, 4, "tail", layer, tt)

            def gla_att(layer, tt):
                pe.wait_ge(sem("qke"), at("qke", layer, tt))
                for r in range(2):
                    claim(6 + r)
                    rs = slice(64 * r, 64 * r + 64)
                    for n in range(4):
                        ins = mm(ps[:, 6 + r, n * P:(n + 1) * P], ke[rs, n, :], qe[rs, n, :])
                    full(ins, 6 + r, "att", layer, tt)

            def gla_state(layer, tt):
                pe.wait_ge(sem("ku"), at("ku", layer, tt))
                if tt == 0:
                    pe.wait_ge(sem("bank_free3"), at("bank_full3", "g_v", layer, 0))
                for j in range(2):
                    claim(4 + j)
                    r = slice(64 * j, 64 * j + 64)
                    for d in range(2):
                        for h in range(HEADS):
                            o, p_ = (h % 2) * 64, h // 2
                            ins = mm(ps[o:o + 64, 4 + j, (2 * d + p_) * P:(2 * d + p_ + 1) * P], ku[r, d, h * 64:h * 64 + 64],
                                     gv[r, tt, h * P:(h + 1) * P])
                    full(ins, 4 + j, "u_state", layer, tt)
                if tt in q_tiles(layer):
                    pe.wait_ge(sem("bank_free7"), at("bank_full7", "att", layer, tt))
                    claim(6)
                    for h in range(HEADS):
                        for d in range(2):
                            ins = mm(ps[:, 6, h * P:(h + 1) * P], att[:, h % 2, 2 * d + h // 2, :], gv[:, tt, h * P:(h + 1) * P],
                                     start=d == 0, stop=d == 1)
                    full(ins, 6, "intra", layer, tt)

            def gla_out(layer, tt):
                if tt == q_tiles(layer)[0]:
                    pe.wait_ge(sem("scanned"), at("scanned", layer))
                for r in range(2):
                    claim(4 + r)
                    rs = slice(64 * r, 64 * r + 64)
                    for j in range(2):
                        c = 2 * tt + j
                        ns = [c, (3 - c) if c < 4 else (11 - c)]
                        ds_ = [d for d in range(2) if ns[d] > 0]
                        for p_ in range(2):
                            for d in ds_:
                                ins = mm(ps[64 * j:64 * j + 64, 4 + r, p_ * P:(p_ + 1) * P],
                                         gqk[rs, 2 * d + p_, tt * P + 64 * j:tt * P + 64 * j + 64], states[rs, d, ns[d] - 1, p_, :],
                                         start=d == ds_[0], stop=d == ds_[-1])
                    full(ins, 4 + r, "inter", layer, tt)

            def up(layer, c0):
                u = list(used)
                t0 = tok0(layer)
                for b in range(8):
                    C.base(f"bank_full{b}", "up", layer)

                def up_group(i, h):
                    for j in range(4):
                        c = c0 + 4 * h + j
                        s = c % NBUF
                        pe.wait_ge(sem("lo_ready"), i * 8 + (c + 1))
                        pe.wait_ge(sem("h_ready"), at("h_ready", layer, 1, 1, j))
                        for n in range(4):
                            b = 4 * h + n
                            if j == 0:
                                pe.wait_ge(sem(f"bank_free{b}"), i + u[b])
                            for kk in range(2):
                                k = 2 * j + kk
                                cs = slice(kk * 512 + n * P, kk * 512 + n * P + P)
                                ins = three(ps[:, b, t0:TOK], w_hi[:, s, cs], w_lo[:, s, cs],
                                            h_hi[:, k, t0:TOK], h_lo[:, k, t0:TOK], k == 0, k == KT - 1)
                            if j == 3:
                                ins.then_inc(sem(f"bank_full{b}"), 1)
                        if j < 3:
                            ins.then_inc(sem("chunk_used"), 1)
                        else:
                            owed[0] = True

                with pe.Fori(0, UP_GROUPS // 2) as i:
                    for h in range(2):
                        up_group(i, h)
                up_group(UP_GROUPS // 2, 0)
                for b in range(8):
                    n = UP_GROUPS // 2 + (1 if b < 4 else 0)
                    used[b] += n
                    C.skip(f"bank_full{b}", n)
                C.base("bank_full3", "up end", layer)

            fns = dict(start=start, params_turn=params_turn, modcols=modcols, turn=turn, chunk=chunk,
                       qk_turn=qk_turn, filter=filter_, attend=attend, y_turn=y_turn, hy_turn=hy_turn, hy_dft=hy_dft,
                       hy_idft=hy_idft, gla_gate=gla_gate, gla_sum=gla_sum, gla_att=gla_att, gla_state=gla_state,
                       gla_out=gla_out, up=up)
            for st in steps:
                if st[0] in fns:
                    fns[st[0]](*st[1:])

        @block.scalar
        def _(act):
            cursor = [0]

            def split(c):
                s = c % NBUF
                act.wait_ge(sem(f"landed{s}"), 32 * (c // NBUF + 1))
                if c >= NBUF:
                    act.wait_ge(sem("chunk_used"), c - NBUF + 2)
                act.activation(w_hi[:, s, :], stage[:, s, :], ACT.Copy).then_inc(sem("hi_ready"), 1)

            def split_to(c):
                while cursor[0] < min(c, n_chunks):
                    split(cursor[0])
                    cursor[0] += 1

            def bank(b, *who):
                act.wait_ge(sem(f"bank_full{b}"), at(f"bank_full{b}", *who))

            def do(ins, stage_, *who):
                ins.then_inc(sem(stage_), tick(stage_, *who))

            def free(ins, b):
                ins.then_inc(sem(f"bank_free{b}"), 1)

            def freed(b, *who):
                act.wait_ge(sem(f"bank_free{b}"), at(f"bank_full{b}", *who))

            def start():
                bank(4, "c")
                free(act.activation(c_act[:], ps[:, 4, 0:16], ACT.Silu), 4)
                freed(4, "c")
                act.wait_ge(sem("ada_zero"), 1)
                act.activation(ada_c[:, :, 0:2].rearrange("p k v -> p v k"),
                               c_act[:].rearrange("p (v k) -> p v k", v=2), ACT.Copy).then_inc(sem("ada_hi"), 1)
                split_to(AHEAD)
                for tt in range(4):
                    src = (A["ctx"] if tt < 2 else A["x"])[0, (tt % 2) * P:(tt % 2 + 1) * P, :]
                    act.dma_start(x_tok[:, tt, :], src).then_inc(sem("x_in"), 16)

            def params_turn(layer):
                bank(4, "params", layer)
                act.activation(pcol[:], ps[:, 4, 0:228], ACT.Copy).then_inc(sem("bank_free4"), 1)
                act.wait_ge(sem("lam_dot"), at("lam_dot", layer))
                do(act.activation(lam[:, 2:4], lam[:, 0:2], ACT.Exp), "lam_exp", layer)



            def modcols(layer, part):
                n = 32 if part == 0 else 64
                b = mod_bank(layer, part)
                bank(b, "mod", layer, part)
                dst = (mod_a if part == 0 else mod_b)[:].rearrange("p v w k -> p (v w k)")
                free(act.activation(dst, ps[:, b, 0:n], ACT.Copy), b)

            def deviation(layer, which, tt):
                if act_moments(layer, which, tt):
                    m, x = moms[:, 4 + tt, :], x_tok[:, tt, :]
                    act.wait_ge(sem("post_x"), at("post_x", layer if which else layer - 1, 0 if which else 1, tt))
                    do(act.activation(xn[which][:, tt, :], x, ACT.Identity, scale=-1.0 / D, accum_out=m[:, 4:5]), "act_mean", layer, which, tt)
                    act.wait_ge(sem("act_mean"), at("act_mean", layer, which, tt))
                    do(act.activation(xn[which][:, tt, :], x, ACT.Square, bias=m[:, 4:5], accum_out=m[:, 1:2]), "act_var", layer, which, tt)
                    act.wait_ge(sem("act_var"), at("act_var", layer, which, tt))
                    do(act.activation(m[:, 3:4], m[:, 1:2], ACT.Sqrt, scale=1.0 / D, bias=eps_col[:]), "ln_std", layer, which, tt)
                    return
                act.wait_ge(sem("ln_var"), at("ln_var", layer, which, tt))
                do(act.activation(moms[:, 4 + tt, 3:4], moms[:, 4 + tt, 2:3], ACT.Sqrt), "ln_std", layer, which, tt)

            def normal(layer, which, tt):
                act.wait_ge(sem("ln_scale"), at("ln_scale", layer, which, tt))
                do(act.activation(xn[which][:, tt, :], x_tok[:, tt, :], ACT.Identity, bias=moms[:, 4 + tt, 4:5],
                                  scale=moms[:, 4 + tt, 2:3]), "ln_x", layer, which, tt)

            def modulate(layer, which, s, b):
                v, q = 1 - s, turn_bank(layer, which, s, b)
                act.wait_ge(sem("mod_cols"), at("mod_cols", layer, which))
                bank(q, "mod_x", layer, which, s)
                n = at("h_ready", layer, which, s, b)
                if n > 2:
                    act.wait_ge(sem("h_ready"), n - 2)
                for kk in range(2):
                    k = 2 * b + kk
                    sc = mod_a[:, v, 1, k:k + 1] if which == 0 else mod_b[:, v, 2, k:k + 1]
                    sh = mod_a[:, v, 0, k:k + 1] if which == 0 else mod_b[:, v, 1, k:k + 1]
                    ins = act.activation(xm[:, n % 2 * 2 + kk, :], ps[:, q, kk * 256:kk * 256 + 256], ACT.Identity,
                                         bias=sh, scale=sc)
                free(ins, q)

            def chunk(g, j):
                split_to(g.at[j] + AHEAD + (0 if g.late and j == g.n - 1 else 1))

            def evac(g):
                layer, kind = g.layer, g.kind
                t0 = tok0(layer)
                if kind == "ada":
                    b, i, q = g.index % 2, g.index, g.bank0 + g.index % 2
                    if (layer, i) == (0, ADA_GROUPS[1][0]):
                        freed(7, "U", layer, 1)
                    if (layer, i) == (1, 0):
                        act.wait_ge(sem("act_lo"), at("act_lo", "base", "end", 0))
                    if (layer, i) > (0, 1):
                        before = (layer, i - 2) if i >= 2 else (layer - 1, i + 10)
                        act.wait_ge(sem(f"mod_out{b}"), 16 * at(f"mod_out{b}", *before))
                    bank(q, *g.key)
                    free(act.activation(mod_row[:, b, :], ps[0:4, q, :], ACT.Copy), q)
                if kind in ("out", "down") and g.index == 1:
                    which = 0 if kind == "out" else 1
                    for tt in g.tiles:
                        act.wait_ge(sem("post_var"), at("post_var", layer, which, tt))
                        do(act.activation(moms[:, tt, 3:4], moms[:, tt, 2:3], ACT.Sqrt), "post_std", layer, which, tt)
                if kind in ("a_q", "a_k"):
                    w = 0 if kind == "a_q" else 1
                    for tt in g.tiles:
                        if tt < 2:
                            if w == 1:
                                if layer < DEPTH - 1:
                                    act.wait_ge(sem(f"bank_full{4 + tt}"), at(f"bank_full{4 + tt}", "qk", layer, 0, tt))
                            bank(tt, *g.key)
                            free(act.activation(qk_tok[:, tt, :], ps[:, tt, :], ACT.Copy), tt)
                if kind == "a_v":
                    for tt in g.tiles:
                        bank(tt, *g.key)
                        free(act.activation(v_tok[:, tt, :], ps[:, tt, :], ACT.Copy), tt)
                if kind == "hy":
                    part = g.index
                    if part == 0:
                        freed(7, "filter", layer, 3)
                    for n in range(4):
                        t = 4 * part + n
                        bank(n, *g.key)
                        if part == 2 and n >= 2:
                            act.wait_ge(sem("u_ready"), at("u_ready", layer, n - 2))
                        dst = (x0T, uT, vvT)[part][:, n % 2 if part == 2 else n, t0:TOK]
                        do(act.activation(dst, ps[:, n, t0:TOK], ACT.Identity, bias=pcol[:, 36 + t:37 + t],
                                          scale=pcol[:, 12 + t:13 + t]), "conv_mid", layer, part, n)
                if kind == "g_v":
                    for tt in g.tiles:
                        bank(tt, *g.key)
                        free(act.activation(gv[:, tt, :], ps[:, tt, :], ACT.Copy), tt)
                if kind == "g_qk":
                    act.wait_ge(sem("bank_full6"), at("bank_full6", "y", layer, 0, 3))
                    for n in range(4):
                        bank(n, *g.key)
                        lo_t = 0 if n >= 2 else t0
                        free(act.activation(gqk[:, n, lo_t:TOK], ps[:, n, lo_t:TOK], ACT.Copy, scale=0.125 if n < 2 else 1.0), n)
                if kind == "z":
                    bank(0, *g.key)
                    free(act.activation(zT[0:32, :], ps[0:32, 0, :], ACT.Copy), 0)
                if kind == "gate":
                    for j in range(4):
                        bank(j, *g.key)
                        if (g.index, j) >= (0, 2):
                            n = 4 * g.index + j - 2
                            act.wait_ge(sem(f"sig_out{j % 2}"), 16 * at(f"sig_out{j % 2}", layer, n // 4, n % 4))
                        free(act.activation(sig[:, j % 2, t0:TOK], ps[:, j, t0:TOK], ACT.Sigmoid), j)
                if kind == "g_r":
                    for n, tt in enumerate(g.tiles):
                        bank(tt, *g.key)
                        if n >= 2:
                            act.wait_ge(sem("y_tok"), at("y_tok", layer, 1, tt - 2))
                        free(act.activation(rg[:, tt % 2, :], ps[:, tt, :], ACT.Silu), tt)
                if kind == "branch":
                    half, br = g.index
                    if br == 2:
                        for n in range(4):
                            act.wait_ge(sem("gated"), at("gated", layer, g.index, n))
                            do(act.activation(h_hi[:, 4 * half + n, t0:TOK], acc[:, n, t0:TOK], ACT.Copy), "merged_hi", layer, 4 * half + n)

            def qk_turn(layer, w):
                for tt in (q_tiles(layer) if w == 0 else range(4)):
                    b = 4 + tt
                    bank(b, "qk", layer, w, tt)
                    dst = (qT if w == 0 else kT)[:, :, tt * P:(tt + 1) * P]
                    if layer:
                            act.wait_ge(sem("x_out"), 16 * at("x_out", layer - 1, 1, 3))
                    free(act.activation(dst, ps[:, b, :].rearrange("p (h t) -> p h t", h=HEADS), ACT.Copy), b)

            def filter_(layer, i):
                if i < 2:
                    act.wait_ge(sem("f_arg"), at("f_arg", layer, i))
                    do(act.activation(f_h[:, i, :], f_arg[:, 0, :], ACT.Sin), "f_sin", layer, i)
                if i == 3:
                    for b in range(2):
                        act.wait_ge(sem(f"mod_out{b}"), 16 * at(f"mod_out{b}", layer, ADA_GROUPS[1 if layer else 0][-2 + b]))
                    for cs in range(2):
                        for kt in range(2):
                            b = 4 + 2 * cs + kt
                            bank(b, "filter", layer, 3)
                            free(act.activation(filt[:, cs, kt, :], ps[:, b, :], ACT.Copy), b)

            def attend(layer, i, n_u):
                us = [(tt, h) for tt in q_tiles(layer) for h in range(HEADS)]
                if i < n_u:
                    nk = SEQ if us[i][0] < 2 else TOK
                    act.wait_ge(sem("neg_max"), at("neg_max", layer, i))
                    for m in range(2):
                        free(act.activation(probs[:, i % 2, m, 0:nk], ps[:, 4 + m, 0:nk], ACT.Exp, bias=soft[:, i % 2, 2 + m:3 + m],
                                            scale=0.125, accum_out=soft[:, i % 2, 4 + m:5 + m]), 4 + m)
                if 1 <= i <= n_u:
                    nk = SEQ if us[i - 1][0] < 2 else TOK
                    bank(6, "attT", layer, i - 1)
                    free(act.activation(attT[:, (i - 1) % 2, 0:nk], ps[:, 6, 0:nk], ACT.Copy), 6)

            def head_norm(layer, tt):
                bank(7, "o", layer, tt)
                do(act.activation(o_sq[:], ps[:, 7, :], ACT.Square), "o_sq", layer, tt)
                act.wait_ge(sem("hn_var"), at("hn_var", layer, 0, tt))
                do(act.activation(hn[:, 1, :], hn[:, 0, :], ACT.Sqrt), "hn_std", layer, 0, tt)

            def y_turn(layer, br, tt):
                bank(6, "y", layer, br, tt)
                free(act.activation(y[:, br, :, tt * P:(tt + 1) * P], ps[:, 6, :].rearrange("p (c t) -> p c t", c=CT), ACT.Copy), 6)

            def hy_turn(layer, s):
                for t in range(2):
                    bank(4 + t, "u", layer, s)
                    free(act.activation(u_tok[:, t, :], ps[:, 4 + t, :], ACT.Copy), 4 + t)

            def gla_gate(layer, tt):
                if tt == 0:
                    act.wait_ge(sem("y_hyena"), at("y_hyena", layer, 1, CT - 1))
                else:
                    freed(4, "logit", layer, tt - 1)
                bank(4, "logit", layer, tt)
                do(act.activation(lg[:], ps[:, 4, :], ACT.Abs), "lg_abs", layer, tt)
                act.wait_ge(sem("lg_abs"), at("lg_abs", layer, tt))
                do(act.activation(lg[:], lg[:], ACT.Exp, scale=-1.0), "lg_exp", layer, tt)
                act.wait_ge(sem("lg_exp"), at("lg_exp", layer, tt))
                do(act.activation(lg[:], lg[:], ACT.Ln, bias=1.0), "lg", layer, tt)
                bank(5, "ktok", layer, tt)
                if tt > 0:
                    act.wait_ge(sem("ku"), at("ku", layer, tt - 1))
                free(act.activation(ktok[:], ps[:, 5, 0:256], ACT.Copy), 5)

            def gla_sum(layer, tt):
                for d in range(2):
                    bank(6 + d, "b", layer, tt)
                src = ps[:, 6:8, :].rearrange("p d (a b t) -> p (d a) b t", a=2, b=2)
                if tt > 0:
                    act.wait_ge(sem("ku"), at("ku", layer, tt - 1))
                    act.wait_ge(sem("dec"), at("dec", layer, tt - 1, 1))
                    if tt - 1 in q_tiles(layer):
                        act.wait_ge(sem("qke"), at("qke", layer, tt - 1))
                ins = act.activation(eb[:, 0, :, :], src[:, :, 0, :], ACT.Exp)
                if tt in q_tiles(layer):
                    act.activation(eb[:, 1, :, :], src[:, :, 1, :], ACT.Exp)
                    ins = act.activation(eb[:, 2, :, :], src[:, :, 1, :], ACT.Exp, scale=-1.0)
                free(ins, 6)
                bank(4, "tail", layer, tt)
                for d, b in ((0, 7), (1, 4)):
                    free(act.activation(etail[:, d, :], ps[:, 4, d * 256:d * 256 + 256], ACT.Exp), b)

            def gla_state(layer, tt):
                for j in range(2):
                    bank(4 + j, "u_state", layer, tt)
                    slots = [((2 * tt + j) if d == 0 else (3 if tt < 2 else 11) - 2 * tt - j, d) for d in range(2)]
                    for n, d in [x for x in slots if x[0] < 7]:
                        ins = act.activation(states[:, d, n, :, :].rearrange("p a v -> p (a v)"),
                                             ps[:, 4 + j, 256 * d:256 * d + 256], ACT.Copy)
                    free(ins, 4 + j)
                if tt in q_tiles(layer):
                    bank(6, "intra", layer, tt)
                    free(act.activation(go[:, tt, :], ps[:, 6, :], ACT.Copy), 6)

            def gla_out(layer, tt):
                freed(5, "inter", layer, tt)
                do(act.activation(g_sq[:], go[:, tt, :], ACT.Square), "g_sq", layer, tt)
                act.wait_ge(sem("hn_var"), at("hn_var", layer, 1, tt))
                do(act.activation(hn[:, 1, :], hn[:, 0, :], ACT.Sqrt), "hn_std", layer, 1, tt)

            def y_split(layer, br):
                t0 = tok0(layer)
                if br < 2:
                    freed(6, "y", layer, br, 3)
                else:
                    act.wait_ge(sem("y_hyena"), at("y_hyena", layer, 1, CT - 1))
                freed(5, "inter", layer, 3)
                for n in range(CT):
                    do(act.activation(ys_hi[:, ys_at[br] + n, t0:TOK], y[:, br, n, t0:TOK], ACT.Copy), "ys_hi", layer, br, n)

            def up(layer, c0):
                split_to(c0 + AHEAD)
                t0 = tok0(layer)
                W0, W1, W2, B = 52, 52 + 44, 140, 184
                e0 = C.base("up_mid", layer)
                b0 = [at(f"bank_full{b}", "base", "up", layer) for b in range(8)]
                l0 = at("act_lo", "base", layer)
                p0 = at("up_prod", "base", layer)
                n_groups = UP_GROUPS
                C.base("up_gelu", layer)
                C.base("act_hi", layer)
                act.wait_ge(sem("x_out"), 16 * at("x_out", layer, 0, 3))
                def up_group(i, h):
                    for j in range(4):
                        c = c0 + AHEAD + 4 * h + j
                        s = c % NBUF
                        act.wait_ge(sem(f"landed{s}"), i * 64 + 32 * (c // NBUF + 1))
                        act.wait_ge(sem("chunk_used"), i * 8 + (c - NBUF + 2))
                        act.activation(w_hi[:, s, :], stage[:, s, :], ACT.Copy).then_inc(sem("hi_ready"), 1)
                    for p_ in range(2):
                        act.wait_ge(sem("act_lo"), i * 4 + (l0 + 2 * h + p_ - 1))
                        for a in range(2):
                            b = 4 * h + 2 * a + p_
                            act.wait_ge(sem(f"bank_full{b}"), i + (b0[b] + 1))
                            act.activation(ffn_t[:, p_, a, t0:TOK], ps[:, b, t0:TOK], ACT.Identity,
                                           bias=pcol[:, bass.ds(i * 4 + (B + 22 * a + 2 * h + p_), 1)],
                                           scale=pcol[:, bass.ds(i * 4 + (W1 + 22 * a + 2 * h + p_), 1)]).then_inc(sem("up_mid"), 1)
                    for p_ in range(2):
                        b = 4 * h + 2 + p_
                        act.wait_ge(sem(f"bank_free{b}"), i + (b0[b] + 1))
                        act.activation(ffn_t[:, p_, 1, t0:TOK], ffn_t[:, p_, 1, t0:TOK], ACT.Gelu_apprx_tanh).then_inc(sem("up_gelu"), 1)
                    for p_ in range(2):
                        act.wait_ge(sem("up_prod"), i * 4 + (p0 + 2 * h + p_ + 1))
                        act.activation(act_hi[:, bass.ds(i * 4 + (2 * h + p_), 1), t0:TOK].rearrange("p a t -> p (a t)"),
                                       ffn_t[:, p_, 0, t0:TOK], ACT.Copy).then_inc(sem("act_hi"), 1)

                with act.Fori(0, UP_GROUPS // 2) as i:
                    for h in range(2):
                        up_group(i, h)
                up_group(UP_GROUPS // 2, 0)
                C.skip("up_mid", 4 * n_groups)
                C.skip("up_gelu", 2 * n_groups)
                C.skip("act_hi", 2 * n_groups)
                C.place[("act_hi", "end", layer)] = C.seen["act_hi"]
                cursor[0] += 4 * n_groups

            fns = dict(start=start, params_turn=params_turn, modcols=modcols, deviation=deviation, normal=normal,
                       modulate=modulate, chunk=chunk, evac=evac, qk_turn=qk_turn, filter=filter_, attend=attend, head_norm=head_norm, y_turn=y_turn,
                       hy_turn=hy_turn, gla_gate=gla_gate, gla_sum=gla_sum, gla_state=gla_state, gla_out=gla_out, y_split=y_split,
                       up=up)
            for st in steps:
                if st[0] in fns:
                    fns[st[0]](*st[1:])

        @block.vector
        def _(dve):
            cursor, chain = [0], [0]

            def link(ins):
                chain[0] += 1
                ins.then_inc(sem("dve_chain"), 1)
                dve.wait_ge(sem("dve_chain"), chain[0])

            def split(c):
                s = c % NBUF
                dve.wait_ge(sem("hi_ready"), c + 1)
                dve.tensor_tensor(w_lo[:, s, :], stage[:, s, :], w_hi[:, s, :].bitcast(F32), ALU.subtract)\
                   .then_inc(sem("lo_ready"), 1)

            def split_to(c):
                while cursor[0] < min(c, n_chunks):
                    split(cursor[0])
                    cursor[0] += 1

            def bank(b, *who):
                dve.wait_ge(sem(f"bank_full{b}"), at(f"bank_full{b}", *who))

            def freed(b, *who):
                dve.wait_ge(sem(f"bank_free{b}"), at(f"bank_full{b}", *who))

            def do(ins, stage_, *who):
                ins.then_inc(sem(stage_), tick(stage_, *who))

            def done(stage_, *who):
                dve.wait_ge(sem(stage_), at(stage_, *who))

            def free(ins, b):
                ins.then_inc(sem(f"bank_free{b}"), 1)

            def wide(ap, n, axis=1):
                a = ap.unsqueeze(axis)
                shape = list(a.shape)
                shape[axis] = n
                return a.broadcast_to(shape)

            def start():

                dve.memset(eps_col[:], EPS)
                dve.memset(ada_c[:].bitcast(F32), 0.0).then_inc(sem("ada_zero"), 1)
                dve.wait_ge(sem("ada_hi"), 1)
                dve.tensor_tensor(ada_c[:, :, 2:4].rearrange("p k v -> p v k"), c_act[:].rearrange("p (v k) -> p v k", v=2),
                                  ada_c[:, :, 0:2].rearrange("p k v -> p v k").bitcast(F32), ALU.subtract).then_inc(sem("ada_lo"), 1)
                split_to(AHEAD)

            def params_turn(layer):
                lam_init = 0.8 - 0.6 * math.exp(-0.3 * layer)
                dve.wait_ge(sem("params_in"), 16 * at("params_in", layer, "last"))
                dve.wait_ge(sem("consts_in"), 6 * 16)
                lv = lam_in[:].rearrange("p (a b) n -> p a b n", b=2)
                link(dve.tensor_tensor(lam_prod[:], lv[:, :, 0, :], lv[:, :, 1, :], ALU.mult))
                do(dve.tensor_reduce(lam[:, 0:2], lam_prod[:], AX_X, ALU.add), "lam_dot", layer)
                done("lam_exp", layer)
                link(dve.tensor_tensor(lam[:, 4:5], lam[:, 3:4], lam[:, 2:3], ALU.subtract))
                link(dve.tensor_scalar(lam[:, 5:6], lam[:, 4:5], -lam_init, None, ALU.add))
                link(dve.tensor_scalar(da_g[:], da_g[:], 1.0 - lam_init, None, ALU.mult))



            def modcols(layer, part):
                n = 32 if part == 0 else 64
                dve.wait_ge(sem("mod_in"), 16 * at("mod_in", layer, part, 1))
                link(dve.tensor_tensor(mrows[0:n, 0, :], mrows[0:n, 0, :], mrows[0:n, 1, :], ALU.add))
                do(dve.tensor_tensor(mrows[0:n, 0, :], mrows[0:n, 0, :], mrows[0:n, 2, :], ALU.add), "mod_sum", layer, part)
                freed(mod_bank(layer, part), "mod", layer, part)
                col = mod_a[:, :, 1, :] if part == 0 else mod_b[:, :, 2, :]
                do(dve.tensor_scalar(col, col, 1.0, None, ALU.add), "mod_cols", layer, part)

            def half_moments(src, m, half):
                return dve.bn_stats(stat[:, m, 6 * half:6 * half + 6], src[:, half * 512:half * 512 + 512])

            def whole_moments(m):
                link(dve.bn_aggr(moms[:, m, 0:2], stat[:, m, :]))
                return dve.tensor_scalar(moms[:, m, 2:3], moms[:, m, 1:2], EPS, None, ALU.add)

            def moments(layer, which, tt):
                if act_moments(layer, which, tt):
                    return
                if (layer, which, tt) == (0, 0, 0):
                    dve.wait_ge(sem("x_in"), 64)
                half_moments(x_tok[:, tt, :], 4 + tt, 0)
                link(half_moments(x_tok[:, tt, :], 4 + tt, 1))
                do(whole_moments(4 + tt), "ln_var", layer, which, tt)

            def normal(layer, which, tt):
                done("ln_std", layer, which, tt)
                m = moms[:, 4 + tt, :]
                link(dve.reciprocal(m[:, 2:3], m[:, 3:4]))
                mean, sign = (m[:, 4:5], 1.0) if act_moments(layer, which, tt) else (m[:, 0:1], -1.0)
                do(dve.scalar_tensor_tensor(out=m[:, 4:5], in0=mean, scalar=sign, in1=m[:, 2:3], op0=ALU.mult, op1=ALU.mult),
                   "ln_scale", layer, which, tt)

            def modulate(layer, which, s, b):
                cols = slice(s * SEQ, (s + 1) * SEQ)
                freed(turn_bank(layer, which, s, b), "mod_x", layer, which, s)
                n = at("h_ready", layer, which, s, b) % 2 * 2
                src = xm[:, n:n + 2, :]
                link(dve.tensor_copy(h_hi[:, 2 * b:2 * b + 2, cols], src))
                do(dve.tensor_tensor(h_lo[:, 2 * b:2 * b + 2, cols], src, h_hi[:, 2 * b:2 * b + 2, cols].bitcast(F32), ALU.subtract),
                   "h_ready", layer, which, s, b)

            def chunk(g, j):
                split_to(g.at[j] + AHEAD + (0 if g.late and j == g.n - 1 else 1))

            def seqs(ap, layer):
                t0 = tok0(layer)
                return ap[:, t0:TOK].rearrange("p (s t) -> p s t", t=SEQ)

            def taps(dst, src, w0, w2):
                first = dve.scalar_tensor_tensor(out=dst[:, :, 1:SEQ], in0=src[:, :, 0:SEQ - 1], scalar=w0, in1=dst[:, :, 1:SEQ],
                                                 op0=ALU.mult, op1=ALU.add)
                link(first)
                return dve.scalar_tensor_tensor(out=dst[:, :, 0:SEQ - 1], in0=src[:, :, 1:SEQ], scalar=w2, in1=dst[:, :, 0:SEQ - 1],
                                                op0=ALU.mult, op1=ALU.add)

            def evac(g):
                layer, kind = g.layer, g.kind
                t0 = tok0(layer)
                if kind in ("a_q", "a_k"):
                    w = 0 if kind == "a_q" else 1
                    for tt in (2, 3):
                        bank(tt, *g.key)
                        if w == 1:
                            bank(4 + tt, "qk", layer, 0, tt)
                            done("qk_ready", layer, 0, tt)
                        src = ps[:, tt, :].rearrange("p (h n) -> p h n", n=64)
                        cos, sin = rope[:, tt - 2, 0, :], rope[:, tt - 2, 1, :]
                        ta, tb = rope_t[:, tt - 2, 0, :], rope_t[:, tt - 2, 1, :]
                        dve.tensor_tensor(ta.rearrange("p (h n) -> p h n", n=64), src, wide(cos, 8), ALU.mult)
                        halves = ps[:, tt, :].rearrange("p (h a n) -> p h a n", a=2, n=16)
                        tv = tb.rearrange("p (h a n) -> p h a n", a=2, n=16)
                        sv = sin.rearrange("p (f a n) -> p f a n", a=2, n=16)
                        for a in range(2):
                            for f in range(2):
                                ins = dve.tensor_tensor(tv.rearrange("p (h f) a n -> p h f a n", f=2)[:, :, f, a, :],
                                                        halves.rearrange("p (h f) a n -> p h f a n", f=2)[:, :, f, 1 - a, :],
                                                        wide(sv[:, f, a, :], 8), ALU.mult)
                        free(ins, tt)
                        freed(tt, *g.key)
                        do(dve.tensor_tensor(qk_tok[:, tt, :], ta, tb, ALU.add), "qk_ready", layer, w, tt)
                if kind == "hy":
                    part = g.index
                    for n in range(4):
                        t = 4 * part + n
                        tile_ = (x0T, uT, vvT)[part][:, n % 2 if part == 2 else n, :]
                        done("conv_mid", layer, part, n)
                        bank(n, *g.key)
                        free(taps(seqs(tile_, layer), seqs(ps[:, n, :], layer), pcol[:, t:t + 1], pcol[:, 24 + t:25 + t]), n)
                        if part == 2:
                            freed(n, *g.key)
                            do(dve.tensor_tensor(uT[:, n, t0:TOK], uT[:, n, t0:TOK], vvT[:, n % 2, t0:TOK], ALU.mult),
                               "u_ready", layer, n)
                if kind == "z":
                    bank(0, *g.key)
                    do(dve.memset(zT[32:33, :], 1.0), "z_one", layer)
                if kind == "g_r":
                    for tt in g.tiles:
                        freed(tt, *g.key)
                        r4 = rg[:, tt % 2, :].rearrange("p (h n) -> p h n", h=HEADS)
                        link(dve.tensor_tensor(r4, r4, wide(gla_g[:], HEADS), ALU.mult))
                        do(dve.tensor_tensor(go[:, tt, :], go[:, tt, :], rg[:, tt % 2, :], ALU.mult), "y_tok", layer, 1, tt)
                if kind == "branch":
                    half, br = g.index
                    for n in range(4):
                        dve.wait_ge(sem(f"sig_in{n}"), 16 * at(f"sig_in{n}", layer, g.index))
                        bank(n, *g.key)
                        if half and br == 0:
                            done("merged", layer, n)
                        if br and (br, n) != (1, 0):
                            prev = ((half, br), n - 2) if n >= 2 else ((half, br - 1), n + 2)
                            if prev[0][1]:
                                done("gated", layer, *prev)
                        dst = acc[:, n, t0:TOK] if br == 0 else prod[:, n % 2, t0:TOK]
                        free(dve.tensor_tensor(dst, ps[:, n, t0:TOK], sig_in[:, n, t0:TOK], ALU.mult), n)
                        if br:
                            freed(n, *g.key)
                            do(dve.tensor_tensor(acc[:, n, t0:TOK], acc[:, n, t0:TOK], dst, ALU.add), "gated", layer, g.index, n)
                    if br == 2:
                        for n in range(4):
                            k = 4 * half + n
                            done("merged_hi", layer, k)
                            do(dve.tensor_tensor(h_lo[:, k, t0:TOK], acc[:, n, t0:TOK], h_hi[:, k, t0:TOK].bitcast(F32), ALU.subtract),
                               "merged", layer, k)
                if kind in ("out", "down"):
                    which = 0 if kind == "out" else 1
                    r, half = R[which], g.index
                    for s in sorted({tt // 2 for tt in g.tiles}):
                        dve.wait_ge(sem(f"res_x{s}"), 16 * at(f"res_x{s}", layer, which, 1))
                        dve.wait_ge(sem(f"gates_in{s}"), 16 * at(f"gates_in{s}", layer, which))
                    cols = slice(half * COLS, half * COLS + COLS)
                    for tt in g.tiles:
                        b = g.bank0 + tt
                        bank(b, *g.key)
                        t = r["t"][:, tt % 2, :]
                        free(dve.tensor_tensor(t, ps[:, b, :], r["g"][:, 1 if tt < 2 else 0, cols], ALU.mult), b)
                        freed(b, *g.key)
                        link(dve.scalar_tensor_tensor(out=r["x"][:, tt, cols], in0=r["x"][:, tt, cols], scalar=ALPHA, in1=t,
                                                      op0=ALU.mult, op1=ALU.add))
                        link(half_moments(r["x"][:, tt, :], tt, half))
                        if half:
                            do(whole_moments(tt), "post_var", layer, which, tt)

            def post(layer, which, tt):
                r = R[which]
                dve.wait_ge(sem("res_ln"), 16 * at("res_ln", layer, which, 1))
                done("post_std", layer, which, tt)
                link(dve.reciprocal(moms[:, tt, 2:3], moms[:, tt, 3:4]))
                link(dve.scalar_tensor_tensor(out=x_tok[:, tt, :], in0=r["x"][:, tt, :], scalar=moms[:, tt, 0:1],
                                              in1=r["ln"][:, 0, :], op0=ALU.subtract, op1=ALU.mult))
                do(dve.scalar_tensor_tensor(out=x_tok[:, tt, :], in0=x_tok[:, tt, :], scalar=moms[:, tt, 2:3],
                                            in1=r["ln"][:, 1, :], op0=ALU.mult, op1=ALU.add), "post_x", layer, which, tt)
                done("post_x", layer, which, tt)

            def filter_(layer, i):
                c1 = 6.28125
                c2 = float(np.float32(np.round((TWO_PI - c1) * 2 ** 20) / 2 ** 20))
                c3 = float(np.float32(TWO_PI - c1 - c2))
                if i < 2:
                    bank(4, "filter", layer, i)
                    free(dve.tensor_scalar(f_arg[:, 0, :], ps[0:64, 4, 0:256], f_col[:, 2 * i:2 * i + 1],
                                           f_col[:, 2 * i + 1:2 * i + 2], ALU.add, ALU.mult), 4)
                    freed(4, "filter", layer, i)
                    link(dve.tensor_scalar(f_arg[:, 1, :], f_arg[:, 0, :], 1.0 / TWO_PI, ROUND, ALU.mult, ALU.add))
                    link(dve.tensor_scalar(f_arg[:, 1, :], f_arg[:, 1, :], -ROUND, None, ALU.add))
                    for c in (c1, c2, c3):
                        link(dve.scalar_tensor_tensor(out=f_arg[:, 0, :], in0=f_arg[:, 1, :], scalar=-c, in1=f_arg[:, 0, :],
                                                      op0=ALU.mult, op1=ALU.add))
                    do(dve.tensor_scalar(f_arg[:, 0, :], f_arg[:, 0, :], -3.1415925, 3.1415925, ALU.max, ALU.min), "f_arg", layer, i)
                if i == 2:
                    bank(7, "filter", layer, 2)
                    for t in range(2):
                        for d in range(2):
                            bank(4 + 2 * t + d, "filter", layer, 2)
                            ins = dve.tensor_tensor(f_t[:, d, :], ps[:, 4 + 2 * t + d, :], decay[:, d, t, :], ALU.mult)
                            free(ins, 4 + 2 * t + d)
                        freed(5 + 2 * t, "filter", layer, 2)
                        dve.tensor_tensor(f_sd[:, 0, t, :], f_t[:, 0, :], f_t[:, 1, :], ALU.add)
                        do(dve.tensor_tensor(f_sd[:, 1, t, :], f_t[:, 0, :], f_t[:, 1, :], ALU.subtract), "f_sd", layer, t)
                        done("f_sd", layer, t)

            def attend(layer, i, n_u):
                us = [(tt, h) for tt in q_tiles(layer) for h in range(HEADS)]
                if i >= n_u:
                    return
                nk = SEQ if us[i][0] < 2 else TOK
                s = soft[:, i % 2, :]
                for m in range(2):
                    bank(4 + m, "scores", layer, i)
                if i >= 2:
                    done("diff", layer, i - 2)
                link(dve.tensor_reduce(s[:, 0:2], ps[:, 4:6, 0:nk], AX_X, ALU.max))
                do(dve.tensor_scalar(s[:, 2:4], s[:, 0:2], -0.125, None, ALU.mult), "neg_max", layer, i)
                for m in range(2):
                    freed(4 + m, "scores", layer, i)
                link(dve.reciprocal(s[:, 6:8], s[:, 4:6]))
                link(dve.tensor_tensor(s[:, 8:9], s[:, 7:8], lam[:, 5:6], ALU.mult))
                link(dve.tensor_scalar(probs[:, i % 2, 1, 0:nk], probs[:, i % 2, 1, 0:nk], s[:, 8:9], None, ALU.mult))
                do(dve.scalar_tensor_tensor(out=probs[:, i % 2, 0, 0:nk], in0=probs[:, i % 2, 0, 0:nk], scalar=s[:, 6:7],
                                            in1=probs[:, i % 2, 1, 0:nk], op0=ALU.mult, op1=ALU.add), "diff", layer, i)

            def norms(sq, layer, br, tt):
                link(dve.tensor_reduce(hn[:, 3, :], sq[:].rearrange("p (h n) -> p h n", h=HEADS), AX_X, ALU.add))
                do(dve.tensor_scalar(hn[:, 0, :], hn[:, 3, :], 1.0 / P, EPS, ALU.mult, ALU.add), "hn_var", layer, br, tt)
                done("hn_std", layer, br, tt)
                link(dve.reciprocal(hn[:, 2, :], hn[:, 1, :]))

            def head_norm(layer, tt):
                done("o_sq", layer, tt)
                norms(o_sq, layer, 0, tt)
                bank(7, "o", layer, tt)
                prev = tt - 1
                if prev in q_tiles(layer):
                    bank(6, "y", layer, 0, prev)
                y4 = y_tok[:].rearrange("p (h n) -> p h n", h=HEADS)
                free(dve.tensor_tensor(y4, ps[:, 7, :].rearrange("p (h n) -> p h n", h=HEADS), wide(hn[:, 2, :], P, 2), ALU.mult), 7)
                freed(7, "o", layer, tt)
                do(dve.tensor_tensor(y4, y4, wide(da_g[:], HEADS), ALU.mult), "y_tok", layer, 0, tt)

            def hy_dft(layer, s):
                for kt in range(2):
                    re, im = 4 + 2 * kt, 5 + 2 * kt
                    bank(re, "U", layer, s)
                    bank(im, "U", layer, s)
                    dve.tensor_tensor(spec_t[:, 0, :], ps[:, re, :], filt[:, 0, kt, :], ALU.mult)
                    link(dve.tensor_tensor(spec_t[:, 1, :], ps[:, im, :], filt[:, 1, kt, :], ALU.mult))
                    link(dve.tensor_tensor(spec[:, 0, kt, :], spec_t[:, 0, :], spec_t[:, 1, :], ALU.subtract))
                    free(dve.tensor_tensor(spec_t[:, 0, :], ps[:, re, :], filt[:, 1, kt, :], ALU.mult), re)
                    free(dve.tensor_tensor(spec_t[:, 1, :], ps[:, im, :], filt[:, 0, kt, :], ALU.mult), im)
                    freed(im, "U", layer, s)
                    do(dve.tensor_tensor(spec[:, 1, kt, :], spec_t[:, 0, :], spec_t[:, 1, :], ALU.add), "spec", layer, s, kt)
                    done("spec", layer, s, kt)

            def hy_idft(layer, s):
                cols = slice(s * SEQ, (s + 1) * SEQ)
                for c in range(CT):
                    b = 4 + c // 2
                    bank(b, "conv", layer, s)
                    if c >= 2:
                        done("y_hyena", layer, s, c - 2)
                    ins = dve.scalar_tensor_tensor(out=hy_t[:, c % 2, :], in0=uT[:, c, cols], scalar=pcol[:, 48 + c:49 + c],
                                                   in1=ps[:, b, (c % 2) * 256:(c % 2) * 256 + 256], op0=ALU.mult, op1=ALU.add)
                    if c % 2:
                        free(ins, b)
                        freed(b, "conv", layer, s)
                    else:
                        link(ins)
                    do(dve.tensor_tensor(y[:, 2, c, cols], hy_t[:, c % 2, :], x0T[:, c, cols], ALU.mult), "y_hyena", layer, s, c)

            def gla_gate(layer, tt):
                done("lg", layer, tt)
                if tt > 0:
                    bank(4, "tail", layer, tt - 1)
                if tt == 0:
                    link(dve.memset(att[:], 0.0))
                free(dve.scalar_tensor_tensor(out=la[:], in0=ps[:, 4, :], scalar=0.0, in1=lg[:], op0=ALU.min, op1=ALU.subtract), 4)

            def gla_sum(layer, tt):
                freed(6, "b", layer, tt)
                freed(4, "tail", layer, tt)
                freed(5, "ktok", layer, tt)
                if tt > 0:
                    bank(5, "u_state", layer, tt - 1)
                do(dve.tensor_tensor(ku[:], etail[:], wide(ktok[:], 2), ALU.mult), "ku", layer, tt)
                for j in range(2):
                    c = 2 * tt + j
                    for d in range(2):
                        n = c if d == 0 else (3 - c if c < 4 else 11 - c)
                        t = 64 * j + (63 if d == 0 else 0)
                        do(dve.tensor_copy(dec[:, d, n, :], eb[:, 0, 2 * d:2 * d + 2, t]), "dec", layer, tt, 2 * j + d)
                if tt in q_tiles(layer):
                    if tt > q_tiles(layer)[0]:
                        bank(7, "att", layer, tt - 1)
                    cols = slice(tt * P, (tt + 1) * P)
                    four = lambda ap: ap.rearrange("p (d a) t -> p d a t", d=2)
                    dve.tensor_tensor(four(qe[:]), four(eb[:, 1, :, :]), wide(gqk[:, 0:2, cols], 2), ALU.mult)
                    link(dve.tensor_tensor(four(ke[:]), four(eb[:, 2, :, :]), wide(gqk[:, 2:4, cols], 2), ALU.mult))
                    link(dve.tensor_tensor(gqk[:, 2:4, cols], gqk[:, 0:2, cols], eb[:, 0, 2:4, :], ALU.mult))
                    do(dve.tensor_tensor(gqk[:, 0:2, cols], gqk[:, 0:2, cols], eb[:, 0, 0:2, :], ALU.mult), "qke", layer, tt)

            def gla_att(layer, tt):
                if tt > q_tiles(layer)[0]:
                    bank(6, "intra", layer, tt - 1)
                for r in range(2):
                    bank(6 + r, "att", layer, tt)
                    free(dve.copy_predicated(att[:, r, :, :].rearrange("p (d a) t -> p d a t", d=2), wide(mask[:], 2, 2),
                                             ps[:, 6 + r, :].rearrange("p (d a t) -> p d a t", d=2, a=2)), 6 + r)

            def gla_scan(layer):
                for d in range(2):
                    freed(4 + d, "u_state", layer, 3)
                done("dec", layer, 3, 3)
                for n in range(1, 7):
                    for d in range(2):
                        for p_ in range(2):
                            ins = dve.scalar_tensor_tensor(out=states[:, d, n, p_, :], in0=states[:, d, n - 1, p_, :],
                                                           scalar=dec[:, d, n, p_:p_ + 1], in1=states[:, d, n, p_, :],
                                                           op0=ALU.mult, op1=ALU.add)
                    if n < 6:
                        link(ins)
                do(ins, "scanned", layer)

            def gla_out(layer, tt):
                freed(6, "intra", layer, tt)
                for r in range(2):
                    bank(4 + r, "inter", layer, tt)
                    part = go[:, tt, :].rearrange("p (a r n) -> p a r n", a=2, r=2)[:, :, r, :]
                    free(dve.tensor_tensor(part, part, ps[:, 4 + r, 0:256].rearrange("p (a n) -> p a n", a=2), ALU.add), 4 + r)
                done("g_sq", layer, tt)
                norms(g_sq, layer, 1, tt)
                g4 = go[:, tt, :].rearrange("p (h n) -> p h n", h=HEADS)
                link(dve.tensor_tensor(g4, g4, wide(hn[:, 2, :], P, 2), ALU.mult))

            def y_split(layer, br):
                t0 = tok0(layer)
                for n in range(CT):
                    done("ys_hi", layer, br, n)
                    k = ys_at[br] + n
                    do(dve.tensor_tensor(ys_lo[:, k, t0:TOK], y[:, br, n, t0:TOK], ys_hi[:, k, t0:TOK].bitcast(F32),
                                         ALU.subtract), "ys_ready", layer, br, n)

            def up(layer, c0):
                split_to(c0 + AHEAD)
                t0 = tok0(layer)
                n_groups = UP_GROUPS
                W0, W2 = 52, 140
                if layer == 0:
                    dve.sem_inc(sem("act_lo"), 2)
                    C.skip("act_lo", 2)
                C.base("act_lo", layer)
                C.base("up_prod", layer)
                C.base("up_tap", layer)
                l0 = C.seen.get("up_tap", 0)
                b0 = [at(f"bank_full{b}", "base", "up", layer) for b in range(8)]
                m0, g0, h0 = at("up_mid", "base", layer), at("up_gelu", "base", layer), at("act_hi", "base", layer)
                dve.wait_ge(sem("x_out"), 16 * at("x_out", layer, 0, 3))
                def up_group(i, h):
                    for j in range(4):
                        c = c0 + AHEAD + 4 * h + j
                        s = c % NBUF
                        dve.wait_ge(sem("hi_ready"), i * 8 + (c + 1))
                        dve.tensor_tensor(w_lo[:, s, :], stage[:, s, :], w_hi[:, s, :].bitcast(F32), ALU.subtract)\
                           .then_inc(sem("lo_ready"), 1)
                    for p_ in range(2):
                        for side in range(2):
                            for a in range(2):
                                b = 4 * h + 2 * a + p_
                                dst, src = seqs(ffn_t[:, p_, a, :], layer), seqs(ps[:, b, :], layer)
                                to, of = (slice(1, SEQ), slice(0, SEQ - 1)) if side == 0 else (slice(0, SEQ - 1), slice(1, SEQ))
                                col = pcol[:, bass.ds(i * 4 + ((W0, W2)[side] + 22 * a + 2 * h + p_), 1)]
                                if side == 0:
                                    dve.wait_ge(sem("up_mid"), i * 8 + (m0 + 4 * h + 2 * p_ + a + 1))
                                else:
                                    dve.wait_ge(sem("up_tap"), i * 8 + (l0 + 4 * h + 2 * p_ + a + 1))
                                dve.scalar_tensor_tensor(out=dst[:, :, to], in0=src[:, :, of], scalar=col, in1=dst[:, :, to],
                                                         op0=ALU.mult, op1=ALU.add)\
                                   .then_inc(sem("up_tap") if side == 0 else sem(f"bank_free{b}"), 1)
                    for p_ in range(2):
                        dve.wait_ge(sem("up_gelu"), i * 4 + (g0 + 2 * h + p_ + 1))
                        dve.wait_ge(sem(f"bank_free{4 * h + p_}"), i + (b0[4 * h + p_] + 1))
                        dve.tensor_tensor(ffn_t[:, p_, 0, t0:TOK], ffn_t[:, p_, 0, t0:TOK], ffn_t[:, p_, 1, t0:TOK], ALU.mult)\
                           .then_inc(sem("up_prod"), 1)
                    for p_ in range(2):
                        dve.wait_ge(sem("act_hi"), i * 4 + (h0 + 2 * h + p_ + 1))
                        dst = act_lo[:, bass.ds(i * 4 + (2 * h + p_), 1), t0:TOK].rearrange("p a t -> p (a t)")
                        hi = act_hi[:, bass.ds(i * 4 + (2 * h + p_), 1), t0:TOK].rearrange("p a t -> p (a t)").bitcast(F32)
                        dve.tensor_tensor(dst, ffn_t[:, p_, 0, t0:TOK], hi, ALU.subtract).then_inc(sem("act_lo"), 1)

                with dve.Fori(0, UP_GROUPS // 2) as i:
                    for h in range(2):
                        up_group(i, h)
                up_group(UP_GROUPS // 2, 0)
                C.skip("act_lo", 2 * n_groups)
                C.skip("up_prod", 2 * n_groups)
                C.skip("up_tap", 4 * n_groups)
                C.base("act_lo", "end", layer)
                cursor[0] += 4 * n_groups

            fns = dict(start=start, params_turn=params_turn, modcols=modcols, moments=moments, normal=normal,
                       modulate=modulate, chunk=chunk, evac=evac, filter=filter_, attend=attend, head_norm=head_norm, hy_dft=hy_dft, hy_idft=hy_idft,
                       gla_gate=gla_gate, gla_sum=gla_sum, gla_att=gla_att, gla_scan=gla_scan, gla_out=gla_out,
                       y_split=y_split, post=post, up=up)
            for st in steps:
                if st[0] in fns:
                    fns[st[0]](*st[1:])
    return C


INPUTS = ["x", "c", "ctx", "c_ctx", "w_ada", "b_ada", "w_in", "da_lambda", "da_norm_g", "gla_w_gate", "gla_b_gate",
          "gla_norm_g", "hy_conv_w", "hy_conv_b", "hy_w1", "hy_b1", "hy_freq1", "hy_w2", "hy_b2", "hy_freq2", "hy_w3",
          "hy_skip", "w_branch", "w_out", "ln1_g", "ln1_b", "ffn_w_up", "ffn_conv_w", "ffn_conv_b", "ffn_w_down",
          "ln2_g", "ln2_b"]


def kernel(**inputs):
    import concourse.bacc as bacc
    from concourse.bass_utils import run_bass_kernel_spmd

    arrays = {name: np.ascontiguousarray(inputs[name]) for name in INPUTS}
    arrays.update(shape_constants())

    def build(known):
        nc = bacc.Bacc("TRN2", target_bir_lowering=False, num_devices=1)
        args = {n: nc.dram_tensor("in_" + n, a.shape, mybir.dt.from_np(a.dtype), kind="ExternalInput").ap()
                for n, a in arrays.items()}
        out = nc.dram_tensor("out_x", (1, SEQ, D), F32, kind="ExternalOutput").ap()
        return nc, build_program(nc, args, out, known)

    _, counts = build(None)
    nc, _ = build(counts)
    r = run_bass_kernel_spmd(nc, [{"in_" + n: a for n, a in arrays.items()}], core_ids=[0])
    return r.results[0]["out_x"]
```
